# Optimizing a Trainium2 kernel written in Bass

```python
import math
import jax, jax.numpy as jnp
from jax import lax
import numpy as np
import jax
import jax.numpy as jnp

D_MODEL = 1024
BATCH = 1
SEQ = 256
DEPTH = 2

N_MEM = 256
N_MIXERS = 2
D_MIX = D_MODEL
XA_HEADS = 4
XA_HEAD_DIM = D_MODEL // 16
D_XA = XA_HEADS * XA_HEAD_DIM
D_TOK = D_MIX - D_XA
CONV_WIDTH = 3
ML_HEADS = 4
ML_HEAD_DIM = D_TOK // ML_HEADS
ML_CHUNK = 64
QK_CONV_WIDTH = 4
D_FF = 256 * int(math.ceil(8 * D_MODEL / 3 / 256))
LN_EPS = 1e-5
DEEPNORM_ALPHA = (2.0 * DEPTH) ** 0.25
DEEPNORM_BETA = (8.0 * DEPTH) ** -0.25
N_CONV_LAYERS = (DEPTH + 1) // 2
N_MLSTM_LAYERS = DEPTH // 2
D_IN_CONV = 3 * D_TOK + D_XA
D_IN_MLSTM = 4 * D_TOK + 2 * ML_HEADS + D_XA


def layer_norm(x, g, b):
    xf = x.astype(jnp.float32)
    mu = jnp.mean(xf, -1, keepdims=True)
    var = jnp.mean(jnp.square(xf - mu), -1, keepdims=True)
    y = (xf - mu) * lax.rsqrt(var + LN_EPS)
    return (y * g.astype(jnp.float32) + b.astype(jnp.float32)).astype(x.dtype)

def swiglu(x, w_gate, w_up, w_down):
    return (jax.nn.silu(x @ w_gate) * (x @ w_up)) @ w_down

def causal_dwconv(u, w):
    width = w.shape[0]
    s = u.shape[1]
    up = jnp.pad(u, ((0, 0), (width - 1, 0), (0, 0)))
    out = up[:, width - 1:width - 1 + s] * w[width - 1]
    for j in range(width - 1):
        out = out + up[:, j:j + s] * w[j]
    return out

def memory_cross_attention(q, mem_kv):
    b, s, _ = q.shape
    q = q.reshape(b, s, XA_HEADS, XA_HEAD_DIM)
    k, v = jnp.split(mem_kv, 2, -1)
    k = k.reshape(b, N_MEM, XA_HEADS, XA_HEAD_DIM)
    v = v.reshape(b, N_MEM, XA_HEADS, XA_HEAD_DIM)
    scores = jnp.einsum('bshd,bmhd->bhsm', q, k).astype(jnp.float32) * (XA_HEAD_DIM ** -0.5)
    p = jax.nn.softmax(scores, -1).astype(v.dtype)
    o = jnp.einsum('bhsm,bmhd->bshd', p, v)
    return o.reshape(b, s, D_XA)

def short_conv_mixer(u, conv_w):
    b_gate, c_gate, x_in = jnp.split(u, 3, -1)
    return b_gate * causal_dwconv(c_gate * x_in, conv_w)

def mlstm_chunkwise(q, k, v, log_i, log_f):
    b, s, _ = q.shape
    h_, dh, L = ML_HEADS, ML_HEAD_DIM, ML_CHUNK
    nc = s // L

    def to_chunks(t):
        return t.astype(jnp.float32).reshape(b, nc, L, h_, dh).transpose(1, 0, 3, 2, 4)

    def gate_chunks(g):
        return g.astype(jnp.float32).reshape(b, nc, L, h_).transpose(1, 0, 3, 2)

    qc, kc, vc = to_chunks(q), to_chunks(k) * (dh ** -0.5), to_chunks(v)
    ic, fc = gate_chunks(log_i), gate_chunks(log_f)
    causal = jnp.tril(jnp.ones((L, L), dtype=bool))

    def step(carry, xs):
        c_st, n_st, m_st = carry
        q_, k_, v_, li, lf = xs
        bcum = jnp.cumsum(lf, -1)
        log_d = bcum[..., :, None] - bcum[..., None, :] + li[..., None, :]
        log_d = jnp.where(causal, log_d, -jnp.inf)
        log_inter = bcum + m_st[..., None]
        m_t = jnp.maximum(log_inter, jnp.max(log_d, -1))
        w_intra = jnp.exp(log_d - m_t[..., None])
        w_inter = jnp.exp(log_inter - m_t)
        sc = jnp.einsum('bhtd,bhsd->bhts', q_, k_) * w_intra
        num = (jnp.einsum('bhts,bhse->bhte', sc, v_)
               + w_inter[..., None] * jnp.einsum('bhtd,bhde->bhte', q_, c_st))
        den = jnp.sum(sc, -1) + w_inter * jnp.einsum('bhtd,bhd->bht', q_, n_st)
        h = num / jnp.maximum(jnp.abs(den), jnp.exp(-m_t))[..., None]
        b_last = bcum[..., -1]
        log_w = b_last[..., None] - bcum + li
        m_new = jnp.maximum(b_last + m_st, jnp.max(log_w, -1))
        w_k = jnp.exp(log_w - m_new[..., None])
        decay = jnp.exp(b_last + m_st - m_new)
        c_new = decay[..., None, None] * c_st + jnp.einsum('bhs,bhsd,bhse->bhde', w_k, k_, v_)
        n_new = decay[..., None] * n_st + jnp.einsum('bhs,bhsd->bhd', w_k, k_)
        return (c_new, n_new, m_new), h

    init = (jnp.zeros((b, h_, dh, dh), jnp.float32),
            jnp.zeros((b, h_, dh), jnp.float32),
            jnp.zeros((b, h_), jnp.float32))
    _, hs = lax.scan(step, init, (qc, kc, vc, ic, fc))
    return hs.transpose(1, 0, 3, 2, 4).reshape(b, s, h_, dh)

def mlstm_mixer(u, b_gates, qk_conv_w, head_norm_g):
    b, s, _ = u.shape
    qk, v, o_pre, gates = jnp.split(u, [2 * D_TOK, 3 * D_TOK, 4 * D_TOK], -1)
    qk = jax.nn.silu(causal_dwconv(qk, qk_conv_w))
    q, k = jnp.split(qk, 2, -1)
    gates = gates.astype(jnp.float32) + b_gates.astype(jnp.float32)
    log_i = gates[..., :ML_HEADS]
    log_f = jax.nn.log_sigmoid(gates[..., ML_HEADS:])
    h = mlstm_chunkwise(q, k, v, log_i, log_f)
    mu = jnp.mean(h, -1, keepdims=True)
    var = jnp.mean(jnp.square(h - mu), -1, keepdims=True)
    h = (h - mu) * lax.rsqrt(var + LN_EPS) * head_norm_g.astype(jnp.float32)
    return jax.nn.sigmoid(o_pre) * h.reshape(b, s, D_TOK).astype(u.dtype)

def first_inputs(seed: int = 0) -> dict:
    key = jax.random.key(seed)
    ks = jax.random.split(key, 20)
    nrm = jax.random.normal
    f32 = jnp.float32
    x = nrm(ks[0], (BATCH, SEQ, D_MODEL), f32)
    mem = nrm(ks[1], (BATCH, N_MEM, D_MODEL), f32)
    ln_g = 1.0 + 0.02 * nrm(ks[2], (DEPTH, 3, D_MODEL), f32)
    ln_b = 0.02 * nrm(ks[3], (DEPTH, 3, D_MODEL), f32)
    ffn_w_gate = nrm(ks[4], (DEPTH, 2, D_MODEL, D_FF), f32) * D_MODEL ** -0.5
    ffn_w_up = nrm(ks[5], (DEPTH, 2, D_MODEL, D_FF), f32) * D_MODEL ** -0.5
    ffn_w_down = nrm(ks[6], (DEPTH, 2, D_FF, D_MODEL), f32) * (D_FF ** -0.5 * DEEPNORM_BETA)
    w_kv_mem = nrm(ks[7], (DEPTH, D_MODEL, 2 * D_XA), f32) * D_MODEL ** -0.5
    w_out = nrm(ks[8], (DEPTH, D_MIX, D_MODEL), f32) * (D_MIX ** -0.5 * DEEPNORM_BETA)
    w_in_conv = nrm(ks[9], (N_CONV_LAYERS, D_MODEL, D_IN_CONV), f32) * D_MODEL ** -0.5
    conv_w = nrm(ks[10], (N_CONV_LAYERS, CONV_WIDTH, D_TOK), f32) * CONV_WIDTH ** -0.5
    w_in_mlstm = nrm(ks[11], (N_MLSTM_LAYERS, D_MODEL, D_IN_MLSTM), f32) * D_MODEL ** -0.5
    w_in_mlstm = w_in_mlstm.at[:, :, 4 * D_TOK:4 * D_TOK + 2 * ML_HEADS].multiply(0.1)
    b_i = 0.1 * nrm(ks[12], (N_MLSTM_LAYERS, ML_HEADS), f32)
    b_f = jnp.linspace(3.0, 6.0, ML_HEADS, dtype=f32) + 0.1 * nrm(ks[13], (N_MLSTM_LAYERS, ML_HEADS), f32)
    b_gates = jnp.concatenate([b_i, b_f], -1)
    qk_conv_w = nrm(ks[14], (N_MLSTM_LAYERS, QK_CONV_WIDTH, 2 * D_TOK), f32) * QK_CONV_WIDTH ** -0.5
    head_norm_g = 1.0 + 0.02 * nrm(ks[15], (N_MLSTM_LAYERS, ML_HEADS, ML_HEAD_DIM), f32)
    return {"x": x, "mem": mem, "ln_g": ln_g, "ln_b": ln_b,
            "ffn_w_gate": ffn_w_gate, "ffn_w_up": ffn_w_up, "ffn_w_down": ffn_w_down,
            "w_kv_mem": w_kv_mem, "w_out": w_out,
            "w_in_conv": w_in_conv, "conv_w": conv_w,
            "w_in_mlstm": w_in_mlstm, "b_gates": b_gates,
            "qk_conv_w": qk_conv_w, "head_norm_g": head_norm_g}

def first_block(x, mem, ln_g, ln_b, ffn_w_gate, ffn_w_up, ffn_w_down, w_kv_mem, w_out,
              w_in_conv, conv_w, w_in_mlstm, b_gates, qk_conv_w, head_norm_g):
    alpha = DEEPNORM_ALPHA
    for l in range(DEPTH):
        x = layer_norm(alpha * x + 0.5 * swiglu(x, ffn_w_gate[l, 0], ffn_w_up[l, 0], ffn_w_down[l, 0]),
                       ln_g[l, 0], ln_b[l, 0])
        mem_kv = mem @ w_kv_mem[l]
        j = l // N_MIXERS
        if l % N_MIXERS == 0:
            u = x @ w_in_conv[j]
            tok = short_conv_mixer(u[..., :3 * D_TOK], conv_w[j])
        else:
            u = x @ w_in_mlstm[j]
            tok = mlstm_mixer(u[..., :4 * D_TOK + 2 * ML_HEADS], b_gates[j], qk_conv_w[j], head_norm_g[j])
        xa = memory_cross_attention(u[..., -D_XA:], mem_kv)
        mix = jnp.concatenate([tok, xa], -1) @ w_out[l]
        x = layer_norm(alpha * x + mix, ln_g[l, 1], ln_b[l, 1])
        x = layer_norm(alpha * x + 0.5 * swiglu(x, ffn_w_gate[l, 1], ffn_w_up[l, 1], ffn_w_down[l, 1]),
                       ln_g[l, 2], ln_b[l, 2])
    return x


DEPTH_2 = 1

CHUNK = 64
MAX_STREAM_CHUNKS = 64
POOL_WINDOWS = (2, 4, 8, 16)
POOL_GROUPS = len(POOL_WINDOWS)
D_POOL = D_MODEL // 2
POOL_GW = D_POOL // POOL_GROUPS
D_CONV = D_MODEL // 2
CONV_WIDTH_2 = 31
N_HEADS = 8
QK_NOPE = 64
QK_ROPE = 32
V_HEAD = 64
Q_LORA = 384
KV_LORA = 256
ROPE_THETA = 10000.0
Q_BLOCK = 128
N_BRANCH = 3
OFF_CONV = D_POOL
OFF_Q = OFF_CONV + 2 * D_CONV
OFF_KV = OFF_Q + Q_LORA
OFF_KR = OFF_KV + KV_LORA
OFF_GATE = OFF_KR + QK_ROPE
D_IN = OFF_GATE + N_BRANCH * D_MODEL
IN_SPLITS = (OFF_CONV, OFF_Q, OFF_KV, OFF_KR, OFF_GATE)
N_EXPERTS = 16
N_GROUPS = 4
EXPERTS_PER_GROUP = N_EXPERTS // N_GROUPS
TOPK_GROUPS = 1
TOP_K = 2
D_EXPERT = 512
MOE_BLOCK = 128
D_PLE = 256
DEEPNORM_ALPHA_2 = (2 * DEPTH_2) ** 0.25
DEEPNORM_BETA_2 = (8 * DEPTH_2) ** -0.25
RMS_EPS = 1e-6


def layer_norm_2(x, g, b):
    xf = x.astype(jnp.float32)
    mu = jnp.mean(xf, axis=-1, keepdims=True)
    xc = xf - mu
    var = jnp.mean(xc * xc, axis=-1, keepdims=True)
    return (xc * lax.rsqrt(var + LN_EPS) * g.astype(jnp.float32) + b.astype(jnp.float32)).astype(x.dtype)

def rms_norm(x, g):
    xf = x.astype(jnp.float32)
    ms = jnp.mean(xf * xf, axis=-1, keepdims=True)
    return (xf * lax.rsqrt(ms + RMS_EPS) * g.astype(jnp.float32)).astype(x.dtype)

def rope_tables(positions):
    inv_freq = jnp.power(ROPE_THETA, -jnp.arange(0, QK_ROPE, 2, dtype=jnp.float32) / QK_ROPE)
    ang = positions.astype(jnp.float32)[..., None] * inv_freq
    return jnp.cos(ang), jnp.sin(ang)

def apply_rope(x, cos, sin):
    cos = cos.astype(x.dtype)
    sin = sin.astype(x.dtype)
    x1, x2 = jnp.split(x, 2, axis=-1)
    return jnp.concatenate([x1 * cos - x2 * sin, x2 * cos + x1 * sin], axis=-1)

def pool_mixer(u, w_grp, scale):
    B, S, C = u.shape
    uf = u.astype(jnp.float32)
    cs = jnp.cumsum(uf, axis=1)
    t = jnp.arange(S)
    means = []
    for g, w in enumerate(POOL_WINDOWS):
        csg = cs[..., g * POOL_GW:(g + 1) * POOL_GW]
        lag = jnp.pad(csg[:, :S - w], ((0, 0), (w, 0), (0, 0)))
        cnt = jnp.minimum(t + 1, w).astype(jnp.float32)[None, :, None]
        means.append((csg - lag) / cnt)
    mixed = (jnp.concatenate(means, axis=-1) - uf).astype(u.dtype)
    mixed = jnp.einsum('bsgc,gcd->bsgd', mixed.reshape(B, S, POOL_GROUPS, POOL_GW), w_grp)
    return mixed.reshape(B, S, C) * scale

def conv_module(u2, dw, db, g, b):
    a, gate = jnp.split(u2, 2, axis=-1)
    z = a * jax.nn.sigmoid(gate)
    z = lax.conv_general_dilated(z, dw[:, None, :], window_strides=(1,),
                                 padding=[(CONV_WIDTH_2 - 1, 0)],
                                 dimension_numbers=('NWC', 'WIO', 'NWC'),
                                 feature_group_count=D_CONV) + db
    return jax.nn.silu(layer_norm_2(z, g, b))

def chunk_causal_attention(q, k, v):
    B, S, H, Dk = q.shape
    nq = S // Q_BLOCK
    scale = Dk ** -0.5
    qb = q.reshape(B, nq, Q_BLOCK, H, Dk).transpose(1, 0, 2, 3, 4)
    key_chunk = jnp.arange(S) // CHUNK

    def block(args):
        qi, i = args
        s = jnp.einsum('bqhd,bkhd->bhqk', qi, k, preferred_element_type=jnp.float32) * scale
        q_chunk = (i * Q_BLOCK + jnp.arange(Q_BLOCK)) // CHUNK
        mask = key_chunk[None, :] <= q_chunk[:, None]
        pr = jax.nn.softmax(jnp.where(mask, s, -jnp.inf), axis=-1).astype(v.dtype)
        return jnp.einsum('bhqk,bkhd->bqhd', pr, v)

    o = lax.map(block, (qb, jnp.arange(nq)))
    return o.transpose(1, 0, 2, 3, 4).reshape(B, S, H, v.shape[-1])

def mla(c_q, c_kv, k_r, cos, sin, q_norm_g, w_uq, kv_norm_g, w_ukv):
    B, S, _ = c_q.shape
    q = jnp.matmul(rms_norm(c_q, q_norm_g), w_uq).reshape(B, S, N_HEADS, QK_NOPE + QK_ROPE)
    q_nope, q_rope = q[..., :QK_NOPE], q[..., QK_NOPE:]
    q_rope = apply_rope(q_rope, cos[:, :, None, :], sin[:, :, None, :])
    kv = jnp.matmul(rms_norm(c_kv, kv_norm_g), w_ukv).reshape(B, S, N_HEADS, QK_NOPE + V_HEAD)
    k_nope, v = kv[..., :QK_NOPE], kv[..., QK_NOPE:]
    k_rope = apply_rope(k_r, cos, sin)
    qf = jnp.concatenate([q_nope, q_rope], axis=-1)
    kf = jnp.concatenate([k_nope, jnp.broadcast_to(k_rope[:, :, None, :], (B, S, N_HEADS, QK_ROPE))], axis=-1)
    o = chunk_causal_attention(qf, kf, v)
    return o.reshape(B, S, N_HEADS * V_HEAD)

def mixer_sublayer(h, cos, sin, w_in, b_gate, pool_w, pool_scale, pool_proj, conv_dw, conv_b,
                   conv_ln_g, conv_ln_b, conv_proj, q_norm_g, w_uq, kv_norm_g, w_ukv, mla_proj, w_out):
    B, S, D = h.shape
    proj = jnp.matmul(h, w_in)
    u_pool, u_conv, c_q, c_kv, k_r, g_logits = jnp.split(proj, IN_SPLITS, axis=-1)
    gates = jax.nn.sigmoid(g_logits.reshape(B, S, N_BRANCH, D) + b_gate)
    y_pool = jnp.matmul(pool_mixer(u_pool, pool_w, pool_scale), pool_proj)
    y_conv = jnp.matmul(conv_module(u_conv, conv_dw, conv_b, conv_ln_g, conv_ln_b), conv_proj)
    y_mla = jnp.matmul(mla(c_q, c_kv, k_r, cos, sin, q_norm_g, w_uq, kv_norm_g, w_ukv), mla_proj)
    merged = gates[:, :, 0] * y_pool + gates[:, :, 1] * y_conv + gates[:, :, 2] * y_mla
    return jnp.matmul(merged, w_out)

def moe_ffn(h, w_router, router_bias, w_up, w_down):
    B, S, D = h.shape
    T = B * S
    A = T * TOP_K
    xt = h.reshape(T, D)
    aff = jax.nn.sigmoid(jnp.matmul(xt, w_router).astype(jnp.float32))
    sel = aff + router_bias.astype(jnp.float32)
    grp_score = jnp.sum(lax.top_k(sel.reshape(T, N_GROUPS, EXPERTS_PER_GROUP), TOP_K)[0], axis=-1)
    _, g_idx = lax.top_k(grp_score, TOPK_GROUPS)
    g_keep = jnp.any(jnp.arange(N_GROUPS)[None, None, :] == g_idx[:, :, None], axis=1)
    e_keep = jnp.repeat(g_keep, EXPERTS_PER_GROUP, axis=-1)
    _, e_idx = lax.top_k(jnp.where(e_keep, sel, -jnp.inf), TOP_K)
    w = jnp.take_along_axis(aff, e_idx, axis=-1)
    w = w / jnp.sum(w, axis=-1, keepdims=True)
    n_slots = ((A + N_EXPERTS * MOE_BLOCK + MOE_BLOCK - 1) // MOE_BLOCK) * MOE_BLOCK
    n_blocks = n_slots // MOE_BLOCK
    flat_e = e_idx.reshape(A)
    order = jnp.argsort(flat_e)
    s_e = flat_e[order]
    s_tok = (order // TOP_K).astype(jnp.int32)
    s_w = w.reshape(A)[order]
    counts = jnp.bincount(flat_e, length=N_EXPERTS)
    start = jnp.cumsum(counts) - counts
    padded = (counts + MOE_BLOCK - 1) // MOE_BLOCK * MOE_BLOCK
    pad_end = jnp.cumsum(padded)
    pad_start = pad_end - padded
    dest = pad_start[s_e] + jnp.arange(A) - start[s_e]
    slot_tok = jnp.full((n_slots,), T, jnp.int32).at[dest].set(s_tok)
    slot_w = jnp.zeros((n_slots,), jnp.float32).at[dest].set(s_w)
    blk_e = jnp.minimum(jnp.searchsorted(pad_end, jnp.arange(n_blocks) * MOE_BLOCK, side='right'),
                        N_EXPERTS - 1)
    xs = jnp.concatenate([xt, jnp.zeros((1, D), xt.dtype)], axis=0)[slot_tok]
    xs = xs.reshape(n_blocks, MOE_BLOCK, D)

    def expert_block(args):
        xb, e = args
        gate, up = jnp.split(jnp.matmul(xb, w_up[e]), 2, axis=-1)
        return jnp.matmul(jax.nn.silu(gate) * up, w_down[e])

    ys = lax.map(expert_block, (xs, blk_e)).reshape(n_slots, D)
    out = jnp.zeros((T + 1, D), h.dtype).at[slot_tok].add(ys * slot_w[:, None].astype(ys.dtype))
    return out[:T].reshape(B, S, D)

def second_inputs(seed: int = 0) -> dict:
    key = jax.random.key(seed)
    ks = iter(jax.random.split(key, 40))
    f32 = jnp.float32
    L, D = DEPTH_2, D_MODEL

    def dense(shape, fan_in, gain=1.0):
        return jax.random.normal(next(ks), shape, f32) * (gain * fan_in ** -0.5)

    def norm_gain(shape):
        return 1.0 + 0.05 * jax.random.normal(next(ks), shape, f32)

    def small(shape, s=0.02):
        return s * jax.random.normal(next(ks), shape, f32)

    x = jax.random.normal(next(ks), (BATCH, SEQ, D), f32)
    p = jax.random.normal(next(ks), (L, BATCH, SEQ, D_PLE), f32)
    offset = jax.random.randint(next(ks), (BATCH, 1), 0, MAX_STREAM_CHUNKS) * CHUNK
    positions = (offset + jnp.arange(SEQ, dtype=jnp.int32)[None, :]).astype(jnp.int32)
    return {
        'x': x,
        'p': p,
        'positions': positions,
        'ln_in_g': norm_gain((D,)),
        'ln_in_b': small((D,)),
        'w_in': dense((L, D, D_IN), D),
        'b_gate': small((L, N_BRANCH, D), 0.1),
        'pool_w': dense((L, POOL_GROUPS, POOL_GW, POOL_GW), POOL_GW),
        'pool_scale': norm_gain((L, D_POOL)),
        'pool_proj': dense((L, D_POOL, D), D_POOL),
        'conv_dw': dense((L, CONV_WIDTH_2, D_CONV), CONV_WIDTH_2),
        'conv_b': small((L, D_CONV)),
        'conv_ln_g': norm_gain((L, D_CONV)),
        'conv_ln_b': small((L, D_CONV)),
        'conv_proj': dense((L, D_CONV, D), D_CONV),
        'q_norm_g': norm_gain((L, Q_LORA)),
        'w_uq': dense((L, Q_LORA, N_HEADS * (QK_NOPE + QK_ROPE)), Q_LORA),
        'kv_norm_g': norm_gain((L, KV_LORA)),
        'w_ukv': dense((L, KV_LORA, N_HEADS * (QK_NOPE + V_HEAD)), KV_LORA),
        'mla_proj': dense((L, N_HEADS * V_HEAD, D), N_HEADS * V_HEAD),
        'w_out': dense((L, D, D), D, DEEPNORM_BETA_2),
        'ln1_g': norm_gain((L, D)),
        'ln1_b': small((L, D)),
        'w_router': dense((D, N_EXPERTS), D),
        'router_bias': small((N_EXPERTS,), 0.01),
        'exp_w_up': dense((L, N_EXPERTS, D, 2 * D_EXPERT), D),
        'exp_w_down': dense((L, N_EXPERTS, D_EXPERT, D), D_EXPERT, DEEPNORM_BETA_2),
        'ple_proj': dense((L, D_PLE, D), D_PLE, DEEPNORM_BETA_2),
        'ple_gate': dense((L, D, D), D),
        'ln2_g': norm_gain((L, D)),
        'ln2_b': small((L, D)),
    }

def second_block(x, p, positions, ln_in_g, ln_in_b, w_in, b_gate, pool_w, pool_scale, pool_proj,
              conv_dw, conv_b, conv_ln_g, conv_ln_b, conv_proj, q_norm_g, w_uq, kv_norm_g, w_ukv,
              mla_proj, w_out, ln1_g, ln1_b, w_router, router_bias, exp_w_up, exp_w_down,
              ple_proj, ple_gate, ln2_g, ln2_b):
    cos, sin = rope_tables(positions)
    h = layer_norm_2(x, ln_in_g, ln_in_b)
    for i in range(DEPTH_2):
        y = mixer_sublayer(h, cos, sin, w_in[i], b_gate[i], pool_w[i], pool_scale[i], pool_proj[i],
                           conv_dw[i], conv_b[i], conv_ln_g[i], conv_ln_b[i], conv_proj[i],
                           q_norm_g[i], w_uq[i], kv_norm_g[i], w_ukv[i], mla_proj[i], w_out[i])
        h = layer_norm_2(DEEPNORM_ALPHA_2 * h + y, ln1_g[i], ln1_b[i])
        e = jnp.matmul(p[i], ple_proj[i]) * jax.nn.sigmoid(jnp.matmul(h, ple_gate[i]))
        m = moe_ffn(h, w_router, router_bias, exp_w_up[i], exp_w_down[i])
        h = layer_norm_2(DEEPNORM_ALPHA_2 * h + m + e, ln2_g[i], ln2_b[i])
    return h


def setup_inputs(seed=0):
    out = dict(first_inputs(seed))
    for name, value in second_inputs(seed + 1).items():
        if name != "x":
            out[name + "_2"] = value
    return out


def reference(
    x, mem, ln_g, ln_b, ffn_w_gate, ffn_w_up, ffn_w_down, w_kv_mem, w_out, w_in_conv, conv_w,
    w_in_mlstm, b_gates, qk_conv_w, head_norm_g, p_2, positions_2, ln_in_g_2, ln_in_b_2, w_in_2,
    b_gate_2, pool_w_2, pool_scale_2, pool_proj_2, conv_dw_2, conv_b_2, conv_ln_g_2,
    conv_ln_b_2, conv_proj_2, q_norm_g_2, w_uq_2, kv_norm_g_2, w_ukv_2, mla_proj_2, w_out_2,
    ln1_g_2, ln1_b_2, w_router_2, router_bias_2, exp_w_up_2, exp_w_down_2, ple_proj_2,
    ple_gate_2, ln2_g_2, ln2_b_2,
):
    x = first_block(
        x, mem, ln_g, ln_b, ffn_w_gate, ffn_w_up, ffn_w_down, w_kv_mem, w_out, w_in_conv,
        conv_w, w_in_mlstm, b_gates, qk_conv_w, head_norm_g,
    )
    return second_block(
        x, p_2, positions_2, ln_in_g_2, ln_in_b_2, w_in_2, b_gate_2, pool_w_2, pool_scale_2,
        pool_proj_2, conv_dw_2, conv_b_2, conv_ln_g_2, conv_ln_b_2, conv_proj_2, q_norm_g_2,
        w_uq_2, kv_norm_g_2, w_ukv_2, mla_proj_2, w_out_2, ln1_g_2, ln1_b_2, w_router_2,
        router_bias_2, exp_w_up_2, exp_w_down_2, ple_proj_2, ple_gate_2, ln2_g_2, ln2_b_2,
    )


_drawn_inputs = setup_inputs


def setup_inputs(seed=0):
    import zlib

    import numpy as np

    out = dict(_drawn_inputs(seed))
    spreads = {}
    factors = {'head_norm_g': 4.162,
     'b_gate_2': 2.727,
     'conv_b_2': 3.393,
     'conv_ln_g_2': 3.398,
     'conv_ln_b_2': 8.0,
     'q_norm_g_2': 8.0,
     'kv_norm_g_2': 4.369,
     'ln2_b_2': 2.796,
     'pool_scale_2': 5.841}
    for name, (base, spread) in spreads.items():
        noise = np.random.default_rng([zlib.crc32(name.encode()), seed]).standard_normal(out[name].shape)
        drawn = base * np.exp(spread * noise) if base else spread * noise
        out[name] = jnp.asarray(drawn.astype(out[name].dtype))
    for name, factor in factors.items():
        out[name] = (out[name] * factor).astype(out[name].dtype)
    return out
```

```python
import math
from contextlib import ExitStack

import numpy as np

import concourse.bass as bass
from concourse import mybir
from concourse.alu_op_type import AluOpType as ALU

D = 1024
T = 256
FF = 2816
NEXP = 16
ALPHA1 = 4.0 ** 0.25
ALPHA2 = 2.0 ** 0.25
LN_EPS = 1e-5
RMS_EPS = 1e-6
TILE = 2048
PI = math.pi


def weight_tiles():
    tiles = []

    def ffn(gate, up, down, gi, ui, di, chunks, up0, late=None):
        for c in range(chunks):
            tiles.append((gate, gi(c), 0, 8, *up0(0, c)))
            tiles.append((up, ui(c), 0, 8, *up0(1, c)))
            if c:
                tiles.append((down, di(c - 1), *late(c - 1), 0, D))
        tiles.append((down, di(chunks - 1), *late(chunks - 1), 0, D))

    def first_ffn(l, s):
        i = (l, s)
        ffn("ffn_w_gate", "ffn_w_up", "ffn_w_down", lambda c: i, lambda c: i, lambda c: i, FF // 256,
            lambda part, c: (256 * c, 256 * c + 256), lambda c: (2 * c, 2 * c + 2))

    def rows(name, idx, blocks, n0, n1, step=2):
        for k in range(0, blocks, step):
            tiles.append((name, idx, k, k + step, n0, n1))

    for l in range(2):
        tiles.append(("w_kv_mem", (l,), 0, 8, 0, 256))
        tiles.append(("w_kv_mem", (l,), 0, 8, 256, 512))
    first_ffn(0, 0)
    tiles.append(("w_in_conv", (0,), 0, 8, 2304, 2560))
    for j in range(3):
        for part in (1, 2, 0):
            n = 768 * part + 256 * j
            tiles.append(("w_in_conv", (0,), 0, 8, n, n + 256))
    rows("w_out", (0,), 8, 0, D)
    first_ffn(0, 1)
    first_ffn(1, 0)
    tiles.append(("w_in_mlstm", (0,), 0, 8, 3072, 3080))
    tiles.append(("w_in_mlstm", (0,), 0, 8, 3080, 3336))
    rows("w_in_mlstm", (0,), 8, 1536, 2304)
    for h in range(4):
        for part in range(2):
            n = 768 * part + 192 * h
            tiles.append(("w_in_mlstm", (0,), 0, 8, n, n + 192))
    rows("w_in_mlstm", (0,), 8, 2304, 3072)
    rows("w_out", (1,), 8, 0, D)
    first_ffn(1, 1)

    rows("w_in_2", (0,), 8, 1536, 2208)
    for j in range(2):
        for part in range(2):
            n = 512 + 512 * part + 256 * j
            tiles.append(("w_in_2", (0,), 0, 8, n, n + 256))
    for j in range(2):
        tiles.append(("w_in_2", (0,), 0, 8, 256 * j, 256 * j + 256))
    tiles.append(("w_uq_2", (0,), 0, 3, 0, 512))
    tiles.append(("w_uq_2", (0,), 0, 3, 512, 768))
    tiles.append(("w_ukv_2", (0,), 0, 2, 0, D))
    for b, proj in enumerate(("pool_proj_2", "conv_proj_2", "mla_proj_2")):
        for j in range(2):
            tiles.append((proj, (0,), 0, 4, 512 * j, 512 * j + 512))
        for j in range(4):
            n = 2208 + 1024 * b + 256 * j
            tiles.append(("w_in_2", (0,), 0, 8, n, n + 256))
    rows("w_out_2", (0,), 8, 0, D)
    tiles.append(("w_router_2", (), 0, 8, 0, NEXP))
    rows("ple_gate_2", (0,), 8, 0, D)
    tiles.append(("ple_proj_2", (0,), 0, 2, 0, D))
    ffn("exp_w_up_2", "exp_w_up_2", "exp_w_down_2", lambda c: (0, c // 2), lambda c: (0, c // 2),
        lambda c: (0, c // 2), 2 * NEXP,
        lambda part, c: (512 * part + 256 * (c % 2), 512 * part + 256 * (c % 2) + 256),
        lambda c: (2 * (c % 2), 2 * (c % 2) + 2))
    return tiles


def tile_width(t):
    return (t[3] - t[2]) * (t[5] - t[4])


PARAMS = [("conv_w", 18), ("qkconv", 64), ("conv_dw", 124), ("conv_b", 4), ("conv_g", 4), ("conv_lb", 4),
          ("b_gate", 24), ("pool_scale", 4), ("q_g", 3), ("kv_g", 2), ("pool_w", 512),
          ("ident", 128), ("mask", 384), ("cnt", 64), ("invf", 16)]
POFF = {}
_o = 0
for _n, _w in PARAMS:
    POFF[_n] = (_o, _o + _w)
    _o += _w
NPAR = _o
ROWS = 8 + 16 + 768


class Queue:

    def __init__(self, sem):
        self.sem, self.count, self.items = sem, 0, []

    def __call__(self, fn, *after, sig=True):
        self.count += 1 if sig else 0
        self.items.append((flat(after), fn, (self.sem, 1) if sig else None))
        return (self.sem, self.count)

    def dma(self, out, in_, sem, *after):
        sem[1] += 16
        self.items.append((flat(after), lambda e: e.dma_start(out, in_), (sem[0], 16)))
        return (sem[0], sem[1])

    def wait(self, *after):
        self.items.append((flat(after), None, None))

    def emit(self, eng):
        seen = {}
        for after, fn, inc in self.items:
            for sem, value in after:
                if seen.get(id(sem), 0) < value:
                    eng.wait_ge(sem, value)
                    seen[id(sem)] = value
            if fn is not None:
                ins = fn(eng)
                if inc is not None:
                    ins.then_inc(*inc)


def flat(after):
    out = []
    for a in after:
        if a is None:
            continue
        if isinstance(a, list):
            out += flat(a)
        else:
            out.append(a)
    return out


class Bank:

    def __init__(self, t):
        self.t, self.free = t, []


def program(nc, A, out):
    f32, f32r, i32 = mybir.dt.float32, mybir.dt.float32r, mybir.dt.int32
    ACT = mybir.ActivationFunctionType
    X = mybir.AxisListType.X
    NR, NS, LOOK = 4, 3, 2

    ctx = ExitStack()
    with ctx:
        def sb(name, shape, dt=f32):
            return ctx.enter_context(nc.sbuf_tensor(name, shape, dt))

        def sem(name):
            return ctx.enter_context(nc.semaphore(name))

        raw = [sb(f"raw{i}", [128, TILE]) for i in range(NR)]
        whi = [sb(f"whi{i}", [128, TILE], f32r) for i in range(NS)]
        wlo = [sb(f"wlo{i}", [128, TILE], f32r) for i in range(NS)]
        x = sb("x", [128, 2, D])
        r = sb("r", [128, 2, D])
        xhi = sb("xhi", [128, 8, T], f32r)
        xlo = sb("xlo", [128, 8, T], f32r)
        mhi = sb("mhi", [128, 8, T], f32r)
        mlo = sb("mlo", [128, 8, T], f32r)
        hf = sb("hf", [128, 2, 2, T])
        hhi = sb("hhi", [128, 2, 2, T], f32r)
        hlo = sb("hlo", [128, 2, 2, T], f32r)
        gb = sb("gb", [128, 2, D])
        par = sb("par", [128, NPAR])
        brow = sb("brow", [128, 24])
        kT = sb("kT", [128, 2, 2, T])
        vm = sb("vm", [128, 2, 2, T])
        stat = sb("stat", [128, 2, 12])
        mv = sb("mv", [128, 2, 2])
        ve = sb("ve", [128, 2])
        rstd = sb("rstd", [128, 2])
        mhalf = sb("mhalf", [128, 8])
        posi = sb("posi", [128, 2], i32)
        cs = sb("cs", [128, 2, 2, 16])
        AR = 11600
        ar = sb("ar", [128, AR])
        W = [Bank(ctx.enter_context(nc.psum_tensor(f"psw{i}", [128, 512], f32))) for i in range(4)]
        Y = [Bank(ctx.enter_context(nc.psum_tensor(f"psy{i}", [128, 512], f32))) for i in range(4)]

        pe, act, dve, pool, sp = [Queue(sem(n)) for n in ("s_pe", "s_act", "s_dve", "s_pool", "s_sp")]
        s_raw = [[sem(f"s_raw{i}"), 0] for i in range(NR)]
        s_par, s_brow, s_pos, s_x, s_xT, s_mem, s_p = [[sem(n), 0] for n in
                                                        ("s_par", "s_brow", "s_pos", "s_x", "s_xT", "s_mem", "s_p")]
        s_gb, s_gbin, s_hn, s_out = [[sem(n), 0] for n in ("s_gb", "s_gbin", "s_hn", "s_out")]

        def P(name, a=0, b=None):
            lo, hi = POFF[name]
            return par[:, lo + a:(hi if b is None else lo + b)]

        ident = P("ident")

        class Arena:
            def __init__(self):
                self.at = 0

            def take(self, n):
                self.at += n
                assert self.at <= AR, self.at
                return ar[:, self.at - n:self.at]

        def blocks(ap, n):
            return ap.rearrange("p (b n) -> p b n", n=n)

        tiles = weight_tiles()
        offs = [0]
        for t in tiles:
            offs.append(offs[-1] + 128 * tile_width(t))
        raw_read = [None] * len(tiles)
        hi_done = [None] * len(tiles)
        lo_done = [None] * len(tiles)
        used = [None] * len(tiles)
        raw_in = [None] * len(tiles)
        state = {"load": 0, "split": 0, "use": 0, "w": 0}

        def load_tile():
            i = state["load"]
            if i >= len(tiles):
                return
            w = tile_width(tiles[i])
            src = A["ws"][offs[i]:offs[i + 1]].rearrange("(p c) -> p c", c=w)
            raw_in[i] = sp.dma(raw[i % NR][:, 0:w], src, s_raw[i % NR], raw_read[i - NR] if i >= NR else None)
            state["load"] += 1

        def split_tile():
            i = state["split"]
            if i >= len(tiles):
                return
            w = tile_width(tiles[i])
            src, hi, lo = raw[i % NR][:, 0:w], whi[i % NS][:, 0:w], wlo[i % NS][:, 0:w]
            free = used[i - NS] if i >= NS else None
            assert i < NS or free is not None
            hi_done[i] = act(lambda e: e.activation(hi, src, ACT.Copy), raw_in[i], free)
            lo_done[i] = dve(lambda e: e.tensor_tensor(lo, src, hi.bitcast(f32), ALU.subtract), hi_done[i], free)
            raw_read[i] = lo_done[i]
            state["split"] += 1
            load_tile()

        class Tile:

            def __init__(self, name, n0=None):
                self.i = i = state["use"]
                t = tiles[i]
                assert t[0] == name and (n0 is None or t[4] == n0), (t, name, n0)
                while state["split"] <= min(i + LOOK, len(tiles) - 1):
                    split_tile()
                state["use"] += 1
                self.kb, self.k0, self.n = t[3] - t[2], t[2], t[5] - t[4]
                w = tile_width(t)
                self.hi = blocks(whi[i % NS][:, 0:w], self.n)
                self.lo = blocks(wlo[i % NS][:, 0:w], self.n)
                self.ready = [hi_done[i], lo_done[i]]

            def done(self, ticket):
                used[self.i] = ticket

        for _ in range(NR):
            load_tile()

        def bank():
            state["w"] += 1
            return W[(state["w"] - 1) % 4]

        def mm(o, l, rr, start, stop, *after, sig=False):
            return pe(lambda e: e.matmul(o, l, rr, start=start, stop=stop), *after, sig=sig)

        def tr(o, i, n, *after, sig=False):
            return pe(lambda e: e.transpose(o, i, ident[0:n, 0:n]), *after, sig=sig)

        def cols(o, w, c0, m, hi, lo, *after):
            for k in range(w.kb):
                wh, wl = w.hi[:, k, c0:c0 + m], w.lo[:, k, c0:c0 + m]
                mm(o, wh, hi[:, k, :], k == 0, False, w.ready, *after)
                mm(o, wh, lo[:, k, :], False, False)
                tick = mm(o, wl, hi[:, k, :], False, k == w.kb - 1, sig=(k == w.kb - 1))
            return tick

        def pair(w, hi, lo, *after, m=128):
            b = bank()
            for j in range(w.n // m):
                tick = cols(b.t[0:m, 256 * j:256 * j + 256], w, m * j, m, hi, lo, b.free, *after)
            b.free = None
            w.done(tick)
            return b, tick

        def rowsof(w, hi, lo, k0, outs, first, last, *after):
            for t in range(2):
                mine = [(o, c0, c1) for tt, o, c0, c1 in outs if tt == t]
                for k in range(w.kb):
                    lh, ll = hi[:, k0 + k, 128 * t:128 * t + 128], lo[:, k0 + k, 128 * t:128 * t + 128]
                    st = first and k == 0
                    sp_ = last and k == w.kb - 1
                    for o, c0, c1 in mine:
                        mm(o, lh, w.hi[:, k, c0:c1], st, False, w.ready, *after)
                    for o, c0, c1 in mine:
                        mm(o, lh, w.lo[:, k, c0:c1], False, False)
                    for n, (o, c0, c1) in enumerate(mine):
                        tick = mm(o, ll, w.hi[:, k, c0:c1], False, sp_,
                                  sig=(k == w.kb - 1 and n == len(mine) - 1))
                if last:
                    yt[t] = tick
            w.done(tick)
            return tick

        yt = [None, None]

        def big_rows(name, ntile, hi, lo, *after, n=D, splits=((0, 512), (512, 1024)), n0=None):
            k = 0
            free = [b.free for b in Y]
            for j in range(ntile):
                w = Tile(name, n0)
                outs = [(t, Y[2 * t + i].t[:, 0:c1 - c0], c0, c1) for t in range(2) for i, (c0, c1) in enumerate(splits)]
                rowsof(w, hi, lo, k, outs, j == 0, j == ntile - 1, *(list(after) + free))
                k += w.kb
            return [yt[0], yt[1]]

        def split_to(hi, lo, src, *after, scale=1.0):
            a = act(lambda e: e.activation(hi, src, ACT.Copy, scale=scale), *after)
            if isinstance(scale, float):
                d = dve(lambda e: e.tensor_tensor(lo, src, hi.bitcast(f32), ALU.subtract), a)
            else:
                d = dve(lambda e: e.scalar_tensor_tensor(out=lo, in0=src, scalar=scale, in1=hi.bitcast(f32),
                                                         op0=ALU.mult, op1=ALU.subtract), a)
            return [a, d]

        t_par = act.dma(par[:, :], A["par"][:, :], s_par)
        t_x = act.dma(x[:, :, :], A["x"][0].rearrange("(t p) d -> p t d", p=128), s_x)
        t_pos = act.dma(posi[:, :], A["pos"][:, :], s_pos)
        t_brow = act.dma(brow[:, :], A["rows"][:, 0:24].broadcast_to((128, 24)), s_brow)
        first = Arena()
        memT = blocks(first.take(8 * T), T)
        xTr = blocks(first.take(8 * T), T)
        t_mem = act.dma(memT, blocks(A["memT"][:, :], T), s_mem)
        t_xT = act.dma(xTr, blocks(A["xT"][:, :], T), s_xT)
        t_gb = pool.dma(gb[:, :, :].rearrange("p a d -> p (a d)"), A["ln"][0:1, :].broadcast_to((128, 2 * D)), s_gb)
        t_mhalf = pool(lambda e: e.memset(mhalf[:, :], -0.5))

        t_m = split_to(mhi[:, :, :], mlo[:, :, :], memT, t_mem)
        kv_ready = []
        for l in range(2):
            w = Tile("w_kv_mem", 0)
            b, tk = pair(w, mhi, mlo, t_m)
            o = kT[:, l, :, :].rearrange("p b n -> p (b n)")
            e1 = act(lambda e, o=o, b=b: e.activation(o, b.t[:, :], ACT.Copy), tk)
            b.free = e1
            w = Tile("w_kv_mem", 256)
            b = bank()
            tk = rowsof(w, mhi, mlo, 0, [(t, b.t[:, 256 * t:256 * t + 256], 0, 256) for t in range(2)], True, True, b.free)
            o = vm[:, l, :, :].rearrange("p b n -> p (b n)")
            e2 = act(lambda e, o=o, b=b: e.activation(o, b.t[:, :], ACT.Copy), tk)
            b.free = e2
            kv_ready.append([e1, e2])

        cw = first.take(2 * 16 * 4).rearrange("p (s t n) -> p s t n", s=4, t=2)
        posf = first.take(2)
        ang, kk, rr, ab = [cw[:, i, :, :] for i in range(4)]
        tk = dve(lambda e: e.tensor_copy(posf, posi[:, :]), t_pos)
        for t in range(2):
            a1 = dve(lambda e, t=t: e.tensor_scalar(ang[:, t, :], P("invf"), posf[:, t:t + 1], None, ALU.mult), tk, t_par)
        MAGIC = 1.5 * 2.0 ** 23
        a2 = dve(lambda e: e.tensor_scalar(kk, ang, 1.0 / (2 * PI), MAGIC, ALU.mult, ALU.add), a1)
        a2 = dve(lambda e: e.tensor_scalar(kk, kk, MAGIC, None, ALU.subtract), a2)
        C1 = 6.28125
        C2 = float(np.float32(np.round((2 * PI - C1) * 2.0 ** 21) / 2.0 ** 21))
        C3 = float(2 * PI - C1 - C2)
        src = ang
        for c in (C1, C2, C3):
            a2 = dve(lambda e, c=c, src=src: e.scalar_tensor_tensor(out=rr, in0=kk, scalar=-c, in1=src,
                                                                    op0=ALU.mult, op1=ALU.add), a2)
            src = rr
        a2 = dve(lambda e: e.tensor_scalar(rr, rr, 3.1415925, -3.1415925, ALU.min, ALU.max), a2)
        a3 = dve(lambda e: e.scalar_tensor_tensor(out=ab, in0=rr, scalar=-1.0, in1=rr, op0=ALU.mult, op1=ALU.min), a2)
        a3 = dve(lambda e: e.tensor_scalar(ab, ab, PI / 2, None, ALU.add), a3)
        cosA = cs[:, 0, :, :]
        sinA = cs[:, 1, :, :]
        act(lambda e: e.activation(sinA, rr, ACT.Sin), a2)
        t_cs = act(lambda e: e.activation(cosA, ab, ACT.Sin), a3)

        xt_ready = [split_to(xhi[:, :, :], xlo[:, :, :], xTr, t_xT)]

        def scale_x(alpha, *after):
            return [pool(lambda e, t=t: e.tensor_scalar(x[:, t, :], x[:, t, :], alpha, None, ALU.mult), *after)
                    for t in range(2)]

        def ffn(gate, up, down, chunks, *after, weight=None):
            h_read = [None, None]
            pend = []

            def down_chunk():
                c, ready = pend.pop(0)
                w = Tile(down)
                s = c % 2
                outs = [(t, Y[2 * t + i].t[:, :], 512 * i, 512 * i + 512) for t in range(2) for i in range(2)]
                h_read[s] = rowsof(w, hhi[:, s, :, :], hlo[:, s, :, :], 0, outs, c == 0, c == chunks - 1, ready,
                                   [b.free for b in Y] if c == 0 else None)

            for c in range(chunks):
                s = c % 2
                wg = Tile(gate)
                bg, tg = pair(wg, xhi, xlo, *after)
                wu = Tile(up)
                bu, tu = pair(wu, xhi, xlo, *after)
                hs = hf[:, s, :, :].rearrange("p b n -> p (b n)")
                hh, hl = [q[:, s, :, :].rearrange("p b n -> p (b n)") for q in (hhi, hlo)]
                t1 = act(lambda e, hs=hs, bg=bg: e.activation(hs, bg.t[:, :], ACT.Silu), tg)
                t2 = dve(lambda e, hs=hs, bu=bu: e.tensor_tensor(hs, hs, bu.t[:, :], ALU.mult), t1, tu)
                bg.free, bu.free = t1, t2
                if weight is not None:
                    t2 = weight(c, hs, t2)
                if c:
                    down_chunk()
                pend.append((c, split_to(hh, hl, hs, t2, h_read[s])))
            down_chunk()
            return [yt[0], yt[1]]

        def layer_norm(ready, gbt, t_g, alpha, turn=True):
            g, bb = gbt[:, 0:D], gbt[:, D:2 * D]
            done, xt, free = [], [], []
            rs = []
            for t in range(2):
                for h in range(2):
                    s1 = dve(lambda e, t=t, h=h: e.bn_stats(stat[:, t, 6 * h:6 * h + 6], r[:, t, 512 * h:512 * h + 512]), ready[t])
                s2 = dve(lambda e, t=t: e.bn_aggr(mv[:, t, :], stat[:, t, :]), s1)
                s3 = dve(lambda e, t=t: e.tensor_scalar(ve[:, t:t + 1], mv[:, t, 1:2], LN_EPS, None, ALU.add), s2)
                rs.append(pool(lambda e, t=t: e.tensor_tensor(rstd[:, t:t + 1], ve[:, t:t + 1], mhalf[:, 0:1], ALU.pow), s3, t_mhalf))
            for t in range(2):
                n1 = dve(lambda e, t=t: e.tensor_scalar(x[:, t, :], r[:, t, :], mv[:, t, 0:1], rstd[:, t:t + 1],
                                                        ALU.subtract, ALU.mult), rs[t])
                n2 = dve(lambda e, t=t: e.tensor_tensor(x[:, t, :], x[:, t, :], g, ALU.mult), n1, t_g)
                n3 = dve(lambda e, t=t: e.tensor_tensor(x[:, t, :], x[:, t, :], bb, ALU.add), n2)
                done.append(n3)
                if turn:
                    for q in range(2):
                        b = bank()
                        for k in range(4):
                            kb = 4 * q + k
                            tk = tr(b.t[:, 128 * k:128 * k + 128], x[:, t, 128 * kb:128 * kb + 128], 128, n3, b.free,
                                    sig=(k == 3))
                        o = [z[:, 4 * q:4 * q + 4, 128 * t:128 * t + 128] for z in (xhi, xlo)]
                        ev = split_to(o[0], o[1], blocks(b.t[:, :], 128), tk)
                        b.free = ev
                        xt.append(ev)
                        free.append(tk)
            if turn:
                t_ax = [pool(lambda e, t=t: e.tensor_scalar(x[:, t, :], x[:, t, :], alpha, None, ALU.mult), free[2 * t + 1])
                        for t in range(2)]
                return done, xt, t_ax
            return done, None, None

        def residual(ticks, t_ax, half):
            out_ = []
            for t in range(2):
                for i in range(2):
                    o = r[:, t, 512 * i:512 * i + 512]
                    xa = x[:, t, 512 * i:512 * i + 512]
                    y = Y[2 * t + i]
                    if half:
                        q = dve(lambda e, o=o, xa=xa, y=y: e.scalar_tensor_tensor(out=o, in0=y.t[:, :], scalar=0.5, in1=xa,
                                                                                  op0=ALU.mult, op1=ALU.add), ticks[t], t_ax[t])
                    else:
                        q = dve(lambda e, o=o, xa=xa, y=y: e.tensor_tensor(o, y.t[:, :], xa, ALU.add), ticks[t], t_ax[t])
                    y.free = q
                out_.append(q)
            return out_

        def next_gb(k, *after):
            return pool.dma(gb[:, :, :].rearrange("p a d -> p (a d)"), A["ln"][k:k + 1, :].broadcast_to((128, 2 * D)), s_gb, *after)

        gbv = gb[:, :, :].rearrange("p a d -> p (a d)")

        def mem_attention(l, qT, t_q, arena, between, over=None):
            pbuf = arena.take(8 * T).rearrange("p (h t n) -> p h t n", h=4, t=2)
            pT = [arena.take(2 * T).rearrange("p (m n) -> p m n", m=2) for _ in range(2)]
            ob = arena.take(2 * T).rearrange("p (t n) -> p t n", t=2)
            mx = arena.take(8)
            sm = arena.take(8)
            ri = arena.take(8)
            ex = []
            for h in range(4):
                b = bank()
                s, blk = 64 * (h % 2), h // 2
                for t in range(2):
                    tk = mm(b.t[:, 256 * t:256 * t + 256], qT[s:s + 64, blk, 128 * t:128 * t + 128], kT[s:s + 64, l, blk, :],
                            True, True, t_q, kv_ready[l], b.free, sig=(t == 1))
                m2 = mx[:, 2 * h:2 * h + 2]
                t1 = dve(lambda e, b=b, m2=m2: e.tensor_reduce(m2, blocks(b.t[:, :], 256), X, ALU.max, negate=True), tk, over)
                t2 = dve(lambda e, m2=m2: e.tensor_scalar(m2, m2, 0.125, None, ALU.mult), t1)
                for t in range(2):
                    t3 = act(lambda e, b=b, h=h, t=t: e.activation(pbuf[:, h, t, :], b.t[:, 256 * t:256 * t + 256], ACT.Exp,
                                                                   bias=mx[:, 2 * h + t:2 * h + t + 1], scale=0.125,
                                                                   accum_out=sm[:, 2 * h + t:2 * h + t + 1]), t2, over)
                b.free = t3
                ex.append(t3)
            between()
            t_r = dve(lambda e: e.reciprocal(ri, sm), ex[-1])
            o_b = bank()
            o_free = o_b.free
            pv = [None, None]
            for h in range(4):
                b = bank()
                if b is o_b:
                    b = bank()
                for m in range(2):
                    for t in range(2):
                        tk = tr(b.t[:, 256 * m + 128 * t:256 * m + 128 * t + 128], pbuf[:, h, t, 128 * m:128 * m + 128], 128,
                                ex[h], b.free, sig=(m == 1 and t == 1))
                p2 = pT[h % 2]
                ev = act(lambda e, b=b, p2=p2: e.activation(p2.rearrange("p m n -> p (m n)"), b.t[:, :], ACT.Copy), tk, pv[h % 2])
                b.free = ev
                for t in range(2):
                    for m in range(2):
                        c = 256 * t + 64 * h
                        pv[h % 2] = mm(o_b.t[:, c:c + 64], p2[:, m, 128 * t:128 * t + 128], vm[:, l, m, 64 * h:64 * h + 64],
                                       m == 0, m == 1, ev, o_free, sig=(t == 1 and m == 1))
            for t in range(2):
                rv = ri.rearrange("p (h t) -> p t h", t=2)[:, t, :].unsqueeze(2).to_broadcast([128, 4, 64])
                t4 = dve(lambda e, t=t, rv=rv: e.tensor_tensor(ob[:, t, :].rearrange("p (h n) -> p h n", n=64),
                                                               o_b.t[:, 256 * t:256 * t + 256].rearrange("p (h n) -> p h n", n=64),
                                                               rv, ALU.mult), pv[1], t_r)
            o_b.free = t4
            b = bank()
            for k in range(2):
                for t in range(2):
                    tk = tr(b.t[:, 256 * k + 128 * t:256 * k + 128 * t + 128], ob[:, t, 128 * k:128 * k + 128], 128, t4, b.free,
                            sig=(k == 1 and t == 1))
            ev = split_to(mhi[:, 6:8, :], mlo[:, 6:8, :], blocks(b.t[:, :], 256), tk)
            b.free = ev
            return ev

        def xa_queries(name, n0, qT, *after):
            w = Tile(name, n0)
            b, tk = pair(w, xhi, xlo, *after)
            b.free = act(lambda e: e.activation(qT.rearrange("p b n -> p (b n)"), b.t[:, :], ACT.Copy), tk)
            return b.free

        def conv_mixer(t_xt):
            arena = Arena()
            qT = arena.take(2 * T).rearrange("p (b n) -> p b n", b=2)
            t_q = xa_queries("w_in_conv", 2304, qT, t_xt)
            cb = arena.take(2 * T)
            z = [arena.take(2 * 258).rearrange("p (b n) -> p b n", b=2) for _ in range(2)]
            acc = [arena.take(2 * T).rearrange("p (b n) -> p b n", b=2) for _ in range(2)]
            cwt = P("conv_w").rearrange("p (b w) -> p b w", w=3)
            zz = [pool(lambda e, q=q: e.memset(z[q][:, :, 0:2], 0.0), t_q) for q in range(2)]
            done = []

            def part(j):
                q = j % 2
                bc, tc = pair(Tile("w_in_conv", 768 + 256 * j), xhi, xlo)
                t1 = act(lambda e: e.activation(cb, bc.t[:, :], ACT.Copy), tc, done[j - 1] if j else None)
                bc.free = t1
                bx, tx = pair(Tile("w_in_conv", 1536 + 256 * j), xhi, xlo)
                t2 = dve(lambda e: e.tensor_tensor(z[q][:, :, 2:258], blocks(cb, 256), blocks(bx.t[:, :], 256), ALU.mult), t1, tx)
                bx.free = t2
                for f in range(2):
                    blk = 2 * j + f
                    t3 = dve(lambda e, f=f, blk=blk: e.tensor_scalar(acc[q][:, f, :], z[q][:, f, 2:258], cwt[:, blk, 2:3], None,
                                                                     ALU.mult), t2, zz[q])
                    for s in range(2):
                        t3 = dve(lambda e, f=f, blk=blk, s=s: e.scalar_tensor_tensor(
                            out=acc[q][:, f, :], in0=z[q][:, f, s:s + 256], scalar=cwt[:, blk, s:s + 1], in1=acc[q][:, f, :],
                            op0=ALU.mult, op1=ALU.add), t3)
                bb, tb = pair(Tile("w_in_conv", 256 * j), xhi, xlo)
                t4 = dve(lambda e: e.tensor_tensor(acc[q], acc[q], blocks(bb.t[:, :], 256), ALU.mult), t3, tb)
                bb.free = t4
                done.append(split_to(mhi[:, 2 * j:2 * j + 2, :], mlo[:, 2 * j:2 * j + 2, :], acc[q], t4))

            def between():
                part(0)
                part(1)

            o = mem_attention(0, qT, t_q, arena, between)
            part(2)
            return [o, done]

        def mlstm_mixer(t_xt, t_prev):
            arena = Arena()
            qT = arena.take(2 * T).rearrange("p (b n) -> p b n", b=2)
            hn = arena.take(768)
            t_hn = pool.dma(hn, A["rows"][:, 24:792].broadcast_to((128, 768)), s_hn, t_prev)
            sel = arena.take(512)[0:4].rearrange("p (h n) -> p h n", h=4)
            s0 = pool(lambda e: e.memset(sel, 0.0), t_prev)
            t_sel = pool(lambda e: e.affine_select(out=sel, in_=sel, compare_op=ALU.not_equal, fill=1.0, base=0,
                                                   pattern=[[-1, 4], [0, 128]], channel_multiplier=1), s0)
            gt = arena.take(16).rearrange("p (t n) -> p t n", t=2)
            w = Tile("w_in_mlstm", 3072)
            b = bank()
            tk = rowsof(w, xhi, xlo, 0, [(t, b.t[:, 8 * t:8 * t + 8], 0, 8) for t in range(2)], True, True, t_xt, b.free)
            gb8 = brow[:, 0:8].unsqueeze(1).to_broadcast([128, 2, 8])
            t1 = dve(lambda e, b=b: e.tensor_tensor(gt, blocks(b.t[:, 0:16], 8), gb8, ALU.add), tk, t_brow)
            b.free = t1
            t_q = xa_queries("w_in_mlstm", 3080, qT)
            gb_ = bank()
            for t in range(2):
                for part in range(2):
                    tk = tr(gb_.t[0:4, 256 * part + 128 * t:256 * part + 128 * t + 128], gt[:, t, 4 * part:4 * part + 4], 128,
                            t1, gb_.free, sig=(t == 1 and part == 1))
            gs = arena.take(8 * T).rearrange("p (s n) -> p s n", s=8)[0:4]
            li, z, e1, lf, B, aa, AA, em = [gs[:, i, :] for i in range(8)]
            t2 = dve(lambda e: e.tensor_copy(gs[:, 0:2, :], blocks(gb_.t[0:4, :], 256)), tk)
            gb_.free = t2
            t3 = dve(lambda e: e.scalar_tensor_tensor(out=e1, in0=z, scalar=-1.0, in1=z, op0=ALU.mult, op1=ALU.max), t2)
            t4 = act(lambda e: e.activation(e1, e1, ACT.Exp, scale=-1.0), t3)
            t4 = act(lambda e: e.activation(e1, e1, ACT.Ln, bias=1.0), t4)
            t5 = dve(lambda e: e.scalar_tensor_tensor(out=lf, in0=z, scalar=0.0, in1=e1, op0=ALU.min, op1=ALU.subtract), t4)
            one = em
            t6 = dve(lambda e: e.memset(one, 1.0))
            t6 = dve(lambda e: e.tensor_tensor_scan(B, one, lf, 0.0, ALU.mult, ALU.add), t5, t6)
            t7 = dve(lambda e: e.tensor_tensor(aa, li, B, ALU.subtract), t6)
            t8 = dve(lambda e: e.tensor_tensor_scan(AA, aa, aa, 0.0, ALU.max, ALU.max), t7)
            t9 = dve(lambda e: e.tensor_tensor(em, AA, B, ALU.add), t8)
            t9 = act(lambda e: e.activation(em, em, ACT.Exp, scale=-1.0), t9)
            cb = bank()
            for t in range(2):
                for i, s in enumerate((aa, em)):
                    tk = tr(cb.t[:, 8 * t + 4 * i:8 * t + 4 * i + 4], s[:, 128 * t:128 * t + 128], 4, t8, t9, cb.free,
                            sig=(t == 1 and i == 1))
            ac = arena.take(16).rearrange("p (t n) -> p t n", t=2)
            t10 = dve(lambda e: e.tensor_copy(ac, blocks(cb.t[:, 0:16], 8)), tk)
            cb.free = t10
            wt = arena.take(4 * 384).rearrange("p (h n) -> p h n", h=4)
            t_wt = []
            for h in range(4):
                b = bank()
                tk = mm(b.t[:, 0:256], sel[:, h, :], AA, True, True, t8, t_sel, b.free, sig=True)
                a1 = act(lambda e, h=h, b=b: e.activation(wt[:, h, 0:256], b.t[:, 0:256], ACT.Exp, bias=ac[:, 0, h:h + 1],
                                                          scale=-1.0), tk, t10)
                a2 = act(lambda e, h=h, b=b: e.activation(wt[:, h, 256:384], b.t[:, 128:256], ACT.Exp, bias=ac[:, 1, h:h + 1],
                                                          scale=-1.0), tk, t10)
                b.free = a2
                for c in (0, 256):
                    a3 = pool(lambda e, h=h, c=c: e.affine_select(out=wt[:, h, c:c + 128], in_=wt[:, h, c:c + 128],
                                                                  compare_op=ALU.is_ge, fill=0.0, base=0, pattern=[[1, 128]],
                                                                  channel_multiplier=-1), a1, a2)
                t_wt.append(a3)
            va = arena.take(2 * 4 * 194).rearrange("p (t h n) -> p t h n", t=2, h=4)
            t_one = pool(lambda e: e.memset(va[:, :, :, 192:194], 1.0), t1)
            ty = big_rows("w_in_mlstm", 4, xhi, xlo, n=768, splits=((0, 384), (384, 768)), n0=1536)
            t_v = []
            for t in range(2):
                for i in range(2):
                    y = Y[2 * t + i]
                    y.free = act(lambda e, t=t, i=i, y=y: e.activation(va[:, t, 2 * i:2 * i + 2, 0:192],
                                                                       blocks(y.t[:, 0:384], 192), ACT.Copy), ty[t])
                    t_v.append(y.free)
            hb = r[:, :, 0:768].rearrange("p t (h n) -> p t h n", h=4)
            cwt = P("qkconv").rearrange("p (b w) -> p b w", w=4)
            zp = [arena.take(2 * 259).rearrange("p (b n) -> p b n", b=2)[0:96] for _ in range(2)]
            zz = [pool(lambda e, q=q: e.memset(zp[q][:, :, 0:3], 0.0), t1) for q in range(2)]
            qk = [arena.take(2 * T).rearrange("p (b n) -> p b n", b=2)[0:96] for _ in range(2)]
            sc = arena.take(384)
            den = arena.take(16).rearrange("p (t h) -> p t h", t=2)
            t_h = []
            pv = None
            qk_read = None
            conv_read = [None, None]

            def head(h):
                nonlocal pv, qk_read
                ready = []
                for part in range(2):
                    b, tk = pair(Tile("w_in_mlstm", 768 * part + 192 * h), xhi, xlo, m=96)
                    z_ = zp[part]
                    c1 = act(lambda e, z_=z_, b=b: e.activation(z_[:, :, 3:259], blocks(b.t[0:96, :], 256), ACT.Copy),
                             tk, conv_read[part])
                    b.free = c1
                    for f in range(2):
                        blk = 8 * part + 2 * h + f
                        o = qk[part][:, f, :]
                        c2 = dve(lambda e, f=f, blk=blk, o=o, z_=z_: e.tensor_scalar(o, z_[:, f, 3:259], cwt[0:96, blk, 3:4], None,
                                                                                     ALU.mult), c1, zz[part], qk_read)
                        for s in range(3):
                            c2 = dve(lambda e, f=f, blk=blk, s=s, o=o, z_=z_: e.scalar_tensor_tensor(
                                out=o, in0=z_[:, f, s:s + 256], scalar=cwt[0:96, blk, s:s + 1], in1=o, op0=ALU.mult,
                                op1=ALU.add), c2)
                    conv_read[part] = c2
                    ready.append(act(lambda e, part=part: e.activation(qk[part], qk[part], ACT.Silu), c2))
                return ready

            def attend(h, ready):
                nonlocal pv, qk_read
                b = bank()
                for f in range(2):
                    mm(b.t[:, 0:256], qk[1][:, f, 0:128], qk[0][:, f, :], f == 0, f == 1, ready, b.free)
                for f in range(2):
                    tk = mm(b.t[:, 256:384], qk[1][:, f, 128:256], qk[0][:, f, 128:256], f == 0, f == 1, sig=(f == 1))
                qk_read = tk
                s1 = dve(lambda e: e.scalar_tensor_tensor(out=sc, in0=b.t[:, 0:384], scalar=192.0 ** -0.5, in1=wt[:, h, :],
                                                          op0=ALU.mult, op1=ALU.mult), tk, t_wt[h], pv)
                b.free = s1
                nb = bank()
                mm(nb.t[:, 0:193], sc[:, 0:128], va[:, 0, h, 0:193], True, True, s1, t_v, t_one, nb.free)
                mm(nb.t[:, 256:449], sc[:, 128:256], va[:, 0, h, 0:193], True, False)
                pv = mm(nb.t[:, 256:449], sc[:, 256:384], va[:, 1, h, 0:193], False, True, sig=True)
                for t in range(2):
                    c = 256 * t
                    d1 = dve(lambda e, t=t, c=c: e.tensor_scalar(den[:, t, h:h + 1], nb.t[:, c + 192:c + 193], -1.0,
                                                                 ac[:, t, 4 + h:5 + h], ALU.mult, ALU.max), pv)
                    d1 = dve(lambda e, t=t, c=c: e.tensor_tensor(den[:, t, h:h + 1], nb.t[:, c + 192:c + 193],
                                                                 den[:, t, h:h + 1], ALU.max), d1)
                    d1 = dve(lambda e, t=t: e.reciprocal(den[:, t, h:h + 1], den[:, t, h:h + 1]), d1)
                    d2 = dve(lambda e, t=t, c=c: e.tensor_scalar(hb[:, t, h, :], nb.t[:, c:c + 192], den[:, t, h:h + 1], None,
                                                                 ALU.mult), d1)
                nb.free = d2
                return d2

            for h in range(4):
                ready = head(h)
                t_h.append(attend(h, ready))

            ty = big_rows("w_in_mlstm", 4, xhi, xlo, n=768, splits=((0, 384), (384, 768)), n0=2304)
            hst = arena.take(2 * 4 * 6).rearrange("p (t h n) -> p t h n", t=2, h=4)
            hmv = arena.take(2 * 4 * 2).rearrange("p (t h n) -> p t h n", t=2, h=4)
            hve = arena.take(16)
            for t in range(2):
                for h in range(4):
                    d1 = dve(lambda e, t=t, h=h: e.bn_stats(hst[:, t, h, :], hb[:, t, h, :]), t_h)
            for t in range(2):
                for h in range(4):
                    d2 = dve(lambda e, t=t, h=h: e.bn_aggr(hmv[:, t, h, :], hst[:, t, h, :]), d1)
            d3 = dve(lambda e: e.tensor_scalar(hve[:, 0:8].rearrange("p (t h) -> p t h", t=2), hmv[:, :, :, 1], LN_EPS, None, ALU.add), d2)
            d4 = pool(lambda e: e.tensor_tensor(hve[:, 8:16], hve[:, 0:8], mhalf[:, :], ALU.pow), d3, t_mhalf)
            og = wt.rearrange("p h n -> p (h n)")[:, 0:1536].rearrange("p (t n) -> p t n", t=2)
            for t in range(2):
                for h in range(4):
                    d5 = dve(lambda e, t=t, h=h: e.tensor_scalar(hb[:, t, h, :], hb[:, t, h, :], hmv[:, t, h, 0:1],
                                                                 hve[:, 8 + 4 * t + h:9 + 4 * t + h], ALU.subtract, ALU.mult), d4)
            for t in range(2):
                hv = hb[:, t, :, :].rearrange("p h n -> p (h n)")
                d6 = dve(lambda e, hv=hv: e.tensor_tensor(hv, hv, hn, ALU.mult), d5, t_hn)
                for i in range(2):
                    y = Y[2 * t + i]
                    a6 = act(lambda e, t=t, i=i, y=y: e.activation(og[:, t, 384 * i:384 * i + 384], y.t[:, 0:384], ACT.Sigmoid),
                             ty[t], t_h)
                    y.free = a6
                d7 = dve(lambda e, t=t, hv=hv: e.tensor_tensor(hv, hv, og[:, t, :], ALU.mult), d6, a6)
            done = []
            for q in range(3):
                b = bank()
                for k in range(2):
                    for t in range(2):
                        hv = hb[:, t, :, :].rearrange("p h n -> p (h n)")
                        tk = tr(b.t[:, 256 * k + 128 * t:256 * k + 128 * t + 128], hv[:, 128 * (2 * q + k):128 * (2 * q + k) + 128],
                                128, d7, b.free, sig=(k == 1 and t == 1))
                ev = split_to(mhi[:, 2 * q:2 * q + 2, :], mlo[:, 2 * q:2 * q + 2, :], blocks(b.t[:, :], 256), tk)
                b.free = ev
                done.append(ev)
            ar2 = Arena()
            ar2.at = 2 * T
            o = mem_attention(1, qT, t_q, ar2, lambda: None, done)
            return [o, done]

        t_ax = scale_x(ALPHA1, t_x)
        for l in range(2):
            ty = ffn("ffn_w_gate", "ffn_w_up", "ffn_w_down", FF // 256, xt_ready)
            rt = residual(ty, t_ax, True)
            done, xt_ready, t_ax = layer_norm(rt, gbv, t_gb, ALPHA1)
            t_gb = next_gb(3 * l + 1, done)
            mix = conv_mixer(xt_ready) if l == 0 else mlstm_mixer(xt_ready, done)
            ty = big_rows("w_out", 4, mhi, mlo, mix)
            rt = residual(ty, t_ax, False)
            done, xt_ready, t_ax = layer_norm(rt, gbv, t_gb, ALPHA1)
            t_gb = next_gb(3 * l + 2, done)
            ty = ffn("ffn_w_gate", "ffn_w_up", "ffn_w_down", FF // 256, xt_ready)
            rt = residual(ty, t_ax, True)
            if l == 0:
                done, xt_ready, t_ax = layer_norm(rt, gbv, t_gb, ALPHA1)
                t_gb = next_gb(3, done)
        gin = ar[:, 0:2 * D]
        t_gin = pool.dma(gin, A["ln"][6:7, :].broadcast_to((128, 2 * D)), s_gbin, t_ax)
        done, _, _ = layer_norm(rt, gbv, t_gb, None, turn=False)
        t_gb = next_gb(7, done)
        cp = [act(lambda e, t=t: e.activation(r[:, t, :], x[:, t, :], ACT.Copy), done[t]) for t in range(2)]
        done, xt_ready, t_ax = layer_norm(cp, gin, t_gin, ALPHA2)

        arena = Arena()
        ty = big_rows("w_in_2", 4, xhi, xlo, xt_ready, n=672, splits=((0, 384), (384, 672)))
        va = ar[:, 0:1024].rearrange("p (t h n) -> p t h n", t=2, h=8)
        cq = arena.take(2 * 384).rearrange("p (t n) -> p t n", t=2)
        ck = arena.take(2 * 288).rearrange("p (t n) -> p t n", t=2)
        ss = arena.take(8)
        hfl = hf[:, :, :, :].rearrange("p a b n -> p (a b n)")
        junk = hfl[:, 512:896]
        tmp = arena.take(4 * 128).rearrange("p (s n) -> p s n", s=4)
        q1 = None
        for t in range(2):
            for i, wdt in ((0, 384), (1, 256)):
                y = Y[2 * t + i]
                q1 = act(lambda e, t=t, i=i, wdt=wdt, y=y: e.activation(junk[:, 0:wdt], y.t[:, 0:wdt], ACT.Square,
                                                                        accum_out=ss[:, 2 * t + i:2 * t + i + 1]), ty[t], done, q1)
        for i, wdt in ((0, 384), (1, 256)):
            sv = ss[:, 0:4].rearrange("p (t i) -> p t i", i=2)[:, :, i]
            q2 = dve(lambda e, sv=sv, wdt=wdt: e.tensor_scalar(sv, sv, 1.0 / wdt, RMS_EPS, ALU.mult, ALU.add), q1)
        q3 = pool(lambda e: e.tensor_tensor(ss[:, 4:8], ss[:, 0:4], mhalf[:, 0:4], ALU.pow), q2, t_mhalf)
        for t in range(2):
            for i, o, wdt in ((0, cq, 384), (1, ck, 256)):
                y = Y[2 * t + i]
                q4 = dve(lambda e, t=t, i=i, o=o, wdt=wdt, y=y: e.tensor_scalar(o[:, t, 0:wdt], y.t[:, 0:wdt],
                                                                                 ss[:, 4 + 2 * t + i:5 + 2 * t + i], None, ALU.mult), q3)
                y.free = q4
        t_kr = None
        kr = arena.take(2 * 32).rearrange("p (t n) -> p t n", t=2)
        for t in range(2):
            y = Y[2 * t + 1]
            y1, y2 = y.t[:, 256:272], y.t[:, 272:288]
            c_, s_ = cosA[:, t, :], sinA[:, t, :]
            q5 = dve(lambda e, y1=y1, c_=c_: e.tensor_tensor(tmp[:, 0, 0:16], y1, c_, ALU.mult), q4, t_cs, t_kr)
            q5 = dve(lambda e, y2=y2, s_=s_: e.tensor_tensor(tmp[:, 1, 0:16], y2, s_, ALU.mult))
            q5 = dve(lambda e, y2=y2, c_=c_: e.tensor_tensor(tmp[:, 2, 0:16], y2, c_, ALU.mult))
            q5 = dve(lambda e, y1=y1, s_=s_: e.tensor_tensor(tmp[:, 3, 0:16], y1, s_, ALU.mult))
            y.free = q5
            dve(lambda e, t=t: e.tensor_tensor(kr[:, t, 0:16], tmp[:, 0, 0:16], tmp[:, 1, 0:16], ALU.subtract), q5)
            t_kr = dve(lambda e, t=t: e.tensor_tensor(kr[:, t, 16:32], tmp[:, 2, 0:16], tmp[:, 3, 0:16], ALU.add), q5)
        t_lat = []
        for i, o, nb_, g in ((0, cq, 3, "q_g"), (1, ck, 2, "kv_g")):
            for k in range(nb_):
                b = bank()
                for t in range(2):
                    tk = tr(b.t[:, 128 * t:128 * t + 128], o[:, t, 128 * k:128 * k + 128], 128, q4, b.free, sig=(t == 1))
                dst = (mhi[:, 4 + k, :], mlo[:, 4 + k, :]) if i == 0 else (hhi[:, 0, k, :], hlo[:, 0, k, :])
                ev = split_to(dst[0], dst[1], b.t[:, 0:256], tk, scale=P(g, k, k + 1))
                b.free = ev
                t_lat.append(ev)

        zc = arena.take(4 * 286).rearrange("p (b n) -> p b n", b=4)
        ca = arena.take(4 * T).rearrange("p (b n) -> p b n", b=4)
        sg = hfl[:, 0:512]
        dwt = P("conv_dw").rearrange("p (b w) -> p b w", w=31)
        z0 = pool(lambda e: e.memset(zc[:, :, 0:30], 0.0), done)
        t_z, t_c = [], [None] * 4
        sg_read = None
        for j in range(2):
            ba, ta = pair(Tile("w_in_2", 512 + 256 * j), xhi, xlo)
            bg, tg = pair(Tile("w_in_2", 1024 + 256 * j), xhi, xlo)
            s1 = act(lambda e, bg=bg: e.activation(sg, bg.t[:, :], ACT.Sigmoid), tg, sg_read)
            bg.free = s1
            s2 = dve(lambda e, j=j, ba=ba: e.tensor_tensor(zc[:, 2 * j:2 * j + 2, 30:286], blocks(sg, 256),
                                                           blocks(ba.t[:, :], 256), ALU.mult), s1, ta, z0)
            ba.free = s2
            sg_read = s2
            t_z.append(s2)
        conv_steps = [(b, w) for b in range(4) for w in range(31)]

        def conv_some(n):
            for _ in range(min(n, len(conv_steps))):
                b, w = conv_steps.pop(0)
                if w == 0:
                    t_c[b] = dve(lambda e, b=b: e.tensor_scalar(ca[:, b, :], zc[:, b, 0:256], dwt[:, b, 0:1], P("conv_b", b, b + 1),
                                                                ALU.mult, ALU.add), t_z[b // 2])
                else:
                    t_c[b] = dve(lambda e, b=b, w=w: e.scalar_tensor_tensor(
                        out=ca[:, b, :], in0=zc[:, b, w:w + 256], scalar=dwt[:, b, w:w + 1], in1=ca[:, b, :],
                        op0=ALU.mult, op1=ALU.add), t_c[b])

        up_ = arena.take(4 * 272).rearrange("p (b n) -> p b n", b=4)
        wsum = arena.take(4 * 272).rearrange("p (b n) -> p b n", b=4)
        p0 = pool(lambda e: e.memset(up_[:, :, 0:16], 0.0), done)
        for j in range(2):
            b, tk = pair(Tile("w_in_2", 256 * j), xhi, xlo)
            ev = act(lambda e, j=j, b=b: e.activation(up_[:, 2 * j:2 * j + 2, 16:272], blocks(b.t[:, :], 256), ACT.Copy), tk)
            b.free = ev
            conv_some(8)
        wt2 = arena.take(4 * 272).rearrange("p (b n) -> p b n", b=4)
        t_pl = []
        for g in range(4):
            src, cur = up_[:, g, :], ev
            bufs = [wsum[:, g, :], wt2[:, g, :]]
            lo = 0
            for s in range(g + 1):
                step = 1 << s
                dst = bufs[s % 2]
                lo += step
                cur = pool(lambda e, dst=dst, src=src, lo=lo, step=step: e.tensor_tensor(
                    dst[:, lo:272], src[:, lo:272], src[:, lo - step:272 - step], ALU.add), cur, p0)
                src = dst
            o = wt2[:, g, :] if g % 2 == 0 else wsum[:, g, :]
            cur = pool(lambda e, src=src, o=o, g=g: e.tensor_tensor(o[:, 16:32], src[:, 16:32], P("cnt", 16 * g, 16 * g + 16), ALU.mult), cur)
            cu2 = pool(lambda e, src=src, o=o, g=g: e.tensor_scalar(o[:, 32:272], src[:, 32:272], 1.0 / (2 << g), None, ALU.mult), cur)
            cur = pool(lambda e, o=o, g=g: e.tensor_tensor(o[:, 16:272], o[:, 16:272], up_[:, g, 16:272], ALU.subtract), cur, cu2)
            t_pl.append((o, cur))

        qf = arena.take(2 * 768).rearrange("p (t h n) -> p t h n", t=2, h=8)
        kf = r[:, :, 0:768].rearrange("p t (h n) -> p t h n", h=8)
        free = [b.free for b in Y]
        for i, wdt in ((0, 512), (1, 256)):
            w = Tile("w_uq_2", 512 * i)
            tk = rowsof(w, mhi[:, 4:7, :], mlo[:, 4:7, :], 0, [(t, Y[2 * t + i].t[:, 0:wdt], 0, wdt) for t in range(2)], True, True,
                        t_lat, free)
            conv_some(8)
            for t in range(2):
                y = Y[2 * t + i]
                o = qf[:, t, :, :].rearrange("p h n -> p (h n)")[:, 512 * i:512 * i + wdt]
                y.free = act(lambda e, o=o, wdt=wdt, y=y: e.activation(o, y.t[:, 0:wdt], ACT.Copy), tk)
                q6 = y.free
        t_q = []
        for t in range(2):
            x1, x2 = qf[:, t, :, 64:80], qf[:, t, :, 80:96]
            tv = [tmp[:, s, :].rearrange("p (h n) -> p h n", h=8) for s in range(4)]
            cb_ = cosA[:, t, :].unsqueeze(1).to_broadcast([128, 8, 16])
            sb_ = sinA[:, t, :].unsqueeze(1).to_broadcast([128, 8, 16])
            m = [pool(lambda e, o=o, a=a, c=c: e.tensor_tensor(o, a, c, ALU.mult), q6, t_cs, t_kr, t_q)
                 for o, a, c in ((tv[0], x1, cb_), (tv[1], x2, sb_), (tv[2], x2, cb_), (tv[3], x1, sb_))]
            m1 = pool(lambda e, x1=x1, tv=tv: e.tensor_tensor(x1, tv[0], tv[1], ALU.subtract), m[-1])
            t_q = [pool(lambda e, x2=x2, tv=tv: e.tensor_tensor(x2, tv[2], tv[3], ALU.add), m1)]
        ty = big_rows("w_ukv_2", 1, hhi[:, 0, :, :], hlo[:, 0, :, :], t_lat)
        t_k, t_v = [], []
        for t in range(2):
            for i in range(2):
                y = Y[2 * t + i]
                yv = y.t[:, :].rearrange("p (h n) -> p h n", h=4)
                a1 = act(lambda e, t=t, i=i, yv=yv: e.activation(kf[:, t, 4 * i:4 * i + 4, 0:64], yv[:, :, 0:64], ACT.Copy), ty[t])
                y.free = act(lambda e, t=t, i=i, yv=yv: e.activation(va[:, t, 4 * i:4 * i + 4, :], yv[:, :, 64:128], ACT.Copy), ty[t])
                t_k.append(y.free)
            krb = kr[:, t, :].unsqueeze(1).to_broadcast([128, 8, 32])
            t_k.append(pool(lambda e, t=t, krb=krb: e.tensor_copy(kf[:, t, :, 64:96], krb), t_kr, ty))
        conv_some(12)

        mg = arena.take(8 * T).rearrange("p (b n) -> p b n", b=8)
        gs = arena.take(2 * T)
        gp = tmp.rearrange("p s n -> p (s n)")
        st = {"gs": None, "mg": [None] * 4}

        def branch(n, name, hi, lo, ready, extra):
            free_ = [b.free for b in Y]
            for j in range(2):
                w = Tile(name, 512 * j)
                for f in range(4):
                    blk = 4 * j + f
                    tk = cols(Y[blk // 2].t[:, 256 * (blk % 2):256 * (blk % 2) + 256], w, 128 * f, 128, hi, lo, ready, free_)
                w.done(tk)
                extra()
            for j in range(4):
                b, tg = pair(Tile("w_in_2", 2208 + 1024 * n + 256 * j), xhi, xlo)
                for f in range(2):
                    s1 = act(lambda e, f=f, j=j, b=b: e.activation(gs[:, 256 * f:256 * f + 256], b.t[:, 256 * f:256 * f + 256], ACT.Sigmoid,
                                                                   bias=P("b_gate", 8 * n + 2 * j + f, 8 * n + 2 * j + f + 1)), tg, st["gs"])
                b.free = s1
                o = mg[:, 2 * j:2 * j + 2, :].rearrange("p b n -> p (b n)")
                y = Y[j]
                if n == 0:
                    s2 = dve(lambda e, o=o, y=y: e.tensor_tensor(o, gs, y.t[:, :], ALU.mult), s1, tk)
                    st["gs"] = s2
                    st["mg"][j] = s2
                else:
                    s2 = dve(lambda e, y=y: e.tensor_tensor(gp, gs, y.t[:, :], ALU.mult), s1, tk, st["mg"])
                    st["gs"] = s2
                    st["mg"][j] = pool(lambda e, o=o: e.tensor_tensor(o, o, gp, ALU.add), s2, st["mg"][j])
                y.free = s2
                extra()

        t_yp = []
        for g in range(4):
            o, cur = t_pl[g]
            b = bank()
            tk = mm(b.t[:, 0:256], P("pool_w", 128 * g, 128 * g + 128), o[:, 16:272], True, True, cur, b.free, sig=True)
            ev = split_to(mhi[:, g, :], mlo[:, g, :], b.t[:, 0:256], tk, scale=P("pool_scale", g, g + 1))
            b.free = ev
            t_yp.append(ev)
        branch(0, "pool_proj_2", mhi[:, 0:4, :], mlo[:, 0:4, :], t_yp, lambda: conv_some(16))
        conv_some(1000)

        ones = gs[:, 0:128]
        t_on = pool(lambda e: e.memset(ones, 1.0 / 512), st["gs"])
        b = bank()
        for k in range(4):
            tk = mm(b.t[:, 0:256], ones, ca[:, k, :], k == 0, k == 3, t_on, t_c, b.free, sig=(k == 3))
        mb = b.t[:, 0:256].unsqueeze(1).to_broadcast([128, 4, 256])
        c1 = dve(lambda e: e.tensor_tensor(ca, ca, mb, ALU.subtract), tk)
        b.free = c1
        sq = zc[:, :, 0:256]
        c2 = act(lambda e: e.activation(sq, ca, ACT.Square), c1)
        b2 = bank()
        for k in range(4):
            tk = mm(b2.t[:, 0:256], ones, sq[:, k, :], k == 0, k == 3, c2, b2.free, sig=(k == 3))
        vr = gp[:, 0:256]
        c3 = dve(lambda e: e.tensor_scalar(vr, b2.t[:, 0:256], LN_EPS, None, ALU.add), tk, t_q)
        b2.free = c3
        nh = gp[:, 256:512]
        c3b = pool(lambda e: e.memset(nh, -0.5), t_on, t_q)
        c4 = pool(lambda e: e.tensor_tensor(vr, vr, nh, ALU.pow), c3, c3b)
        rb = vr.unsqueeze(1).to_broadcast([128, 4, 256])
        c5 = dve(lambda e: e.tensor_tensor(ca, ca, rb, ALU.mult), c4)
        t_yc = []
        for k in range(4):
            c6 = act(lambda e, k=k: e.activation(ca[:, k, :], ca[:, k, :], ACT.Silu, bias=P("conv_lb", k, k + 1),
                                                 scale=P("conv_g", k, k + 1)), c5)
        t_yc = split_to(mhi[:, 4:8, :], mlo[:, 4:8, :], ca, c6)
        st["mg"] = [st["mg"][j] for j in range(4)] if True else None
        gp_free = c5
        st["gs"] = [st["gs"], tk]
        st["mg"] = [[m_, gp_free] for m_ in st["mg"]]
        branch(1, "conv_proj_2", mhi[:, 4:8, :], mlo[:, 4:8, :], t_yc, lambda: None)

        t_br1 = list(st["mg"])
        qkT = [zc[0:96].rearrange("p b n -> p (b n)")[:, 512 * i:512 * i + 512] for i in range(2)]
        S = [up_.rearrange("p b n -> p (b n)")[:, 384 * i:384 * i + 384] for i in range(2)]
        pTb = [wsum.rearrange("p b n -> p (b n)")[:, 384 * i:384 * i + 384] for i in range(2)]
        ob = wt2.rearrange("p b n -> p (b n)")[:, 0:1024].rearrange("p (t n) -> p t n", t=2)
        mx = arena.take(16)
        sm = arena.take(16)
        ri = arena.take(16)
        qscale = 96.0 ** -0.5
        o_b = [Y[0], Y[1]]
        o_free = [Y[0].free, Y[1].free]
        s_read, p_read, pT_read, q_read = [None] * 2, [None] * 2, [None] * 2, [None] * 2
        for h in range(8):
            i = h % 2
            b = bank()
            for n, src in enumerate((qf, kf)):
                for t in range(2):
                    tk = tr(b.t[0:96, 256 * n + 128 * t:256 * n + 128 * t + 128], src[:, t, h, :], 128, t_q, t_k, b.free,
                            sig=(n == 1 and t == 1))
            a1 = act(lambda e, i=i, b=b: e.activation(qkT[i], b.t[0:96, :], ACT.Copy), tk, q_read[i], t_br1)
            b.free = a1
            b = bank()
            mm(b.t[:, 0:128], qkT[i][:, 0:128], qkT[i][:, 256:384], True, True, a1, b.free)
            tk = mm(b.t[:, 128:384], qkT[i][:, 128:256], qkT[i][:, 256:512], True, True, sig=True)
            q_read[i] = tk
            d1 = dve(lambda e, i=i, b=b: e.scalar_tensor_tensor(out=S[i], in0=b.t[:, 0:384], scalar=qscale, in1=P("mask"),
                                                                op0=ALU.mult, op1=ALU.add), tk, p_read[i])
            b.free = d1
            for t, (c0, c1_) in enumerate(((0, 128), (128, 384))):
                d2 = dve(lambda e, i=i, h=h, t=t, c0=c0, c1_=c1_: e.tensor_reduce(mx[:, 2 * h + t:2 * h + t + 1], S[i][:, c0:c1_],
                                                                                  X, ALU.max, negate=True), d1)
            for t, (c0, c1_) in enumerate(((0, 128), (128, 384))):
                a2 = act(lambda e, i=i, h=h, t=t, c0=c0, c1_=c1_: e.activation(
                    S[i][:, c0:c1_], S[i][:, c0:c1_], ACT.Exp, bias=mx[:, 2 * h + t:2 * h + t + 1],
                    accum_out=sm[:, 2 * h + t:2 * h + t + 1]), d2)
            b = bank()
            for n in range(3):
                tk = tr(b.t[:, 128 * n:128 * n + 128], S[i][:, 128 * n:128 * n + 128], 128, a2, b.free, sig=(n == 2))
            p_read[i] = tk
            a3 = act(lambda e, i=i, b=b: e.activation(pTb[i], b.t[:, 0:384], ACT.Copy), tk, pT_read[i])
            b.free = a3
            mm(o_b[0].t[:, 64 * h:64 * h + 64], pTb[i][:, 0:128], va[:, 0, h, :], True, True, a3, t_k, o_free)
            mm(o_b[1].t[:, 64 * h:64 * h + 64], pTb[i][:, 128:256], va[:, 0, h, :], True, False)
            pT_read[i] = mm(o_b[1].t[:, 64 * h:64 * h + 64], pTb[i][:, 256:384], va[:, 1, h, :], False, True, sig=True)
        d3 = dve(lambda e: e.reciprocal(ri, sm), a2)
        for t in range(2):
            rv = ri.rearrange("p (h t) -> p t h", t=2)[:, t, :].unsqueeze(2).to_broadcast([128, 8, 64])
            d4 = dve(lambda e, t=t, rv=rv: e.tensor_tensor(ob[:, t, :].rearrange("p (h n) -> p h n", n=64),
                                                           o_b[t].t[:, :].rearrange("p (h n) -> p h n", n=64), rv, ALU.mult),
                     d3, pT_read)
            o_b[t].free = d4
        t_yo = []
        for q in range(2):
            b = bank()
            for k in range(2):
                for t in range(2):
                    tk = tr(b.t[:, 256 * k + 128 * t:256 * k + 128 * t + 128], ob[:, t, 128 * (2 * q + k):128 * (2 * q + k) + 128], 128,
                            d4, b.free, sig=(k == 1 and t == 1))
            ev = split_to(mhi[:, 2 * q:2 * q + 2, :], mlo[:, 2 * q:2 * q + 2, :], blocks(b.t[:, :], 256), tk)
            b.free = ev
            t_yo.append(ev)
        branch(2, "mla_proj_2", mhi[:, 0:4, :], mlo[:, 0:4, :], t_yo, lambda: None)
        tm = split_to(mhi[:, :, :], mlo[:, :, :], mg, st["mg"])
        ty = big_rows("w_out_2", 4, mhi, mlo, tm)
        rt = residual(ty, t_ax, False)
        done, xt_ready, t_ax = layer_norm(rt, gbv, t_gb, ALPHA2)
        t_gb = next_gb(8, done)

        arena = Arena()
        pTr = blocks(arena.take(2 * T), T)
        t_p = pool.dma(pTr, blocks(A["pT"][:, :], T), s_p, done)
        wbc = arena.take(NEXP * T).rearrange("p (e n) -> p e n", e=NEXP)
        sel16 = arena.take(NEXP * 128)[0:16].rearrange("p (e n) -> p e n", e=NEXP)
        z16 = pool(lambda e: e.memset(sel16, 0.0), done)
        t_s16 = pool(lambda e: e.affine_select(out=sel16, in_=sel16, compare_op=ALU.not_equal, fill=1.0, base=0,
                                               pattern=[[-1, NEXP], [0, 128]], channel_multiplier=1), z16)
        w = Tile("w_router_2", 0)
        b = bank()
        tk = rowsof(w, xhi, xlo, 0, [(t, b.t[:, 16 * t:16 * t + 16], 0, 16) for t in range(2)], True, True, xt_ready, b.free)
        v = arena.take(32 * 8).rearrange("p (s t n) -> p s t n", s=8, t=2)
        aff, sel, s3, s4, oh1, oh2, desc, wgt = [v[:, i, :, :] for i in range(8)]
        a1 = act(lambda e, b=b: e.activation(aff, blocks(b.t[:, 0:32], 16), ACT.Sigmoid), tk, done)
        b.free = a1
        for n in range(16):
            t_d = pool(lambda e, n=n: e.memset(desc[:, :, n:n + 1], 16.0 - n), done)
        rb_ = brow[:, 8:24].unsqueeze(1).to_broadcast([128, 2, 16])
        d = dve(lambda e: e.tensor_tensor(sel, aff, rb_, ALU.add), a1, t_brow)
        sg4 = sel.rearrange("p t (g n) -> p (t g) n", n=4)
        pr = arena.take(8 * 6).rearrange("p (g n) -> p g n", n=6)
        d1 = dve(lambda e: e.tensor_tensor(pr[:, :, 0:3], sg4[:, :, 0:3], sg4[:, :, 1:4], ALU.add), d)
        d1 = dve(lambda e: e.tensor_tensor(pr[:, :, 3:5], sg4[:, :, 0:2], sg4[:, :, 2:4], ALU.add))
        d1 = dve(lambda e: e.tensor_tensor(pr[:, :, 5:6], sg4[:, :, 0:1], sg4[:, :, 3:4], ALU.add))
        gsc = arena.take(8).rearrange("p (t g) -> p t g", t=2)
        d1 = dve(lambda e: e.tensor_reduce(gsc.rearrange("p t g -> p (t g)"), pr, X, ALU.max), d1)

        small = arena.take(8)

        def first_max(oh, src, n, d):
            m_ = small[:, 0:2]
            dd = desc[:, :, 0:n]
            d = dve(lambda e: e.tensor_reduce(m_, src, X, ALU.max), d)
            d = dve(lambda e: e.tensor_tensor(oh, src, m_.unsqueeze(2).to_broadcast([128, 2, n]), ALU.is_equal), d)
            d = dve(lambda e: e.tensor_tensor(oh, oh, dd, ALU.mult), d, t_d)
            d = dve(lambda e: e.tensor_reduce(m_, oh, X, ALU.max), d)
            return dve(lambda e: e.tensor_tensor(oh, dd, m_.unsqueeze(2).to_broadcast([128, 2, n]), ALU.is_equal), d)

        gk = arena.take(8).rearrange("p (t g) -> p t g", t=2)
        d1 = first_max(gk, gsc, 4, d1)
        BIG = 1e30
        gkb = arena.take(8).rearrange("p (t g) -> p t g", t=2)
        d2 = dve(lambda e: e.tensor_scalar(gkb, gk, BIG, -BIG, ALU.mult, ALU.add), d1)
        s34 = s3.rearrange("p t (g n) -> p (t g) n", n=4)
        gk8 = gk.rearrange("p t g -> p (t g)").unsqueeze(2).to_broadcast([128, 8, 4])
        gkb8 = gkb.rearrange("p t g -> p (t g)").unsqueeze(2).to_broadcast([128, 8, 4])
        d2 = dve(lambda e: e.tensor_tensor(s34, sg4, gk8, ALU.mult), d2)
        d2 = dve(lambda e: e.tensor_tensor(s34, s34, gkb8, ALU.add), d2)
        d2 = first_max(oh1, s3, 16, d2)
        d2 = dve(lambda e: e.scalar_tensor_tensor(out=s4, in0=oh1, scalar=-2 * BIG, in1=s3, op0=ALU.mult, op1=ALU.add), d2)
        d2 = first_max(oh2, s4, 16, d2)
        d2 = dve(lambda e: e.tensor_tensor(oh1, oh1, oh2, ALU.add), d2)
        d2 = dve(lambda e: e.tensor_tensor(wgt, oh1, aff, ALU.mult), d2)
        m_ = small[:, 2:4]
        d2 = dve(lambda e: e.tensor_reduce(m_, wgt, X, ALU.add), d2)
        d2 = dve(lambda e: e.reciprocal(small[:, 4:6], m_), d2)
        d2 = dve(lambda e: e.tensor_tensor(wgt, wgt, small[:, 4:6].unsqueeze(2).to_broadcast([128, 2, 16]), ALU.mult), d2)
        t_wgt = d2

        ty = big_rows("ple_gate_2", 4, xhi, xlo)
        pg = r
        t_sg = []
        for t in range(2):
            for i in range(2):
                y = Y[2 * t + i]
                y.free = act(lambda e, t=t, i=i, y=y: e.activation(pg[:, t, 512 * i:512 * i + 512], y.t[:, :], ACT.Sigmoid), ty[t], done)
                t_sg.append(y.free)
        t_pp = split_to(mhi[:, 0:2, :], mlo[:, 0:2, :], pTr, t_p)
        ty = big_rows("ple_proj_2", 1, mhi, mlo, t_pp)
        for t in range(2):
            for i in range(2):
                y = Y[2 * t + i]
                o = pg[:, t, 512 * i:512 * i + 512]
                e1 = dve(lambda e, o=o, y=y: e.tensor_tensor(o, o, y.t[:, :], ALU.mult), ty[t], t_sg)
                y.free = e1
            t_ax[t] = pool(lambda e, t=t: e.tensor_tensor(x[:, t, :], x[:, t, :], pg[:, t, :], ALU.add), e1, t_ax[t])

        b = bank()
        for t in range(2):
            tk = tr(b.t[0:16, 128 * t:128 * t + 128], wgt[:, t, :], 128, t_wgt, b.free, sig=(t == 1))
        wT = arena.take(T)[0:16]
        d3 = dve(lambda e, b=b: e.tensor_copy(wT, b.t[0:16, 0:256]), tk)
        b.free = d3
        t_wb = []
        for e2 in range(NEXP // 2):
            b = bank()
            for q in range(2):
                tk = mm(b.t[:, 256 * q:256 * q + 256], sel16[:, 2 * e2 + q, :], wT, True, True, d3, t_s16, b.free, sig=(q == 1))
            ev = act(lambda e, e2=e2, b=b: e.activation(wbc[:, 2 * e2:2 * e2 + 2, :].rearrange("p e n -> p (e n)"), b.t[:, :], ACT.Copy), tk)
            b.free = ev
            t_wb.append(ev)

        def weigh(c, hs, tick):
            wv = wbc[:, c // 2, :].unsqueeze(1).to_broadcast([128, 2, 256])
            hv = blocks(hs, 256)
            return dve(lambda e: e.tensor_tensor(hv, hv, wv, ALU.mult), tick, t_wb[c // 4])

        ty = ffn("exp_w_up_2", "exp_w_up_2", "exp_w_down_2", 2 * NEXP, xt_ready, weight=weigh)
        rt = residual(ty, t_ax, False)
        done, _, _ = layer_norm(rt, gbv, t_gb, None, turn=False)
        ov = out[0].rearrange("(t p) d -> p t d", p=128)
        for t in range(2):
            t_out = sp.dma(ov[:, t, :], x[:, t, :], s_out, done[t])
        sp.wait(t_out)
        assert state["use"] == len(tiles)

        with nc.Block() as block:
            @block.sync
            def _(e):
                sp.emit(e)

            @block.scalar
            def _(e):
                act.emit(e)

            @block.vector
            def _(e):
                dve.emit(e)

            @block.gpsimd
            def _(e):
                pool.emit(e)

            @block.tensor
            def _(e):
                pe.emit(e)


def feature_major(a):
    a = np.asarray(a)
    n = a.shape[-1] // 128
    a = a.reshape(-1, n, 128).transpose(2, 1, 0)
    return a.reshape(128, -1)


def token_major_T(a):
    tok, f = a.shape
    return np.ascontiguousarray(a.T.reshape(f // 128, 128, tok).transpose(1, 0, 2).reshape(128, -1))


def lay_out(inputs):
    a = {k: np.asarray(v) for k, v in inputs.items()}
    parts = []
    for name, idx, k0, k1, n0, n1 in weight_tiles():
        w = a[name][idx] if idx else a[name]
        w = w[128 * k0:128 * k1, n0:n1].reshape(k1 - k0, 128, n1 - n0).transpose(1, 0, 2)
        parts.append(w.reshape(-1))
    ws = np.concatenate(parts)

    par = np.zeros((128, NPAR), np.float32)

    def put(name, v):
        lo, hi = POFF[name]
        par[:v.shape[0], lo:hi] = v.reshape(v.shape[0], -1)

    put("conv_w", feature_major(a["conv_w"][0]))
    put("qkconv", a["qk_conv_w"][0].reshape(4, 16, 96).transpose(2, 1, 0))
    put("conv_dw", feature_major(a["conv_dw_2"][0]))
    put("conv_b", feature_major(a["conv_b_2"][0]))
    put("conv_g", feature_major(a["conv_ln_g_2"][0]))
    put("conv_lb", feature_major(a["conv_ln_b_2"][0]))
    put("b_gate", np.ascontiguousarray(a["b_gate_2"][0].reshape(24, 128).T))
    put("pool_scale", feature_major(a["pool_scale_2"][0]))
    put("q_g", feature_major(a["q_norm_g_2"][0]))
    put("kv_g", feature_major(a["kv_norm_g_2"][0]))
    put("pool_w", np.ascontiguousarray(a["pool_w_2"][0].transpose(1, 0, 2)))
    put("ident", np.eye(128, dtype=np.float32))
    mask = np.zeros((128, 384), np.float32)
    mask[0:64, 64:128] = -1e30
    mask[0:64, 128 + 192:384] = -1e30
    put("mask", mask)
    cnt = np.zeros((128, 4, 16), np.float32)
    for g in range(4):
        cnt[:, g, :] = 1.0 / np.minimum(np.arange(16) + 1, 2 << g)
    put("cnt", cnt)
    invf = np.power(np.float32(10000.0), -np.arange(0, 32, 2, dtype=np.float32) / np.float32(32))
    put("invf", np.tile(invf.astype(np.float32), (128, 1)))

    g = [a["ln_g"][l, j] for l in range(2) for j in range(3)] + [a["ln_in_g_2"], a["ln1_g_2"][0], a["ln2_g_2"][0]]
    b = [a["ln_b"][l, j] for l in range(2) for j in range(3)] + [a["ln_in_b_2"], a["ln1_b_2"][0], a["ln2_b_2"][0]]
    ln = np.stack([np.concatenate([p, q]) for p, q in zip(g, b)])
    rows = np.concatenate([a["b_gates"][0], a["router_bias_2"], a["head_norm_g"][0].reshape(-1)])[None, :]
    return {"ws": ws, "par": par, "ln": ln, "rows": np.ascontiguousarray(rows), "x": a["x"], "xT": token_major_T(a["x"][0]),
            "memT": token_major_T(a["mem"][0]), "pT": token_major_T(a["p_2"][0, 0]), "pos": a["positions_2"].reshape(2, 128).T}


def kernel(**inputs):
    import concourse.bacc as _bacc
    from concourse.bass_utils import run_bass_kernel_spmd as _run

    nc = _bacc.Bacc("TRN2", target_bir_lowering=False, num_devices=1)
    arrays, aps = {}, {}
    for name, a in lay_out(inputs).items():
        a = np.ascontiguousarray(a)
        arrays[f"in_{name}"] = a
        aps[name] = nc.dram_tensor(f"in_{name}", a.shape, mybir.dt.from_np(a.dtype), kind="ExternalInput").ap()
    out = nc.dram_tensor("out_0", (1, T, D), mybir.dt.float32, kind="ExternalOutput").ap()
    program(nc, aps, out)
    res = _run(nc, [arrays], core_ids=[0])
    return res.results[0]["out_0"]
```

```python
import math
from contextlib import ExitStack

import numpy as np

import concourse.bass as bass
from concourse import mybir
from concourse.alu_op_type import AluOpType as ALU

D = 1024
T = 256
FF = 2816
NEXP = 16
ALPHA1 = 4.0 ** 0.25
ALPHA2 = 2.0 ** 0.25
LN_EPS = 1e-5
RMS_EPS = 1e-6
TILE = 2048
PI = math.pi
MIX_ORDER = (6, 0, 2, 4)


def weight_tiles():
    tiles = []

    def ffn(gate, up, down, gi, ui, di, chunks, up0, late=None):
        for c in range(chunks):
            tiles.append((gate, gi(c), 0, 8, *up0(0, c)))
            tiles.append((up, ui(c), 0, 8, *up0(1, c)))
            if c:
                tiles.append((down, di(c - 1), *late(c - 1), 0, D))
        tiles.append((down, di(chunks - 1), *late(chunks - 1), 0, D))

    def first_ffn(l, s):
        i = (l, s)
        ffn("ffn_w_gate", "ffn_w_up", "ffn_w_down", lambda c: i, lambda c: i, lambda c: i, FF // 256,
            lambda part, c: (256 * c, 256 * c + 256), lambda c: (2 * c, 2 * c + 2))

    def rows(name, idx, blocks, n0, n1, step=2):
        for k in range(0, blocks, step):
            tiles.append((name, idx, k, k + step, n0, n1))

    def mixed(l):
        for k in MIX_ORDER:
            tiles.append(("w_out", (l,), k, k + 2, 0, D))

    def memory(l):
        tiles.append(("w_kv_mem", (l,), 0, 8, 0, 256))
        tiles.append(("w_kv_mem", (l,), 0, 8, 256, 512))

    first_ffn(0, 0)
    memory(0)
    tiles.append(("w_in_conv", (0,), 0, 8, 2304, 2560))
    for j in range(3):
        for part in (1, 2, 0):
            n = 768 * part + 256 * j
            tiles.append(("w_in_conv", (0,), 0, 8, n, n + 256))
    mixed(0)
    first_ffn(0, 1)
    memory(1)
    first_ffn(1, 0)
    tiles.append(("w_in_mlstm", (0,), 0, 8, 3072, 3080))
    tiles.append(("w_in_mlstm", (0,), 0, 8, 3080, 3336))
    rows("w_in_mlstm", (0,), 8, 1536, 2304)
    for h in range(4):
        for part in range(2):
            n = 768 * part + 192 * h
            tiles.append(("w_in_mlstm", (0,), 0, 8, n, n + 192))
    rows("w_in_mlstm", (0,), 8, 2304, 3072)
    mixed(1)
    first_ffn(1, 1)

    rows("w_in_2", (0,), 8, 1536, 2208)
    for j in range(2):
        tiles.append(("w_in_2", (0,), 0, 8, 256 * j, 256 * j + 256))
    for j in range(2):
        for part in range(2):
            n = 512 + 512 * part + 256 * j
            tiles.append(("w_in_2", (0,), 0, 8, n, n + 256))
    tiles.append(("w_uq_2", (0,), 0, 3, 0, 512))
    tiles.append(("w_uq_2", (0,), 0, 3, 512, 768))
    tiles.append(("w_ukv_2", (0,), 0, 2, 0, D))

    def gates(b):
        for j in range(4):
            n = 2208 + 1024 * b + 256 * j
            tiles.append(("w_in_2", (0,), 0, 8, n, n + 256))

    def proj(name):
        for j in range(2):
            tiles.append((name, (0,), 0, 4, 512 * j, 512 * j + 512))

    gates(0)
    proj("pool_proj_2")
    gates(1)
    gates(2)
    proj("mla_proj_2")
    proj("conv_proj_2")
    rows("w_out_2", (0,), 8, 0, D)
    tiles.append(("w_router_2", (), 0, 8, 0, NEXP))
    rows("ple_gate_2", (0,), 8, 0, D)
    tiles.append(("ple_proj_2", (0,), 0, 2, 0, D))
    for e in range(NEXP):
        rows("exp_w_up_2", (0, e), 8, 0, D)
        rows("exp_w_down_2", (0, e), 4, 0, D)
    return tiles


def tile_width(t):
    return (t[3] - t[2]) * (t[5] - t[4])


PARAMS = [("conv_w", 18), ("qkconv", 64), ("conv_dw", 124), ("conv_b", 4), ("conv_g", 4), ("conv_lb", 4),
          ("b_gate", 24), ("pool_scale", 4), ("q_g", 3), ("kv_g", 2), ("pool_w", 512),
          ("ident", 128), ("mask", 384), ("cnt", 64), ("invf", 16)]
POFF = {}
_o = 0
for _n, _w in PARAMS:
    POFF[_n] = (_o, _o + _w)
    _o += _w
NPAR = _o
ROWS = 8 + 16 + 768


class Queue:

    def __init__(self, sem, name):
        self.sem, self.name, self.count, self.items = sem, name, 0, []

    def __call__(self, fn, *after, sig=True):
        self.count += 1 if sig else 0
        self.items.append((flat(after), fn, (self.sem, 1) if sig else None))
        return (self.sem, self.count)

    def dma(self, out, in_, sem, *after):
        sem[1] += 16
        self.items.append((flat(after), lambda e: e.dma_start(out, in_), (sem[0], 16)))
        return (sem[0], sem[1])

    def wait(self, *after):
        self.items.append((flat(after), None, None))

    def branch(self, other, flag, after):
        self.items.append(([after], None, (other, flag)))

    def emit(self, eng):
        seen = {}
        for after, fn, inc in self.items:
            for sem, value in after:
                if seen.get(id(sem), 0) < value:
                    eng.wait_ge(sem, value)
                    seen[id(sem)] = value
            if fn is None and inc is not None:
                other, flag = inc
                reg = eng.alloc_register("flag_" + other.name)
                eng.reg_load(reg, flag)
                with eng.If_ne(reg, 0):
                    other.emit(eng)
            if fn is not None:
                ins = fn(eng)
                if inc is not None:
                    ins.then_inc(*inc)


def flat(after):
    out = []
    for a in after:
        if a is None:
            continue
        if isinstance(a, list):
            out += flat(a)
        else:
            out.append(a)
    return out


class Bank:

    def __init__(self, t):
        self.t, self.free = t, []


def program(nc, A, out):
    f32, f32r, i32 = mybir.dt.float32, mybir.dt.float32r, mybir.dt.int32
    ACT = mybir.ActivationFunctionType
    X = mybir.AxisListType.X
    NR, NS, LOOK = 4, 3, 2

    ctx = ExitStack()
    with ctx:
        def sb(name, shape, dt=f32):
            return ctx.enter_context(nc.sbuf_tensor(name, shape, dt))

        def sem(name):
            return ctx.enter_context(nc.semaphore(name))

        raw = [sb(f"raw{i}", [128, TILE]) for i in range(NR)]
        whi = [sb(f"whi{i}", [128, TILE], f32r) for i in range(NS)]
        wlo = [sb(f"wlo{i}", [128, TILE], f32r) for i in range(NS)]
        x = sb("x", [128, 2, D])
        r = sb("r", [128, 2, D])
        xhi = sb("xhi", [128, 8, T], f32r)
        xlo = sb("xlo", [128, 8, T], f32r)
        mhi = sb("mhi", [128, 8, T], f32r)
        mlo = sb("mlo", [128, 8, T], f32r)
        hf = sb("hf", [128, 2, 2, T])
        hhi = sb("hhi", [128, 2, 2, T], f32r)
        hlo = sb("hlo", [128, 2, 2, T], f32r)
        gb = sb("gb", [128, 2, D])
        par = sb("par", [128, NPAR])
        brow = sb("brow", [128, 24])
        kT = sb("kT", [128, 2, 2, T])
        vm = sb("vm", [128, 2, 2, T])
        stat = sb("stat", [128, 2, 12])
        mv = sb("mv", [128, 2, 2])
        ve = sb("ve", [128, 2])
        rstd = sb("rstd", [128, 2])
        mhalf = sb("mhalf", [128, 8])
        posi = sb("posi", [128, 2], i32)
        cs = sb("cs", [128, 2, 2, 16])
        gsel = sb("gsel", [128, 2, 2, 128], f32r)
        tsel = sb("tsel", [128, 2, T], f32r)
        AR = 10500
        ar = sb("ar", [128, AR])
        W = [Bank(ctx.enter_context(nc.psum_tensor(f"psw{i}", [128, 512], f32))) for i in range(4)]
        Y = [Bank(ctx.enter_context(nc.psum_tensor(f"psy{i}", [128, 512], f32))) for i in range(4)]

        pe, act, dve, pool, sp = [Queue(sem(n), n) for n in ("s_pe", "s_act", "s_dve", "s_pool", "s_sp")]
        s_raw = [[sem(f"s_raw{i}"), 0] for i in range(NR)]
        s_par, s_brow, s_pos, s_x, s_xT, s_mem, s_p = [[sem(n), 0] for n in
                                                        ("s_par", "s_brow", "s_pos", "s_x", "s_xT", "s_mem", "s_p")]
        s_gb, s_gbin, s_hn, s_out = [[sem(n), 0] for n in ("s_gb", "s_gbin", "s_hn", "s_out")]

        def P(name, a=0, b=None):
            lo, hi = POFF[name]
            return par[:, lo + a:(hi if b is None else lo + b)]

        ident = P("ident")

        class Arena:
            def __init__(self):
                self.at = 0

            def take(self, n):
                self.at += n
                assert self.at <= AR, self.at
                return ar[:, self.at - n:self.at]

        def blocks(ap, n):
            return ap.rearrange("p (b n) -> p b n", n=n)

        tiles = weight_tiles()
        offs = [0]
        for t in tiles:
            offs.append(offs[-1] + 128 * tile_width(t))
        main_tiles = len(tiles)
        expert0 = next(i for i, t in enumerate(tiles) if t[0] == "exp_w_up_2")
        offs = offs[:-1] + offs[expert0:-1]
        tiles = tiles + tiles[expert0:]
        raw_read = [None] * len(tiles)
        hi_done = [None] * len(tiles)
        lo_done = [None] * len(tiles)
        used = [None] * len(tiles)
        raw_in = [None] * len(tiles)
        state = {"load": 0, "split": 0, "use": 0, "w": 0, "end": main_tiles}

        def load_tile():
            i = state["load"]
            if i >= state["end"]:
                return
            w = tile_width(tiles[i])
            src = A["ws"][offs[i]:offs[i] + 128 * w].rearrange("(p c) -> p c", c=w)
            raw_in[i] = sp.dma(raw[i % NR][:, 0:w], src, s_raw[i % NR], raw_read[i - NR] if i >= NR else None)
            state["load"] += 1

        def split_tile():
            i = state["split"]
            if i >= state["end"]:
                return
            w = tile_width(tiles[i])
            src, hi, lo = raw[i % NR][:, 0:w], whi[i % NS][:, 0:w], wlo[i % NS][:, 0:w]
            free = used[i - NS] if i >= NS else None
            assert i < NS or free is not None
            hi_done[i] = act(lambda e: e.activation(hi, src, ACT.Copy), raw_in[i], free)
            lo_done[i] = dve(lambda e: e.tensor_tensor(lo, src, hi.bitcast(f32), ALU.subtract), hi_done[i], free)
            raw_read[i] = lo_done[i]
            state["split"] += 1
            load_tile()

        class Tile:

            def __init__(self, name, n0=None, look=LOOK):
                self.i = i = state["use"]
                t = tiles[i]
                assert t[0] == name and (n0 is None or t[4] == n0), (t, name, n0)
                while state["split"] <= min(i + look, state["end"] - 1):
                    split_tile()
                state["use"] += 1
                self.kb, self.k0, self.n = t[3] - t[2], t[2], t[5] - t[4]
                w = tile_width(t)
                self.hi = blocks(whi[i % NS][:, 0:w], self.n)
                self.lo = blocks(wlo[i % NS][:, 0:w], self.n)
                self.ready = [hi_done[i], lo_done[i]]

            def done(self, ticket):
                used[self.i] = ticket

        def bank():
            state["w"] += 1
            return W[(state["w"] - 1) % 4]

        def mm(o, l, rr, start, stop, *after, sig=False):
            return pe(lambda e: e.matmul(o, l, rr, start=start, stop=stop), *after, sig=sig)

        def tr(o, i, n, *after, sig=False):
            return pe(lambda e: e.transpose(o, i, ident[0:n, 0:n]), *after, sig=sig)

        def cols(o, w, c0, m, hi, lo, *after):
            for k in range(w.kb):
                wh, wl = w.hi[:, k, c0:c0 + m], w.lo[:, k, c0:c0 + m]
                mm(o, wh, hi[:, k, :], k == 0, False, w.ready, *after)
                mm(o, wh, lo[:, k, :], False, False)
                tick = mm(o, wl, hi[:, k, :], False, k == w.kb - 1, sig=(k == w.kb - 1))
            return tick

        def pair(w, hi, lo, *after, m=128):
            b = bank()
            for j in range(w.n // m):
                tick = cols(b.t[0:m, 256 * j:256 * j + 256], w, m * j, m, hi, lo, b.free, *after)
            b.free = None
            w.done(tick)
            return b, tick

        def rows_of(w, t, hi, lo, k0, mine, first, last, *after):
            for k in range(w.kb):
                lh, ll = hi[:, k0 + k, 128 * t:128 * t + 128], lo[:, k0 + k, 128 * t:128 * t + 128]
                st = first and k == 0
                en = last and k == w.kb - 1
                for o, c0, c1 in mine:
                    mm(o, lh, w.hi[:, k, c0:c1], st, False, w.ready, *after)
                for o, c0, c1 in mine:
                    mm(o, lh, w.lo[:, k, c0:c1], False, False)
                for n, (o, c0, c1) in enumerate(mine):
                    tick = mm(o, ll, w.hi[:, k, c0:c1], False, en, sig=(k == w.kb - 1 and n == len(mine) - 1))
            if last:
                yt[t] = tick
            return tick

        def rowsof(w, hi, lo, k0, outs, first, last, *after):
            for t in range(2):
                tick = rows_of(w, t, hi, lo, k0, [o[1:] for o in outs if o[0] == t], first, last, *after)
            w.done(tick)
            return tick

        yt = [None, None]

        def big_rows(name, ntile, hi, lo, *after, n=D, splits=((0, 512), (512, 1024)), n0=None, each=None, hook={}):
            free = [b.free for b in Y]
            for j in range(ntile):
                w = Tile(name, n0)
                outs = [(t, Y[2 * t + i].t[:, 0:c1 - c0], c0, c1) for t in range(2) for i, (c0, c1) in enumerate(splits)]
                rowsof(w, hi, lo, w.k0, outs, j == 0, j == ntile - 1, *(list(after) + free + (each[j] if each else [])))
                if j in hook:
                    hook[j]()
            return [yt[0], yt[1]]

        def split_to(hi, lo, src, *after, scale=1.0):
            a = act(lambda e: e.activation(hi, src, ACT.Copy, scale=scale), *after)
            if isinstance(scale, float):
                d = dve(lambda e: e.tensor_tensor(lo, src, hi.bitcast(f32), ALU.subtract), a)
            else:
                d = dve(lambda e: e.scalar_tensor_tensor(out=lo, in0=src, scalar=scale, in1=hi.bitcast(f32),
                                                         op0=ALU.mult, op1=ALU.subtract), a)
            return [a, d]

        first = Arena()
        memT = blocks(first.take(8 * T), T)
        xTr = blocks(first.take(8 * T), T)
        t_xT = sp.dma(xTr, blocks(A["xT"][:, :], T), s_xT)
        for _ in range(NR):
            load_tile()
        t_par = sp.dma(par[:, :], A["par"][:, :], s_par)
        t_pos = sp.dma(posi[:, :], A["pos"][:, :], s_pos)
        t_x = sp.dma(x[:, :, :], A["x"][0].rearrange("(t p) d -> p t d", p=128), s_x)
        t_brow = sp.dma(brow[:, :], A["rows"][:, 0:24].broadcast_to((128, 24)), s_brow)
        t_mem = sp.dma(memT, blocks(A["memT"][:, :], T), s_mem)
        t_gb = pool.dma(gb[:, :, :].rearrange("p a d -> p (a d)"), A["ln"][0:1, :].broadcast_to((128, 2 * D)), s_gb)
        t_mhalf = pool(lambda e: e.memset(mhalf[:, :], -0.5))
        xt_ready = [split_to(xhi[:, 4 * q:4 * q + 4, :], xlo[:, 4 * q:4 * q + 4, :], xTr[:, 4 * q:4 * q + 4, :], t_xT)
                    for q in range(2)]

        kv_ready = {}

        def memory_keys(l, t_m):
            b, tk = pair(Tile("w_kv_mem", 0), mhi, mlo, t_m)
            o = kT[:, l, :, :].rearrange("p b n -> p (b n)")
            b.free = act(lambda e: e.activation(o, b.t[:, :], ACT.Copy), tk)
            kv_ready[l] = [b.free]

        def memory_values(l, t_m):
            w = Tile("w_kv_mem", 256)
            b = bank()
            tk = rowsof(w, mhi, mlo, 0, [(t, b.t[:, 256 * t:256 * t + 256], 0, 256) for t in range(2)], True, True, b.free, t_m)
            o = vm[:, l, :, :].rearrange("p b n -> p (b n)")
            b.free = act(lambda e: e.activation(o, b.t[:, :], ACT.Copy), tk)
            kv_ready[l].append(b.free)

        cw = first.take(2 * 16 * 4).rearrange("p (s t n) -> p s t n", s=4, t=2)
        posf = first.take(2)
        ang, kk, rr, ab = [cw[:, i, :, :] for i in range(4)]
        tk = dve(lambda e: e.tensor_copy(posf, posi[:, :]), t_pos)
        for t in range(2):
            a1 = dve(lambda e, t=t: e.tensor_scalar(ang[:, t, :], P("invf"), posf[:, t:t + 1], None, ALU.mult), tk, t_par)
        MAGIC = 1.5 * 2.0 ** 23
        a2 = dve(lambda e: e.tensor_scalar(kk, ang, 1.0 / (2 * PI), MAGIC, ALU.mult, ALU.add), a1)
        a2 = dve(lambda e: e.tensor_scalar(kk, kk, MAGIC, None, ALU.subtract), a2)
        C1 = 6.28125
        C2 = float(np.float32(np.round((2 * PI - C1) * 2.0 ** 21) / 2.0 ** 21))
        C3 = float(2 * PI - C1 - C2)
        src = ang
        for c in (C1, C2, C3):
            a2 = dve(lambda e, c=c, src=src: e.scalar_tensor_tensor(out=rr, in0=kk, scalar=-c, in1=src,
                                                                    op0=ALU.mult, op1=ALU.add), a2)
            src = rr
        a2 = dve(lambda e: e.tensor_scalar(rr, rr, 3.1415925, -3.1415925, ALU.min, ALU.max), a2)
        a3 = dve(lambda e: e.scalar_tensor_tensor(out=ab, in0=rr, scalar=-1.0, in1=rr, op0=ALU.mult, op1=ALU.min), a2)
        a3 = dve(lambda e: e.tensor_scalar(ab, ab, PI / 2, None, ALU.add), a3)
        cosA = cs[:, 0, :, :]
        sinA = cs[:, 1, :, :]
        act(lambda e: e.activation(sinA, rr, ACT.Sin), a2)
        t_cs = act(lambda e: e.activation(cosA, ab, ACT.Sin), a3)

        def scale_x(alpha, *after):
            return [pool(lambda e, t=t: e.tensor_scalar(x[:, t, :], x[:, t, :], alpha, None, ALU.mult), *after)
                    for t in range(2)]

        def ffn(gate, up, down, chunks, *after, between={}):
            h_read = [None, None]
            pend = []
            y0 = [b.free for b in Y]

            def outs(t):
                return [(Y[2 * t + i].t[:, :], 512 * i, 512 * i + 512) for i in range(2)]

            def down_chunk():
                c, ready = pend.pop(0)
                w = Tile(down)
                s = c % 2
                for t in range(2):
                    tk = rows_of(w, t, hhi[:, s, :, :], hlo[:, s, :, :], 0, outs(t), c == 0, False, ready, y0)
                w.done(tk)
                h_read[s] = tk

            def last_chunks():
                ws = [Tile(down), Tile(down, look=1)]
                for t in range(2):
                    for w, (c, ready) in zip(ws, pend):
                        s = c % 2
                        tk = rows_of(w, t, hhi[:, s, :, :], hlo[:, s, :, :], 0, outs(t), False, c == chunks - 1, ready)
                        if t:
                            w.done(tk)

            for c in range(chunks):
                s = c % 2
                wg = Tile(gate)
                bg, tg = pair(wg, xhi, xlo, *after)
                wu = Tile(up)
                bu, tu = pair(wu, xhi, xlo, *after)
                hs = hf[:, s, :, :].rearrange("p b n -> p (b n)")
                hh, hl = [q[:, s, :, :].rearrange("p b n -> p (b n)") for q in (hhi, hlo)]
                t1 = act(lambda e, hs=hs, bg=bg: e.activation(hs, bg.t[:, :], ACT.Silu), tg)
                t2 = dve(lambda e, hs=hs, bu=bu: e.tensor_tensor(hs, hs, bu.t[:, :], ALU.mult), t1, tu)
                bg.free, bu.free = t1, t2
                if c in between:
                    between[c]()
                if 0 < c < chunks - 1:
                    down_chunk()
                pend.append((c, split_to(hh, hl, hs, t2, h_read[s])))
            last_chunks()
            return [yt[0], yt[1]]

        def layer_norm(ticks, t_ax, half, gbt, t_g, alpha=None, turn=True, dst=x, fill=()):
            g, bb = gbt[:, 0:D], gbt[:, D:2 * D]
            done, xt, read = [], [], []

            def half_of(z, t, h):
                return z[:, t, 512 * h:512 * h + 512]

            def stats(t):
                for h in range(2):
                    o, y = half_of(r, t, h), Y[2 * t + h]
                    q = t_ax[t]
                    if ticks is not None:
                        xa = half_of(x, t, h)
                        if half:
                            q = dve(lambda e, o=o, xa=xa, y=y: e.scalar_tensor_tensor(out=o, in0=y.t[:, :], scalar=0.5, in1=xa,
                                                                                      op0=ALU.mult, op1=ALU.add), ticks[t], q)
                        else:
                            q = dve(lambda e, o=o, xa=xa, y=y: e.tensor_tensor(o, y.t[:, :], xa, ALU.add), ticks[t], q)
                        y.free = q
                    s1 = dve(lambda e, o=o, h=h: e.bn_stats(stat[:, t, 6 * h:6 * h + 6], o), q)
                s2 = dve(lambda e: e.bn_aggr(mv[:, t, :], stat[:, t, :]), s1)
                s3 = dve(lambda e: e.tensor_scalar(ve[:, t:t + 1], mv[:, t, 1:2], LN_EPS, None, ALU.add), s2)
                return pool(lambda e: e.tensor_tensor(rstd[:, t:t + 1], ve[:, t:t + 1], mhalf[:, 0:1], ALU.pow), s3, t_mhalf)

            def norm(t, rs):
                out_ = []
                for h in range(2):
                    o, src, d = half_of(x, t, h), half_of(r, t, h), half_of(dst, t, h)
                    gh, bh = g[:, 512 * h:512 * h + 512], bb[:, 512 * h:512 * h + 512]
                    n1 = dve(lambda e, o=o, src=src, gh=gh: e.scalar_tensor_tensor(
                        out=o, in0=src, scalar=mv[:, t, 0:1], in1=gh, op0=ALU.subtract, op1=ALU.mult), rs, t_g)
                    out_.append(dve(lambda e, o=o, d=d, bh=bh: e.scalar_tensor_tensor(
                        out=d, in0=o, scalar=rstd[:, t:t + 1], in1=bh, op0=ALU.mult, op1=ALU.add), n1))
                done.append(out_[-1])
                return out_

            def turned(t, n):
                bs = []
                for q in range(2):
                    b = bank()
                    for k in range(4):
                        kb = 4 * q + k
                        tk = tr(b.t[:, 128 * k:128 * k + 128], x[:, t, 128 * kb:128 * kb + 128], 128, n[q], b.free,
                                sig=(k == 3))
                    bs.append((b, tk))
                read.append(tk)
                return bs

            def parts(t, bs):
                for q, (b, tk) in enumerate(bs):
                    o = [z[:, 4 * q:4 * q + 4, 128 * t:128 * t + 128] for z in (xhi, xlo)]
                    ev = split_to(o[0], o[1], blocks(b.t[:, :], 128), tk)
                    b.free = ev
                    xt.append(ev)

            n0 = norm(0, stats(0))
            if fill:
                fill[0]()
            if turn:
                b0 = turned(0, n0)
            rs1 = stats(1)
            if turn:
                parts(0, b0)
            n1 = norm(1, rs1)
            if fill:
                fill[1]()
            if turn:
                parts(1, turned(1, n1))
                if alpha is None:
                    return done, xt, read
                return done, xt, [pool(lambda e, t=t: e.tensor_scalar(x[:, t, :], x[:, t, :], alpha, None, ALU.mult), read[t])
                                  for t in range(2)]
            return done, None, None

        def next_gb(k, *after):
            return pool.dma(gb[:, :, :].rearrange("p a d -> p (a d)"), A["ln"][k:k + 1, :].broadcast_to((128, 2 * D)), s_gb, *after)

        gbv = gb[:, :, :].rearrange("p a d -> p (a d)")

        def mem_attention(l, qT, t_q, pbuf, arena, *after):
            pT = [arena.take(2 * T).rearrange("p (m n) -> p m n", m=2) for _ in range(2)]
            ob = r[:, :, 768:1024]
            mx = arena.take(8)
            sm = arena.take(8)
            ri = arena.take(8)
            ex, t_pT, pv, t_o = [], {}, [None, None], [None]
            o_b = Y[0]

            def score(h):
                b = bank()
                s, blk = 64 * (h % 2), h // 2
                for t in range(2):
                    tk = mm(b.t[:, 256 * t:256 * t + 256], qT[s:s + 64, blk, 128 * t:128 * t + 128], kT[s:s + 64, l, blk, :],
                            True, True, t_q, kv_ready[l], b.free, sig=(t == 1))
                m2 = mx[:, 2 * h:2 * h + 2]
                t1 = dve(lambda e: e.tensor_reduce(m2, blocks(b.t[:, :], 256), X, ALU.max, negate=True), tk, list(after))
                t2 = dve(lambda e: e.tensor_scalar(m2, m2, 0.125, None, ALU.mult), t1)
                for t in range(2):
                    t3 = act(lambda e, t=t: e.activation(pbuf[:, h, t, :], b.t[:, 256 * t:256 * t + 256], ACT.Exp,
                                                         bias=mx[:, 2 * h + t:2 * h + t + 1], scale=0.125,
                                                         accum_out=sm[:, 2 * h + t:2 * h + t + 1]), t2, list(after))
                b.free = t3
                ex.append(t3)

            def turn(h):
                b = bank()
                for m in range(2):
                    for t in range(2):
                        tk = tr(b.t[:, 256 * m + 128 * t:256 * m + 128 * t + 128], pbuf[:, h, t, 128 * m:128 * m + 128], 128,
                                ex[h], b.free, sig=(m == 1 and t == 1))
                p2 = pT[h % 2]
                b.free = t_pT[h] = act(lambda e: e.activation(p2.rearrange("p m n -> p (m n)"), b.t[:, :], ACT.Copy), tk, pv[h % 2],
                                       list(after))

            def value(h):
                p2 = pT[h % 2]
                for t in range(2):
                    for m in range(2):
                        c = 256 * t + 64 * h
                        pv[h % 2] = mm(o_b.t[:, c:c + 64], p2[:, m, 128 * t:128 * t + 128], vm[:, l, m, 64 * h:64 * h + 64],
                                       m == 0, m == 1, t_pT[h], o_b.free, sig=(t == 1 and m == 1))

            def scale():
                t_r = dve(lambda e: e.reciprocal(ri, sm), ex[-1])
                for t in range(2):
                    rv = ri.rearrange("p (h t) -> p t h", t=2)[:, t, :].unsqueeze(2).to_broadcast([128, 4, 64])
                    t_o[0] = dve(lambda e, t=t, rv=rv: e.tensor_tensor(ob[:, t, :].rearrange("p (h n) -> p h n", n=64),
                                                                       o_b.t[:, 256 * t:256 * t + 256].rearrange("p (h n) -> p h n", n=64),
                                                                       rv, ALU.mult), pv[1], t_r, list(after))
                o_b.free = t_o[0]

            def finish():
                b = bank()
                for k in range(2):
                    for t in range(2):
                        tk = tr(b.t[:, 256 * k + 128 * t:256 * k + 128 * t + 128], ob[:, t, 128 * k:128 * k + 128], 128, t_o[0], b.free,
                                sig=(k == 1 and t == 1))
                b.free = split_to(mhi[:, 6:8, :], mlo[:, 6:8, :], blocks(b.t[:, :], 256), tk)
                return b.free

            return score, turn, value, scale, finish

        def prob_buffer(z):
            return z.rearrange("p (h t n) -> p h t n", h=4, t=2)

        def xa_queries(name, n0, qT, *after):
            w = Tile(name, n0)
            b, tk = pair(w, xhi, xlo, *after)
            b.free = act(lambda e: e.activation(qT.rearrange("p b n -> p (b n)"), b.t[:, :], ACT.Copy), tk)
            return b.free

        def conv_mixer(t_xt, t_prev):
            arena = Arena()
            qT = arena.take(2 * T).rearrange("p (b n) -> p b n", b=2)
            t_q = xa_queries("w_in_conv", 2304, qT, t_xt)
            cb = arena.take(2 * T)
            z = [arena.take(2 * 258).rearrange("p (b n) -> p b n", b=2) for _ in range(2)]
            acc = [arena.take(2 * T).rearrange("p (b n) -> p b n", b=2) for _ in range(2)]
            cwt = P("conv_w").rearrange("p (b w) -> p b w", w=3)
            zz = [pool(lambda e, q=q: e.memset(z[q][:, :, 0:2], 0.0), t_q) for q in range(2)]
            done = []
            score, turn, value, scale, finish = mem_attention(0, qT, t_q, prob_buffer(arena.take(8 * T)), arena, t_prev)
            t_mem = []
            steps = [lambda: (score(0), score(1)), lambda: (score(2), score(3)), lambda: turn(0), lambda: (value(0), turn(1)),
                     lambda: (value(1), turn(2)), lambda: (value(2), turn(3)), lambda: (value(3), scale()),
                     lambda: t_mem.append(finish()), lambda: None]

            def part(j):
                q = j % 2
                bc, tc = pair(Tile("w_in_conv", 768 + 256 * j), xhi, xlo)
                t1 = act(lambda e: e.activation(cb, bc.t[:, :], ACT.Copy), tc, done[j - 1] if j else None)
                bc.free = t1
                steps.pop(0)()
                bx, tx = pair(Tile("w_in_conv", 1536 + 256 * j), xhi, xlo)
                t2 = dve(lambda e: e.tensor_tensor(z[q][:, :, 2:258], blocks(cb, 256), blocks(bx.t[:, :], 256), ALU.mult), t1, tx)
                bx.free = t2
                steps.pop(0)()
                t3 = [t2, t2]
                for f in range(2):
                    blk = 2 * j + f
                    t3[f] = dve(lambda e, f=f, blk=blk: e.tensor_scalar(acc[q][:, f, :], z[q][:, f, 2:258], cwt[:, blk, 2:3], None,
                                                                        ALU.mult), t2, zz[q])
                for s in range(2):
                    for f in range(2):
                        blk = 2 * j + f
                        t3[f] = dve(lambda e, f=f, blk=blk, s=s: e.scalar_tensor_tensor(
                            out=acc[q][:, f, :], in0=z[q][:, f, s:s + 256], scalar=cwt[:, blk, s:s + 1], in1=acc[q][:, f, :],
                            op0=ALU.mult, op1=ALU.add), t3[f])
                bb, tb = pair(Tile("w_in_conv", 256 * j), xhi, xlo)
                t4 = dve(lambda e: e.tensor_tensor(acc[q], acc[q], blocks(bb.t[:, :], 256), ALU.mult), t3, tb)
                bb.free = t4
                steps.pop(0)()
                done.append(split_to(mhi[:, 2 * j:2 * j + 2, :], mlo[:, 2 * j:2 * j + 2, :], acc[q], t4))

            for j in range(3):
                part(j)
            return t_mem + done

        def mlstm_mixer(t_xt, t_prev):
            arena = Arena()
            qT = arena.take(2 * T).rearrange("p (b n) -> p b n", b=2)
            hn = arena.take(768)
            t_hn = pool.dma(hn, A["rows"][:, 24:792].broadcast_to((128, 768)), s_hn, t_prev)
            sel = arena.take(512)[0:4].rearrange("p (h n) -> p h n", h=4)
            s0 = pool(lambda e: e.memset(sel, 0.0), t_prev)
            t_sel = pool(lambda e: e.affine_select(out=sel, in_=sel, compare_op=ALU.not_equal, fill=1.0, base=0,
                                                   pattern=[[-1, 4], [0, 128]], channel_multiplier=1), s0)
            gt = arena.take(16).rearrange("p (t n) -> p t n", t=2)
            w = Tile("w_in_mlstm", 3072)
            b = bank()
            tk = rowsof(w, xhi, xlo, 0, [(t, b.t[:, 8 * t:8 * t + 8], 0, 8) for t in range(2)], True, True, t_xt, b.free)
            gb8 = brow[:, 0:8].unsqueeze(1).to_broadcast([128, 2, 8])
            t1 = dve(lambda e, b=b: e.tensor_tensor(gt, blocks(b.t[:, 0:16], 8), gb8, ALU.add), tk, t_brow)
            b.free = t1
            t_q = xa_queries("w_in_mlstm", 3080, qT)
            gs = arena.take(5 * T).rearrange("p (s n) -> p s n", s=5)[0:4]
            li, z, e1, AA, em = [gs[:, i, :] for i in range(5)]
            lf, B, aa = e1, z, li
            t_c = {}

            def decays():
                b = bank()
                for t in range(2):
                    for part in range(2):
                        tk = tr(b.t[0:4, 256 * part + 128 * t:256 * part + 128 * t + 128], gt[:, t, 4 * part:4 * part + 4], 128,
                                t1, b.free, sig=(t == 1 and part == 1))
                t2 = dve(lambda e: e.tensor_copy(gs[:, 0:2, :], blocks(b.t[0:4, :], 256)), tk)
                b.free = t2
                t3 = dve(lambda e: e.scalar_tensor_tensor(out=e1, in0=z, scalar=-1.0, in1=z, op0=ALU.mult, op1=ALU.max), t2)
                t4 = act(lambda e: e.activation(e1, e1, ACT.Exp, scale=-1.0), t3)
                t4 = act(lambda e: e.activation(e1, e1, ACT.Ln, bias=1.0), t4)
                t5 = dve(lambda e: e.scalar_tensor_tensor(out=lf, in0=z, scalar=0.0, in1=e1, op0=ALU.min, op1=ALU.subtract), t4)
                one = em
                t6 = dve(lambda e: e.memset(one, 1.0))
                t6 = dve(lambda e: e.tensor_tensor_scan(B, one, lf, 0.0, ALU.mult, ALU.add), t5, t6)
                t7 = dve(lambda e: e.tensor_tensor(aa, li, B, ALU.subtract), t6)
                t_c[8] = dve(lambda e: e.tensor_tensor_scan(AA, aa, aa, 0.0, ALU.max, ALU.max), t7)
                t9 = dve(lambda e: e.tensor_tensor(em, AA, B, ALU.add), t_c[8])
                t_c[9] = act(lambda e: e.activation(em, em, ACT.Exp, scale=-1.0), t9)

            ac = arena.take(16).rearrange("p (t n) -> p t n", t=2)

            def decay_columns():
                b = bank()
                for t in range(2):
                    for i, s in enumerate((aa, em)):
                        tk = tr(b.t[:, 8 * t + 4 * i:8 * t + 4 * i + 4], s[:, 128 * t:128 * t + 128], 4, t_c[8], t_c[9], b.free,
                                sig=(t == 1 and i == 1))
                b.free = t_c[10] = dve(lambda e: e.tensor_copy(ac, blocks(b.t[:, 0:16], 8)), tk)

            wt = arena.take(4 * 384).rearrange("p (h n) -> p h n", h=4)
            t_wt = []

            def weights(h):
                b = bank()
                tk = mm(b.t[:, 0:256], sel[:, h, :], AA, True, True, t_c[8], t_sel, b.free, sig=True)
                a1 = act(lambda e: e.activation(wt[:, h, 0:256], b.t[:, 0:256], ACT.Exp, bias=ac[:, 0, h:h + 1],
                                                scale=-1.0), tk, t_c[10])
                a2 = act(lambda e: e.activation(wt[:, h, 256:384], b.t[:, 128:256], ACT.Exp, bias=ac[:, 1, h:h + 1],
                                                scale=-1.0), tk, t_c[10])
                b.free = a2
                for c in (0, 256):
                    a3 = pool(lambda e, c=c: e.affine_select(out=wt[:, h, c:c + 128], in_=wt[:, h, c:c + 128],
                                                             compare_op=ALU.is_ge, fill=0.0, base=0, pattern=[[1, 128]],
                                                             channel_multiplier=-1), a1, a2)
                t_wt.append(a3)

            va = arena.take(2 * 4 * 194).rearrange("p (t h n) -> p t h n", t=2, h=4)
            t_one = pool(lambda e: e.memset(va[:, :, :, 192:194], 1.0), t1)
            cwt = P("qkconv").rearrange("p (b w) -> p b w", w=4)
            zp = [arena.take(2 * 259).rearrange("p (b n) -> p b n", b=2)[0:96] for _ in range(2)]
            zz = [pool(lambda e, q=q: e.memset(zp[q][:, :, 0:3], 0.0), t1) for q in range(2)]
            qk = [[arena.take(2 * T).rearrange("p (b n) -> p b n", b=2)[0:96] for _ in range(2)], [hf[0:96, s, :, :] for s in range(2)]]
            sc = [arena.take(384) for _ in range(2)]
            score, turn, value, scale, finish = mem_attention(1, qT, t_q, prob_buffer(gbv), arena, t_prev)
            ty = big_rows("w_in_mlstm", 4, xhi, xlo, n=768, splits=((0, 384), (384, 768)), n0=1536,
                          hook={0: decays, 1: lambda: (score(0), score(1)), 2: lambda: (decay_columns(), score(2)), 3: lambda: score(3)})
            t_v = []
            for t in range(2):
                for i in range(2):
                    y = Y[2 * t + i]
                    y.free = act(lambda e, t=t, i=i, y=y: e.activation(va[:, t, 2 * i:2 * i + 2, 0:192],
                                                                       blocks(y.t[:, 0:384], 192), ACT.Copy), ty[t])
                    t_v.append(y.free)
            hb = r[:, :, 0:768].rearrange("p t (h n) -> p t h n", h=4)
            den = arena.take(16).rearrange("p (s h t) -> p s h t", s=2, h=4)
            hst = arena.take(2 * 4 * 6).rearrange("p (t h n) -> p t h n", t=2, h=4)
            hmv = arena.take(2 * 4 * 2).rearrange("p (t h n) -> p t h n", t=2, h=4)
            hve = arena.take(16).rearrange("p (s h t) -> p s h t", s=2, h=4)
            t_h, t_a = {}, {}
            ready = {}
            conv_read = [None, None]
            qk_read = [None, None]
            sc_read = [None, None]

            def head(h, part):
                b, tk = pair(Tile("w_in_mlstm", 768 * part + 192 * h), xhi, xlo, m=96)
                z_ = zp[part]
                q_ = qk[h % 2][part]
                c1 = act(lambda e: e.activation(z_[:, :, 3:259], blocks(b.t[0:96, :], 256), ACT.Copy), tk, conv_read[part])
                b.free = c1
                c2 = [c1, c1]
                for f in range(2):
                    blk = 8 * part + 2 * h + f
                    c2[f] = pool(lambda e, f=f, blk=blk: e.tensor_scalar(q_[:, f, :], z_[:, f, 3:259], cwt[0:96, blk, 3:4], None,
                                                                         ALU.mult), c1, zz[part], qk_read[h % 2])
                for s in range(3):
                    for f in range(2):
                        blk = 8 * part + 2 * h + f
                        c2[f] = dve(lambda e, f=f, blk=blk, s=s: e.scalar_tensor_tensor(
                            out=q_[:, f, :], in0=z_[:, f, s:s + 256], scalar=cwt[0:96, blk, s:s + 1], in1=q_[:, f, :], op0=ALU.mult,
                            op1=ALU.add), c2[f], c1)
                conv_read[part] = c2
                ready[h, part] = act(lambda e: e.activation(q_, q_, ACT.Silu), c2)

            def attend(h):
                q_, k_ = qk[h % 2]
                b = bank()
                for f in range(2):
                    mm(b.t[:, 0:256], k_[:, f, 0:128], q_[:, f, :], f == 0, f == 1, ready[h, 0], ready[h, 1], b.free)
                for f in range(2):
                    tk = mm(b.t[:, 256:384], k_[:, f, 128:256], q_[:, f, 128:256], f == 0, f == 1, sig=(f == 1))
                qk_read[h % 2] = tk
                b.free = t_a[h] = dve(lambda e: e.scalar_tensor_tensor(out=sc[h % 2], in0=b.t[:, 0:384], scalar=192.0 ** -0.5,
                                                                       in1=wt[:, h, :], op0=ALU.mult, op1=ALU.mult),
                                      tk, t_wt[h], sc_read[h % 2])

            def states(h):
                nb = bank()
                s_ = sc[h % 2]
                mm(nb.t[:, 0:193], s_[:, 0:128], va[:, 0, h, 0:193], True, True, t_a[h], t_v, t_one, nb.free)
                mm(nb.t[:, 256:449], s_[:, 128:256], va[:, 0, h, 0:193], True, False)
                pv = mm(nb.t[:, 256:449], s_[:, 256:384], va[:, 1, h, 0:193], False, True, sig=True)
                sc_read[h % 2] = pv
                nd = blocks(nb.t[:, :], 256)[:, :, 192]
                d1 = dve(lambda e: e.scalar_tensor_tensor(out=den[:, 0, h, :], in0=nd, scalar=-1.0, in1=ac[:, :, 4 + h],
                                                          op0=ALU.mult, op1=ALU.max), pv)
                d1 = dve(lambda e: e.tensor_tensor(den[:, 0, h, :], nd, den[:, 0, h, :], ALU.max), d1)
                d1 = dve(lambda e: e.reciprocal(den[:, 1, h, :], den[:, 0, h, :]), d1)
                d2 = []
                for t in range(2):
                    d2.append(act(lambda e, t=t: e.activation(hb[:, t, h, :], nb.t[:, 256 * t:256 * t + 192], ACT.Copy,
                                                              scale=den[:, 1, h, t:t + 1]), d1, t_prev))
                nb.free = d2
                for t in range(2):
                    d3 = dve(lambda e, t=t: e.bn_stats(hst[:, t, h, :], hb[:, t, h, :]), d2[t])
                for t in range(2):
                    d3 = dve(lambda e, t=t: e.bn_aggr(hmv[:, t, h, :], hst[:, t, h, :]), d3)
                d3 = dve(lambda e: e.tensor_scalar(hve[:, 0, h, :], hmv[:, :, h, 1], LN_EPS, None, ALU.add), d3)
                d4 = pool(lambda e: e.tensor_tensor(hve[:, 1, h, :], hve[:, 0, h, :], mhalf[:, 0:2], ALU.pow), d3, t_mhalf)
                for t in range(2):
                    t_h[h] = pool(lambda e, t=t: e.tensor_scalar(hb[:, t, h, :], hb[:, t, h, :], hmv[:, t, h, 0:1],
                                                                 hve[:, 1, h, t:t + 1], ALU.subtract, ALU.mult), d4)

            t_mem = []
            steps = [lambda: ([weights(h) for h in range(4)], turn(0)), lambda: (value(0), turn(1)),
                     lambda: (attend(0), value(1), turn(2)), lambda: (states(0), value(2), turn(3)),
                     lambda: (attend(1), value(3), scale()), lambda: (states(1), t_mem.append(finish())),
                     lambda: attend(2), lambda: states(2)]
            for h in range(4):
                for part in range(2):
                    head(h, part)
                    steps.pop(0)()

            ty = big_rows("w_in_mlstm", 4, xhi, xlo, n=768, splits=((0, 384), (384, 768)), n0=2304,
                          hook={0: lambda: attend(3), 1: lambda: states(3)})
            og = wt.rearrange("p h n -> p (h n)")[:, 0:1536].rearrange("p (t n) -> p t n", t=2)
            hv = [hb[:, t, :, :].rearrange("p h n -> p (h n)") for t in range(2)]
            t_g = [[], []]
            for t in range(2):
                for i in range(2):
                    y = Y[2 * t + i]
                    c = slice(384 * i, 384 * i + 384)
                    y.free = act(lambda e, y=y, t=t, c=c: e.activation(og[:, t, c], y.t[:, 0:384], ACT.Sigmoid), ty[t], t_a[3])
                    d6 = dve(lambda e, t=t, c=c: e.tensor_tensor(og[:, t, c], og[:, t, c], hn[:, c], ALU.mult), y.free, t_hn)
                    t_g[i].append(dve(lambda e, t=t, c=c: e.tensor_tensor(hv[t][:, c], hv[t][:, c], og[:, t, c], ALU.mult), d6,
                                      [t_h[h] for h in range(4)]))
            done = [[], [], []]

            def turned(q):
                b = bank()
                for k in range(2):
                    for t in range(2):
                        tk = tr(b.t[:, 256 * k + 128 * t:256 * k + 128 * t + 128], hv[t][:, 128 * (2 * q + k):128 * (2 * q + k) + 128],
                                128, t_g[0], t_g[1] if q else None, b.free, sig=(k == 1 and t == 1))
                b.free = split_to(mhi[:, 2 * q:2 * q + 2, :], mlo[:, 2 * q:2 * q + 2, :], blocks(b.t[:, :], 256), tk)
                done[q].extend(b.free)

            return t_mem + done, {0: lambda: (turned(0), turned(1), turned(2))}

        t_ax = scale_x(ALPHA1, t_x)
        t_m = []

        def split_memory(t_load):
            for q in range(4):
                t_m.append(split_to(mhi[:, 2 * q:2 * q + 2, :], mlo[:, 2 * q:2 * q + 2, :], memT[:, 2 * q:2 * q + 2, :], t_load))

        FFN = ("ffn_w_gate", "ffn_w_up", "ffn_w_down", FF // 256)
        for l in range(2):
            ty = ffn(*FFN, xt_ready, between={6: lambda: split_memory(t_mem)} if l == 0 else {})
            fill = [lambda: memory_keys(0, t_m), lambda: memory_values(0, t_m)] if l == 0 else []
            done, xt_ready, t_ax = layer_norm(ty, t_ax, True, gbv, t_gb, ALPHA1, fill=fill)
            if l == 0:
                t_gb = next_gb(1, done)
                mix, hook = conv_mixer(xt_ready, done), {}
            else:
                mix, hook = mlstm_mixer(xt_ready, done)
                t_gb = next_gb(4, mix[0])
            ty = big_rows("w_out", 4, mhi, mlo, each=mix, hook=hook)
            done, xt_ready, t_ax = layer_norm(ty, t_ax, False, gbv, t_gb, ALPHA1)
            t_gb = next_gb(3 * l + 2, done)
            if l == 0:
                t_mem = sp.dma(memT, blocks(A["memT"][:, :], T), s_mem, done, xt_ready)
                t_m = []
                ty = ffn(*FFN, xt_ready, between={6: lambda: split_memory(t_mem)})
                done, xt_ready, t_ax = layer_norm(ty, t_ax, True, gbv, t_gb, ALPHA1,
                                                  fill=[lambda: memory_keys(1, t_m), lambda: memory_values(1, t_m)])
                t_gb = next_gb(3, done)
            else:
                gin = ar[:, 0:2 * D]
                t_gin = pool.dma(gin, A["ln"][6:7, :].broadcast_to((128, 2 * D)), s_gbin, done, xt_ready)
                ty = ffn(*FFN, xt_ready)
                done, _, _ = layer_norm(ty, t_ax, True, gbv, t_gb, turn=False, dst=r)
        done, xt_ready, t_ax = layer_norm(None, done, False, gin, t_gin, ALPHA2)

        arena = Arena()
        ty = big_rows("w_in_2", 4, xhi, xlo, xt_ready, n=672, splits=((0, 384), (384, 672)))
        va = ar[:, 0:1024].rearrange("p (t h n) -> p t h n", t=2, h=8)
        cq = arena.take(2 * 384).rearrange("p (t n) -> p t n", t=2)
        ck = arena.take(2 * 288).rearrange("p (t n) -> p t n", t=2)
        ss = arena.take(8)
        hfl = hf[:, :, :, :].rearrange("p a b n -> p (a b n)")
        junk = hfl[:, 512:896]
        tmp = arena.take(4 * 128).rearrange("p (s n) -> p s n", s=4)
        q1 = None
        for t in range(2):
            for i, wdt in ((0, 384), (1, 256)):
                y = Y[2 * t + i]
                q1 = act(lambda e, t=t, i=i, wdt=wdt, y=y: e.activation(junk[:, 0:wdt], y.t[:, 0:wdt], ACT.Square,
                                                                        accum_out=ss[:, 2 * t + i:2 * t + i + 1]), ty[t], done, q1)
        for i, wdt in ((0, 384), (1, 256)):
            sv = ss[:, 0:4].rearrange("p (t i) -> p t i", i=2)[:, :, i]
            q2 = dve(lambda e, sv=sv, wdt=wdt: e.tensor_scalar(sv, sv, 1.0 / wdt, RMS_EPS, ALU.mult, ALU.add), q1)
        q3 = pool(lambda e: e.tensor_tensor(ss[:, 4:8], ss[:, 0:4], mhalf[:, 0:4], ALU.pow), q2, t_mhalf)
        for t in range(2):
            for i, o, wdt in ((0, cq, 384), (1, ck, 256)):
                y = Y[2 * t + i]
                q4 = dve(lambda e, t=t, i=i, o=o, wdt=wdt, y=y: e.tensor_scalar(o[:, t, 0:wdt], y.t[:, 0:wdt],
                                                                                 ss[:, 4 + 2 * t + i:5 + 2 * t + i], None, ALU.mult), q3)
                y.free = q4
        t_kr = None
        kr = arena.take(2 * 32).rearrange("p (t n) -> p t n", t=2)
        for t in range(2):
            y = Y[2 * t + 1]
            y1, y2 = y.t[:, 256:272], y.t[:, 272:288]
            c_, s_ = cosA[:, t, :], sinA[:, t, :]
            q5 = dve(lambda e, y1=y1, c_=c_: e.tensor_tensor(tmp[:, 0, 0:16], y1, c_, ALU.mult), q4, t_cs, t_kr)
            q5 = dve(lambda e, y2=y2, s_=s_: e.tensor_tensor(tmp[:, 1, 0:16], y2, s_, ALU.mult))
            q5 = dve(lambda e, y2=y2, c_=c_: e.tensor_tensor(tmp[:, 2, 0:16], y2, c_, ALU.mult))
            q5 = dve(lambda e, y1=y1, s_=s_: e.tensor_tensor(tmp[:, 3, 0:16], y1, s_, ALU.mult))
            y.free = q5
            dve(lambda e, t=t: e.tensor_tensor(kr[:, t, 0:16], tmp[:, 0, 0:16], tmp[:, 1, 0:16], ALU.subtract), q5)
            t_kr = dve(lambda e, t=t: e.tensor_tensor(kr[:, t, 16:32], tmp[:, 2, 0:16], tmp[:, 3, 0:16], ALU.add), q5)
        up_ = arena.take(4 * 272).rearrange("p (b n) -> p b n", b=4)
        up_wsum = ar[:, arena.at - 4 * 272:arena.at + 4 * 272]
        wsum = arena.take(4 * 272).rearrange("p (b n) -> p b n", b=4)
        p0 = pool(lambda e: e.memset(up_[:, :, 0:16], 0.0), done)
        for j in range(2):
            b, tk = pair(Tile("w_in_2", 256 * j), xhi, xlo)
            ev = act(lambda e, j=j, b=b: e.activation(up_[:, 2 * j:2 * j + 2, 16:272], blocks(b.t[:, :], 256), ACT.Copy), tk)
            b.free = ev
        wt2 = arena.take(4 * 272).rearrange("p (b n) -> p b n", b=4)
        t_pl = []
        for g in range(4):
            src, cur = up_[:, g, :], ev
            bufs = [wsum[:, g, :], wt2[:, g, :]]
            lo = 0
            for s in range(g + 1):
                step = 1 << s
                dst = bufs[s % 2]
                lo += step
                cur = pool(lambda e, dst=dst, src=src, lo=lo, step=step: e.tensor_tensor(
                    dst[:, lo:272], src[:, lo:272], src[:, lo - step:272 - step], ALU.add), cur, p0)
                src = dst
            o = wt2[:, g, :] if g % 2 == 0 else wsum[:, g, :]
            cur = pool(lambda e, src=src, o=o, g=g: e.tensor_tensor(o[:, 16:32], src[:, 16:32], P("cnt", 16 * g, 16 * g + 16), ALU.mult), cur)
            cu2 = pool(lambda e, src=src, o=o, g=g: e.tensor_scalar(o[:, 32:272], src[:, 32:272], 1.0 / (2 << g), None, ALU.mult), cur)
            cur = pool(lambda e, o=o, g=g: e.tensor_tensor(o[:, 16:272], o[:, 16:272], up_[:, g, 16:272], ALU.subtract), cur, cu2)
            t_pl.append((o, cur))

        t_lat = []
        for i, o, nb_, g in ((0, cq, 3, "q_g"), (1, ck, 2, "kv_g")):
            for k in range(nb_):
                b = bank()
                for t in range(2):
                    tk = tr(b.t[:, 128 * t:128 * t + 128], o[:, t, 128 * k:128 * k + 128], 128, q4, b.free, sig=(t == 1))
                dst = (mhi[:, 4 + k, :], mlo[:, 4 + k, :]) if i == 0 else (hhi[:, 0, k, :], hlo[:, 0, k, :])
                ev = split_to(dst[0], dst[1], b.t[:, 0:256], tk, scale=P(g, k, k + 1))
                b.free = ev
                t_lat.append(ev)

        zc = arena.take(4 * 286).rearrange("p (b n) -> p b n", b=4)
        ca = kT[:, :, :, :].rearrange("p a b n -> p (a b) n")
        sg = hfl[:, 0:512]
        dwt = P("conv_dw").rearrange("p (b w) -> p b w", w=31)
        z0 = pool(lambda e: e.memset(zc[:, :, 0:30], 0.0), done)
        t_z, t_c = [], [None] * 4
        cp = tmp.rearrange("p (s r) n -> p s (r n)", s=2)
        sg_read = None
        for j in range(2):
            ba, ta = pair(Tile("w_in_2", 512 + 256 * j), xhi, xlo)
            bg, tg = pair(Tile("w_in_2", 1024 + 256 * j), xhi, xlo)
            s1 = act(lambda e, bg=bg: e.activation(sg, bg.t[:, :], ACT.Sigmoid), tg, sg_read)
            bg.free = s1
            s2 = dve(lambda e, j=j, ba=ba: e.tensor_tensor(zc[:, 2 * j:2 * j + 2, 30:286], blocks(sg, 256),
                                                           blocks(ba.t[:, :], 256), ALU.mult), s1, ta, z0)
            ba.free = s2
            sg_read = s2
            t_z.append(s2)
            t_cz = s2
        conv_steps = [(q, w) for w in range(31) for q in range(2)] + [(2, w) for w in range(31)]

        def conv_pool():
            t_c[3] = pool(lambda e: e.tensor_scalar(ca[:, 3, :], zc[:, 3, 0:256], dwt[:, 3, 0:1], P("conv_b", 3, 4),
                                                    ALU.mult, ALU.add), t_z[1])
            for w in range(1, 31):
                o = cp[:, w % 2, :]
                m_ = pool(lambda e, w=w, o=o: e.tensor_scalar(o, zc[:, 3, w:w + 256], dwt[:, 3, w:w + 1], None, ALU.mult), t_c[3], t_q)
                t_c[3] = pool(lambda e, o=o: e.tensor_tensor(ca[:, 3, :], ca[:, 3, :], o, ALU.add), m_)

        def conv_some(n):
            for _ in range(min(n, len(conv_steps))):
                b, w = conv_steps.pop(0)
                if w == 0:
                    t_c[b] = dve(lambda e, b=b: e.tensor_scalar(ca[:, b, :], zc[:, b, 0:256], dwt[:, b, 0:1], P("conv_b", b, b + 1),
                                                                ALU.mult, ALU.add), t_z[b // 2])
                else:
                    t_c[b] = dve(lambda e, b=b, w=w: e.scalar_tensor_tensor(
                        out=ca[:, b, :], in0=zc[:, b, w:w + 256], scalar=dwt[:, b, w:w + 1], in1=ca[:, b, :],
                        op0=ALU.mult, op1=ALU.add), t_c[b])

        qf = arena.take(2 * 768).rearrange("p (t h n) -> p t h n", t=2, h=8)
        kf = r[:, :, 0:768].rearrange("p t (h n) -> p t h n", h=8)
        free = [b.free for b in Y]
        for i, wdt in ((0, 512), (1, 256)):
            w = Tile("w_uq_2", 512 * i)
            tk = rowsof(w, mhi[:, 4:7, :], mlo[:, 4:7, :], 0, [(t, Y[2 * t + i].t[:, 0:wdt], 0, wdt) for t in range(2)], True, True,
                        t_lat, free)
            conv_some(6)
            for t in range(2):
                y = Y[2 * t + i]
                o = qf[:, t, :, :].rearrange("p h n -> p (h n)")[:, 512 * i:512 * i + wdt]
                y.free = act(lambda e, o=o, wdt=wdt, y=y: e.activation(o, y.t[:, 0:wdt], ACT.Copy), tk)
                q6 = y.free
        t_q = []
        for t in range(2):
            x1, x2 = qf[:, t, :, 64:80], qf[:, t, :, 80:96]
            tv = [tmp[:, s, :].rearrange("p (h n) -> p h n", h=8) for s in range(4)]
            cb_ = cosA[:, t, :].unsqueeze(1).to_broadcast([128, 8, 16])
            sb_ = sinA[:, t, :].unsqueeze(1).to_broadcast([128, 8, 16])
            m = [pool(lambda e, o=o, a=a, c=c: e.tensor_tensor(o, a, c, ALU.mult), q6, t_cs, t_kr, t_q)
                 for o, a, c in ((tv[0], x1, cb_), (tv[1], x2, sb_), (tv[2], x2, cb_), (tv[3], x1, sb_))]
            m1 = pool(lambda e, x1=x1, tv=tv: e.tensor_tensor(x1, tv[0], tv[1], ALU.subtract), m[-1])
            t_q = [pool(lambda e, x2=x2, tv=tv: e.tensor_tensor(x2, tv[2], tv[3], ALU.add), m1)]
        ty = big_rows("w_ukv_2", 1, hhi[:, 0, :, :], hlo[:, 0, :, :], t_lat)
        t_k, t_v = [], []
        for t in range(2):
            for i in range(2):
                y = Y[2 * t + i]
                yv = y.t[:, :].rearrange("p (h n) -> p h n", h=4)
                a1 = act(lambda e, t=t, i=i, yv=yv: e.activation(kf[:, t, 4 * i:4 * i + 4, 0:64], yv[:, :, 0:64], ACT.Copy), ty[t])
                y.free = act(lambda e, t=t, i=i, yv=yv: e.activation(va[:, t, 4 * i:4 * i + 4, :], yv[:, :, 64:128], ACT.Copy), ty[t])
                t_k.append(y.free)
            krb = kr[:, t, :].unsqueeze(1).to_broadcast([128, 8, 32])
            t_k.append(pool(lambda e, t=t, krb=krb: e.tensor_copy(kf[:, t, :, 64:96], krb), t_kr, ty))
        conv_some(12)

        mg = arena.take(8 * T)
        mgb = mg.rearrange("p (b n) -> p b n", b=8)

        def flat3(z):
            return z.rearrange("p b n -> p (b n)")

        G0 = [mg[:, 512 * j:512 * j + 512] for j in range(4)]
        G1 = [flat3(z[:, s, :, :]) for z in (vm, hf) for s in range(2)]
        G2 = [gb[:, s, 512 * h:512 * h + 512] for s in range(2) for h in range(2)]
        gate = {"n": 0}
        t_gate = {}

        def gate_half(*after):
            n, j, f = gate["n"] // 8, gate["n"] // 2 % 4, gate["n"] % 2
            gate["n"] += 1
            if f == 0:
                gate["w"] = Tile("w_in_2", 2208 + 1024 * n + 256 * j)
            w, b = gate["w"], bank()
            tk = cols(b.t[:, 0:256], w, 128 * f, 128, xhi, xlo, b.free)
            if f == 1:
                w.done(tk)
            o, blk = (G0, G1, G2)[n][j][:, 256 * f:256 * f + 256], 8 * n + 2 * j + f
            b.free = act(lambda e: e.activation(o, b.t[:, 0:256], ACT.Identity if n else ACT.Sigmoid,
                                                bias=P("b_gate", blk, blk + 1)), tk, list(after))
            t_gate[n, j] = b.free

        def gate_sigmoid(n, j):
            o = (G0, G1, G2)[n][j]
            t_gate[n, j] = act(lambda e: e.activation(o, o, ACT.Sigmoid), t_gate[n, j])

        def project(name, hi, lo, ready, use):
            free_ = [b.free for b in Y]
            for j in range(2):
                w = Tile(name, 512 * j)
                for f in range(4):
                    blk = 4 * j + f
                    tk = cols(Y[blk // 2].t[:, 256 * (blk % 2):256 * (blk % 2) + 256], w, 128 * f, 128, hi, lo, ready, free_)
                w.done(tk)
                use(2 * j, tk)
                use(2 * j + 1, tk)

        conv_pool()
        for _ in range(8):
            gate_half()
            conv_some(3)
        t_yp = []
        for g in range(4):
            o, cur = t_pl[g]
            b = bank()
            t_pw = mm(b.t[:, 0:256], P("pool_w", 128 * g, 128 * g + 128), o[:, 16:272], True, True, cur, b.free, sig=True)
            ev = split_to(mhi[:, g, :], mlo[:, g, :], b.t[:, 0:256], t_pw, scale=P("pool_scale", g, g + 1))
            b.free = ev
            t_yp.append(ev)
        conv_some(4)
        t_mg = [None] * 4

        def use_pool(j, tk):
            y = Y[j]
            y.free = t_mg[j] = dve(lambda e: e.tensor_tensor(G0[j], G0[j], y.t[:, :], ALU.mult), tk, t_gate[0, j])
            conv_some(4)

        project("pool_proj_2", mhi[:, 0:4, :], mlo[:, 0:4, :], t_yp, use_pool)

        qkT = [r[0:96, :, 768:1024], blocks(up_wsum[0:96, 1536:2048], 256)]
        S = [up_wsum[:, 384 * i:384 * i + 384] for i in range(2)]
        pTb = [up_wsum[:, 768 + 384 * i:1152 + 384 * i] for i in range(2)]
        ob = flat3(wt2)[:, 0:1024].rearrange("p (t n) -> p t n", t=2)
        mx = arena.take(16)
        sm = arena.take(16)
        ri = arena.take(16)
        qscale = 96.0 ** -0.5
        o_b = [Y[0], Y[1]]
        o_free = [Y[0].free, Y[1].free]
        p_read, pT_read, q_read = [t_pw] * 2, [t_pw] * 2, [None] * 2
        t_qk, t_s, t_pT = {}, {}, {}

        def turn_qk(h):
            i = h % 2
            b = bank()
            for n, src in enumerate((qf, kf)):
                for t in range(2):
                    tk = tr(b.t[0:96, 256 * n + 128 * t:256 * n + 128 * t + 128], src[:, t, h, :], 128, t_q, t_k, b.free,
                            sig=(n == 1 and t == 1))
            b.free = t_qk[h] = act(lambda e: e.activation(qkT[i], blocks(b.t[0:96, :], 256), ACT.Copy), tk, q_read[i], t_pw)

        def scores(h):
            i = h % 2
            b = bank()
            mm(b.t[:, 0:128], qkT[i][:, 0, 0:128], qkT[i][:, 1, 0:128], True, True, t_qk[h], b.free)
            tk = mm(b.t[:, 128:384], qkT[i][:, 0, 128:256], qkT[i][:, 1, :], True, True, sig=True)
            q_read[i] = tk
            d1 = dve(lambda e: e.scalar_tensor_tensor(out=S[i], in0=b.t[:, 0:384], scalar=qscale, in1=P("mask"),
                                                      op0=ALU.mult, op1=ALU.add), tk, p_read[i])
            b.free = d1
            for t, (c0, c1_) in enumerate(((0, 128), (128, 384))):
                d2 = dve(lambda e, t=t, c0=c0, c1_=c1_: e.tensor_reduce(mx[:, 2 * h + t:2 * h + t + 1], S[i][:, c0:c1_],
                                                                        X, ALU.max, negate=True), d1)
            for t, (c0, c1_) in enumerate(((0, 128), (128, 384))):
                t_s[h] = act(lambda e, t=t, c0=c0, c1_=c1_: e.activation(
                    S[i][:, c0:c1_], S[i][:, c0:c1_], ACT.Exp, bias=mx[:, 2 * h + t:2 * h + t + 1],
                    accum_out=sm[:, 2 * h + t:2 * h + t + 1]), d2)

        def turn_p(h):
            i = h % 2
            b = bank()
            for n in range(3):
                tk = tr(b.t[:, 128 * n:128 * n + 128], S[i][:, 128 * n:128 * n + 128], 128, t_s[h], b.free, sig=(n == 2))
            p_read[i] = tk
            b.free = t_pT[h] = act(lambda e: e.activation(pTb[i], b.t[:, 0:384], ACT.Copy), tk, pT_read[i])

        def values(h):
            i = h % 2
            mm(o_b[0].t[:, 64 * h:64 * h + 64], pTb[i][:, 0:128], va[:, 0, h, :], True, True, t_pT[h], t_k, o_free)
            mm(o_b[1].t[:, 64 * h:64 * h + 64], pTb[i][:, 128:256], va[:, 0, h, :], True, False)
            pT_read[i] = mm(o_b[1].t[:, 64 * h:64 * h + 64], pTb[i][:, 256:384], va[:, 1, h, :], False, True, sig=True)

        g_free = [done, t_cz, q1]
        for step in range(11):
            for back, stage in ((3, values), (2, turn_p), (1, scores), (0, turn_qk)):
                if 0 <= step - back < 8:
                    stage(step - back)
            gate_half(g_free)
            conv_some(5)
        conv_some(1000)
        d3 = dve(lambda e: e.reciprocal(ri, sm), t_s[7])
        for t in range(2):
            rv = ri.rearrange("p (h t) -> p t h", t=2)[:, t, :].unsqueeze(2).to_broadcast([128, 8, 64])
            d4 = dve(lambda e, t=t, rv=rv: e.tensor_tensor(ob[:, t, :].rearrange("p (h n) -> p h n", n=64),
                                                           o_b[t].t[:, :].rearrange("p (h n) -> p h n", n=64), rv, ALU.mult),
                     d3, pT_read, t_pw)
            o_b[t].free = d4

        ones = arena.take(128)
        dg = arena.take(256)
        vc = arena.take(4)
        t_on = pool(lambda e: e.memset(ones, 1.0 / 512), done)
        bm = bank()
        for k in range(4):
            tk = mm(bm.t[:, 0:256], ones, ca[:, k, :], k == 0, k == 3, t_on, t_c, bm.free, sig=(k == 3))
        mb = bm.t[:, 0:256].unsqueeze(1).to_broadcast([128, 4, 256])
        c1 = dve(lambda e: e.tensor_tensor(ca, ca, mb, ALU.subtract), tk)
        bm.free = c1
        sq = zc[:, :, 0:256]
        c2 = act(lambda e: e.activation(sq, ca, ACT.Square), c1)
        gate_half(g_free)
        gate_half(g_free)
        t_yo = []
        for q in range(2):
            b = bank()
            for k in range(2):
                for t in range(2):
                    tk = tr(b.t[:, 256 * k + 128 * t:256 * k + 128 * t + 128], ob[:, t, 128 * (2 * q + k):128 * (2 * q + k) + 128], 128,
                            d4, b.free, sig=(k == 1 and t == 1))
            ev = split_to(mhi[:, 2 * q:2 * q + 2, :], mlo[:, 2 * q:2 * q + 2, :], blocks(b.t[:, :], 256), tk)
            b.free = ev
            t_yo.append(ev)
        bv = bank()
        for t in range(2):
            for k in range(4):
                tk = mm(bv.t[:, t:t + 1], sq[:, k, 128 * t:128 * t + 128], ones[:, 0:1], k == 0, k == 3, c2, bv.free,
                        sig=(t == 1 and k == 3))
        c3 = dve(lambda e: e.tensor_scalar(vc[:, 0:2], bv.t[:, 0:2], LN_EPS, None, ALU.add), tk)
        bv.free = c3
        c4 = pool(lambda e: e.tensor_tensor(vc[:, 2:4], vc[:, 0:2], mhalf[:, 0:2], ALU.pow), c3, t_mhalf)
        for t in range(2):
            c5 = dve(lambda e, t=t: e.tensor_scalar(dg[:, 128 * t:128 * t + 128], ident, vc[:, 2 + t:3 + t], 512.0, ALU.mult, ALU.mult), c4)
        gate_half(g_free)
        br = bank()
        tk = mm(br.t[:, 0:256], ones, dg, True, True, c5, br.free, sig=True)
        rb = br.t[:, 0:256].unsqueeze(1).to_broadcast([128, 4, 256])
        c6 = dve(lambda e: e.tensor_tensor(ca, ca, rb, ALU.mult), tk)
        br.free = c6
        for k in range(4):
            c7 = act(lambda e, k=k: e.activation(ca[:, k, :], ca[:, k, :], ACT.Silu, bias=P("conv_lb", k, k + 1),
                                                 scale=P("conv_g", k, k + 1)), c6)
        gate_half(g_free)
        gate_half(g_free)
        assert gate["n"] == 24
        for j in range(4):
            gate_sigmoid(2, j)
        t_yc = split_to(mhi[:, 4:8, :], mlo[:, 4:8, :], ca, c7)


        def use_mla(j, tk):
            y = Y[j]
            s1 = dve(lambda e: e.tensor_tensor(G2[j], G2[j], y.t[:, :], ALU.mult), tk, t_gate[2, j])
            y.free = s1
            t_mg[j] = pool(lambda e: e.tensor_tensor(G0[j], G0[j], G2[j], ALU.add), s1, t_mg[j])

        project("mla_proj_2", mhi[:, 0:4, :], mlo[:, 0:4, :], t_yo, use_mla)
        t_gb = next_gb(7, t_mg)
        for j in range(4):
            gate_sigmoid(1, j)
        tm = []

        def use_conv(j, tk):
            y = Y[j]
            s1 = dve(lambda e: e.tensor_tensor(G1[j], G1[j], y.t[:, :], ALU.mult), tk, t_gate[1, j])
            y.free = s1
            s2 = dve(lambda e: e.tensor_tensor(G0[j], G0[j], G1[j], ALU.add), s1, t_mg[j])
            tm.append(split_to(mhi[:, 2 * j:2 * j + 2, :], mlo[:, 2 * j:2 * j + 2, :], mgb[:, 2 * j:2 * j + 2, :], s2))

        project("conv_proj_2", mhi[:, 4:8, :], mlo[:, 4:8, :], t_yc, use_conv)
        ty = big_rows("w_out_2", 4, mhi, mlo, each=tm)
        done, xt_ready, t_ax = layer_norm(ty, t_ax, False, gbv, t_gb)
        t_gb = next_gb(8, done)

        arena = Arena()
        pTr = blocks(arena.take(2 * T), T)
        t_p = pool.dma(pTr, blocks(A["pT"][:, :], T), s_p, done)
        pbc = arena.take(NEXP * T).rearrange("p (e n) -> p e n", e=NEXP)
        sel16 = arena.take(NEXP * 128)[0:16].rearrange("p (e n) -> p e n", e=NEXP)
        z16 = pool(lambda e: e.memset(sel16, 0.0), done)
        t_s16 = pool(lambda e: e.affine_select(out=sel16, in_=sel16, compare_op=ALU.not_equal, fill=1.0, base=0,
                                               pattern=[[-1, NEXP], [0, 128]], channel_multiplier=1), z16)
        before = arena.take(128)
        allone = arena.take(128)
        z1 = pool(lambda e: e.memset(before, 1.0), done)
        z1 = pool(lambda e: e.affine_select(out=before, in_=before, compare_op=ALU.is_gt, fill=0.0, base=0,
                                            pattern=[[1, 128]], channel_multiplier=-1), z1)
        t_bef = pool(lambda e: e.memset(allone, 1.0), z1)
        slot_i = arena.take(256).bitcast(i32)
        slot_row = arena.take(128)
        slot_col = arena.take(2)
        z2 = pool(lambda e: e.iota(slot_i[:, 0:128], [[1, 128]], base=0, channel_multiplier=0), done)
        z2 = pool(lambda e: e.iota(slot_i[:, 128:129], [[0, 1]], base=0, channel_multiplier=1), z2)
        z3 = pool(lambda e: e.tensor_copy(slot_row, slot_i[:, 0:128]), z2)
        t_slot = pool(lambda e: e.tensor_copy(slot_col[:, 0:1], slot_i[:, 128:129]), z3)
        w = Tile("w_router_2", 0)
        b = bank()
        tk = rowsof(w, xhi, xlo, 0, [(t, b.t[:, 16 * t:16 * t + 16], 0, 16) for t in range(2)], True, True, xt_ready, b.free)
        v = arena.take(32 * 8).rearrange("p (s t n) -> p s t n", s=8, t=2)
        aff, sel, s3, s4, oh1, oh2, desc, wgt = [v[:, i, :, :] for i in range(8)]
        a1 = act(lambda e, b=b: e.activation(aff, blocks(b.t[:, 0:32], 16), ACT.Sigmoid), tk, done)
        b.free = a1
        for n in range(16):
            t_d = pool(lambda e, n=n: e.memset(desc[:, :, n:n + 1], 16.0 - n), done)
        rb_ = brow[:, 8:24].unsqueeze(1).to_broadcast([128, 2, 16])
        d = dve(lambda e: e.tensor_tensor(sel, aff, rb_, ALU.add), a1, t_brow)
        sg4 = sel.rearrange("p t (g n) -> p (t g) n", n=4)
        pr = arena.take(8 * 6).rearrange("p (g n) -> p g n", n=6)
        d1 = dve(lambda e: e.tensor_tensor(pr[:, :, 0:3], sg4[:, :, 0:3], sg4[:, :, 1:4], ALU.add), d)
        d1 = dve(lambda e: e.tensor_tensor(pr[:, :, 3:5], sg4[:, :, 0:2], sg4[:, :, 2:4], ALU.add))
        d1 = dve(lambda e: e.tensor_tensor(pr[:, :, 5:6], sg4[:, :, 0:1], sg4[:, :, 3:4], ALU.add))
        gsc = arena.take(8).rearrange("p (t g) -> p t g", t=2)
        d1 = dve(lambda e: e.tensor_reduce(gsc.rearrange("p t g -> p (t g)"), pr, X, ALU.max), d1)

        small = arena.take(8)

        def first_max(oh, src, n, d):
            m_ = small[:, 0:2]
            dd = desc[:, :, 0:n]
            d = dve(lambda e: e.tensor_reduce(m_, src, X, ALU.max), d)
            d = dve(lambda e: e.tensor_tensor(oh, src, m_.unsqueeze(2).to_broadcast([128, 2, n]), ALU.is_equal), d)
            d = dve(lambda e: e.tensor_tensor(oh, oh, dd, ALU.mult), d, t_d)
            d = dve(lambda e: e.tensor_reduce(m_, oh, X, ALU.max), d)
            return dve(lambda e: e.tensor_tensor(oh, dd, m_.unsqueeze(2).to_broadcast([128, 2, n]), ALU.is_equal), d)

        gk = arena.take(8).rearrange("p (t g) -> p t g", t=2)
        d1 = first_max(gk, gsc, 4, d1)
        BIG = 1e30
        gkb = arena.take(8).rearrange("p (t g) -> p t g", t=2)
        d2 = dve(lambda e: e.tensor_scalar(gkb, gk, BIG, -BIG, ALU.mult, ALU.add), d1)
        s34 = s3.rearrange("p t (g n) -> p (t g) n", n=4)
        gk8 = gk.rearrange("p t g -> p (t g)").unsqueeze(2).to_broadcast([128, 8, 4])
        gkb8 = gkb.rearrange("p t g -> p (t g)").unsqueeze(2).to_broadcast([128, 8, 4])
        d2 = dve(lambda e: e.tensor_tensor(s34, sg4, gk8, ALU.mult), d2)
        d2 = dve(lambda e: e.tensor_tensor(s34, s34, gkb8, ALU.add), d2)
        d2 = first_max(oh1, s3, 16, d2)
        d2 = dve(lambda e: e.scalar_tensor_tensor(out=s4, in0=oh1, scalar=-2 * BIG, in1=s3, op0=ALU.mult, op1=ALU.add), d2)
        d2 = first_max(oh2, s4, 16, d2)
        d2 = dve(lambda e: e.tensor_tensor(oh1, oh1, oh2, ALU.add), d2)
        t_pick = d2
        d2 = dve(lambda e: e.tensor_tensor(wgt, oh1, aff, ALU.mult), d2)
        m_ = small[:, 2:4]
        d2 = dve(lambda e: e.tensor_reduce(m_, wgt, X, ALU.add), d2)
        d2 = dve(lambda e: e.reciprocal(small[:, 4:6], m_), d2)
        d2 = dve(lambda e: e.tensor_tensor(wgt, wgt, small[:, 4:6].unsqueeze(2).to_broadcast([128, 2, 16]), ALU.mult), d2)
        t_wgt = d2

        t_tok = []
        for t in range(2):
            v0 = [z[:, :, :].rearrange("p b n -> p (b n)")[:, D * t:D * t + D] for z in (mhi, mlo)]
            t_tok.append(split_to(v0[0], v0[1], x[:, t, :], done))
        t_ax = [pool(lambda e, t=t: e.tensor_scalar(x[:, t, :], x[:, t, :], ALPHA2, None, ALU.mult), t_ax[t], t_tok[t]) for t in range(2)]

        ty = big_rows("ple_gate_2", 4, xhi, xlo)
        t_tail = [ty]
        pg = r
        t_sg = []
        for t in range(2):
            for i in range(2):
                y = Y[2 * t + i]
                y.free = act(lambda e, t=t, i=i, y=y: e.activation(pg[:, t, 512 * i:512 * i + 512], y.t[:, :], ACT.Sigmoid), ty[t], done)
                t_sg.append(y.free)
        t_pp = split_to(hhi[:, 0, :, :], hlo[:, 0, :, :], pTr, t_p)
        ty = big_rows("ple_proj_2", 1, hhi[:, 0, :, :], hlo[:, 0, :, :], t_pp)
        t_tail.append(ty)
        for t in range(2):
            for i in range(2):
                y = Y[2 * t + i]
                o = pg[:, t, 512 * i:512 * i + 512]
                e1 = dve(lambda e, o=o, y=y: e.tensor_tensor(o, o, y.t[:, :], ALU.mult), ty[t], t_sg)
                y.free = e1
            t_ax[t] = pool(lambda e, t=t: e.tensor_tensor(x[:, t, :], x[:, t, :], pg[:, t, :], ALU.add), e1, t_ax[t])

        posm = arena.take(32).rearrange("p (t n) -> p t n", t=2)
        posT = arena.take(T)[0:16]
        flag = arena.take(4)
        b = bank()
        mm(b.t[:, 0:16], before, oh1[:, 0, :], True, True, t_pick, t_bef, b.free)
        mm(b.t[:, 16:32], before, oh1[:, 1, :], True, False)
        mm(b.t[:, 16:32], allone, oh1[:, 0, :], False, True)
        mm(b.t[:, 32:48], allone, oh1[:, 0, :], True, False)
        tk = mm(b.t[:, 32:48], allone, oh1[:, 1, :], False, True, sig=True)
        d3 = dve(lambda e, b=b: e.scalar_tensor_tensor(out=posm, in0=blocks(b.t[:, 0:32], 16), scalar=1e4, in1=oh1,
                                                       op0=ALU.add, op1=ALU.mult), tk)
        d4 = dve(lambda e, b=b: e.tensor_reduce(flag[:, 0:1], b.t[:, 32:48], X, ALU.max), d3)
        b.free = d4
        d3 = dve(lambda e: e.tensor_scalar(posm, posm, 1e4, None, ALU.subtract), d3)
        t_flag = dve(lambda e: e.tensor_scalar(flag[:, 1:2].bitcast(i32), flag[:, 0:1], 128.5, None, ALU.is_gt), d4)
        b = bank()
        for t in range(2):
            tk = tr(b.t[0:16, 128 * t:128 * t + 128], posm[:, t, :], 128, d3, b.free, sig=(t == 1))
        d5 = dve(lambda e, b=b: e.tensor_copy(posT, b.t[0:16, 0:256]), tk)
        b.free = d5
        t_pb = []
        for e2 in range(NEXP // 2):
            b = bank()
            for q in range(2):
                tk = mm(b.t[:, 256 * q:256 * q + 256], sel16[:, 2 * e2 + q, :], posT, True, True, d5, t_s16, b.free, sig=(q == 1))
            ev = act(lambda e, e2=e2, b=b: e.activation(pbc[:, 2 * e2:2 * e2 + 2, :].rearrange("p e n -> p (e n)"), b.t[:, :], ACT.Copy), tk)
            b.free = ev
            t_pb.append(ev)

        gx_hi, gx_lo = [z[:, 0:4, :].rearrange("p b n -> p (b n)").rearrange("p (k n) -> p k n", n=128) for z in (xhi, xlo)]
        y_hi, y_lo = [z[:, 4:8, :].rearrange("p b n -> p (b n)") for z in (xhi, xlo)]
        tok_hi, tok_lo = [z[:, :, :].rearrange("p b n -> p (b n)").rearrange("p (t d) -> p t d", t=2) for z in (mhi, mlo)]
        hT = [[z[:, s, :, :].rearrange("p b n -> p (b n)").rearrange("p (k n) -> p k n", n=128) for z in (hhi, hlo)] for s in range(2)]
        wsl = arena.take(2)
        places = arena.take(32).rearrange("p (t n) -> p t n", t=2)
        col0 = arena.take(2)

        def experts(place0, t_x, *after):
            after = list(after)
            start = place0 == 0
            if start:
                place, col, t_pl = posm, slot_col, [t_slot, d3]
            else:
                place, col = places, col0
                p1 = dve(lambda e: e.tensor_scalar(places, posm, float(place0), None, ALU.subtract), after)
                t_pl = [dve(lambda e: e.tensor_scalar(col0[:, 0:1], slot_col[:, 0:1], float(place0), None, ALU.add), after), p1]
            S_read, T_read = [None, None], [None, None]
            t_gx, t_h, t_hT, t_y, t_T, up_done, w_read = [None], {}, {}, [None], {}, [None], [None]
            t_ws = {}
            y0 = [b.free for b in Y]

            def pick(e):
                s = e % 2
                for t in range(2):
                    q = dve(lambda g, t=t: g.tensor_scalar(gsel[:, s, t, :], slot_row, place[:, t, e:e + 1], None, ALU.is_equal),
                            t_pl, t_slot, S_read[s], after)
                return q

            def gather(e):
                s = e % 2
                t_s = t_pick_[e]
                evs = []
                for src, dst, eng in ((tok_hi, gx_hi, act), (tok_lo, gx_lo, act)):
                    for q in range(2):
                        b = bank()
                        for k in range(4):
                            for t in range(2):
                                c = 128 * (4 * q + k)
                                tk = mm(b.t[:, 128 * k:128 * k + 128], src[:, t, c:c + 128], gsel[:, s, t, :], t == 0, t == 1,
                                        t_s, t_x, b.free, sig=(k == 3 and t == 1))
                        b.free = act(lambda g, b=b, dst=dst, q=q: g.activation(dst[:, 4 * q:4 * q + 4, :], blocks(b.t[:, :], 128),
                                                                               ACT.Copy), tk, up_done[0], after)
                        evs.append(b.free)
                b = bank()
                for t in range(2):
                    tk = mm(b.t[:, 0:1], gsel[:, s, t, :].bitcast(f32), wgt[:, t, e:e + 1], t == 0, t == 1, t_wgt, b.free, sig=(t == 1))
                S_read[s] = tk
                b.free = dve(lambda g, b=b: g.tensor_copy(wsl[:, s:s + 1], b.t[:, 0:1]), tk, w_read[0])
                t_ws[e] = b.free
                t_gx[0] = evs

            def up(e):
                bg, bu = bank(), bank()
                k0 = 0
                for j in range(4):
                    w = Tile("exp_w_up_2")
                    for k in range(w.kb):
                        st, en = k0 + k == 0, k0 + k == 7
                        lh, ll = gx_hi[:, k0 + k, :], gx_lo[:, k0 + k, :]
                        for b, c in ((bg, 0), (bu, 512)):
                            mm(b.t[:, :], lh, w.hi[:, k, c:c + 512], st, False, w.ready, t_gx[0], b.free)
                        for b, c in ((bg, 0), (bu, 512)):
                            mm(b.t[:, :], lh, w.lo[:, k, c:c + 512], False, False)
                        for b, c in ((bg, 0), (bu, 512)):
                            tk = mm(b.t[:, :], ll, w.hi[:, k, c:c + 512], False, en, sig=(c == 512 and k == w.kb - 1))
                    w.done(tk)
                    k0 += w.kb
                up_done[0] = tk
                hs = hf[:, e % 2, :, :].rearrange("p b n -> p (b n)")
                t1 = act(lambda g: g.activation(hs, bg.t[:, :], ACT.Silu), tk, t_hT.get(e - 2), after)
                ws = wsl[:, e % 2:e % 2 + 1]
                t2 = dve(lambda g: g.scalar_tensor_tensor(out=hs, in0=bu.t[:, :], scalar=ws, in1=hs, op0=ALU.mult, op1=ALU.mult),
                         t1, tk, t_ws[e])
                w_read[0] = t2
                bg.free, bu.free = t1, t2
                t_h[e] = t2

            def turn(e):
                hs = hf[:, e % 2, :, :].rearrange("p b n -> p (b n)")
                b = bank()
                for k in range(4):
                    tk = tr(b.t[:, 128 * k:128 * k + 128], hs[:, 128 * k:128 * k + 128], 128, t_h[e], b.free, sig=(k == 3))
                hh, hl = hT[e % 2]
                b.free = t_hT[e] = split_to(hh, hl, blocks(b.t[:, :], 128), tk, t_hT.get(("read", e - 2)), after)

            def down(e):
                bs = [bank(), bank()]
                hh, hl = hT[e % 2]
                k0 = 0
                for j in range(2):
                    w = Tile("exp_w_down_2")
                    for k in range(w.kb):
                        st, en = k0 + k == 0, k0 + k == 3
                        for n, b in enumerate(bs):
                            mm(b.t[:, :], hh[:, k0 + k, :], w.hi[:, k, 512 * n:512 * n + 512], st, False, w.ready, t_hT[e], b.free)
                        for n, b in enumerate(bs):
                            mm(b.t[:, :], hh[:, k0 + k, :], w.lo[:, k, 512 * n:512 * n + 512], False, False)
                        for n, b in enumerate(bs):
                            tk = mm(b.t[:, :], hl[:, k0 + k, :], w.hi[:, k, 512 * n:512 * n + 512], False, en,
                                    sig=(n == 1 and k == w.kb - 1))
                    w.done(tk)
                    k0 += w.kb
                t_hT[("read", e)] = tk
                ys = []
                for n, b in enumerate(bs):
                    b.free = split_to(y_hi[:, 512 * n:512 * n + 512], y_lo[:, 512 * n:512 * n + 512], b.t[:, :], tk, T_read, after)
                    ys.append(b.free)
                t_y[0] = ys
                s = e % 2
                t_T[e] = dve(lambda g: g.tensor_scalar(tsel[:, s, :], pbc[:, e, :], col[:, 0:1], None, ALU.is_equal),
                             t_pb[e // 2], t_pl, T_read[s], after)

            def scatter(e):
                s = e % 2
                for t in range(2):
                    for n in range(2):
                        o = Y[2 * t + n].t[:, :]
                        st = e == 0
                        mm(o, tsel[:, s, 128 * t:128 * t + 128], y_hi[:, 512 * n:512 * n + 512], st, False, t_T[e], t_y[0], y0)
                        tk = mm(o, tsel[:, s, 128 * t:128 * t + 128], y_lo[:, 512 * n:512 * n + 512], False, e == NEXP - 1,
                                sig=(n == 1))
                    yt[t] = tk
                T_read[s] = tk

            t_pick_ = {0: pick(0)}
            gather(0)
            for e in range(NEXP):
                if e + 1 < NEXP:
                    t_pick_[e + 1] = pick(e + 1)
                up(e)
                if e + 1 < NEXP:
                    gather(e + 1)
                turn(e)
                if e:
                    scatter(e - 1)
                down(e)
            scatter(NEXP - 1)
            return [yt[0], yt[1]]

        ty = experts(0, t_tok, t_tail)

        main = [pe, act, dve, pool, sp]
        kept = [b.free for b in W + Y]
        last = [(q.sem, q.count) for q in main[:4]] + [(s_raw[i][0], s_raw[i][1]) for i in range(NR)]
        pe, act, dve, pool, sp = [Queue(sem(n), n) for n in ("o_pe", "o_act", "o_dve", "o_pool", "o_sp")]
        over = [pe, act, dve, pool, sp]
        for q in over:
            q.wait(last)
        state["end"] = len(tiles)
        for _ in range(NR):
            load_tile()
        t_sum = []
        for t in range(2):
            for n in range(2):
                xa, b = x[:, t, 512 * n:512 * n + 512], Y[2 * t + n]
                t_sum.append(dve(lambda e, xa=xa, b=b: e.tensor_tensor(xa, xa, b.t[:, :], ALU.add), last))
                b.free = t_sum[-1]
        to = experts(128, last, last)
        for q in over:
            q.wait(to, [(z.sem, z.count) for z in (act, dve)])
        pe, act, dve, pool, sp = main
        for b, f in zip(W + Y, kept):
            b.free = f
        for q, o in zip(main, over):
            q.branch(o, flag[0:1, 1:2].bitcast(i32), t_flag)

        done, _, _ = layer_norm(ty, t_ax, False, gbv, t_gb, turn=False)
        ov = out[0].rearrange("(t p) d -> p t d", p=128)
        for t in range(2):
            t_out = sp.dma(ov[:, t, :], x[:, t, :], s_out, done[t])
        sp.wait(t_out)
        assert state["use"] == len(tiles)

        with nc.Block() as block:
            @block.sync
            def _(e):
                sp.emit(e)

            @block.scalar
            def _(e):
                act.emit(e)

            @block.vector
            def _(e):
                dve.emit(e)

            @block.gpsimd
            def _(e):
                pool.emit(e)

            @block.tensor
            def _(e):
                pe.emit(e)


def feature_major(a):
    a = np.asarray(a)
    n = a.shape[-1] // 128
    a = a.reshape(-1, n, 128).transpose(2, 1, 0)
    return a.reshape(128, -1)


def token_major_T(a):
    tok, f = a.shape
    return np.ascontiguousarray(a.T.reshape(f // 128, 128, tok).transpose(1, 0, 2).reshape(128, -1))


def lay_out(inputs):
    a = {k: np.asarray(v) for k, v in inputs.items()}
    parts = []
    for name, idx, k0, k1, n0, n1 in weight_tiles():
        w = a[name][idx] if idx else a[name]
        w = w[128 * k0:128 * k1, n0:n1].reshape(k1 - k0, 128, n1 - n0).transpose(1, 0, 2)
        parts.append(w.reshape(-1))
    ws = np.concatenate(parts)

    par = np.zeros((128, NPAR), np.float32)

    def put(name, v):
        lo, hi = POFF[name]
        par[:v.shape[0], lo:hi] = v.reshape(v.shape[0], -1)

    put("conv_w", feature_major(a["conv_w"][0]))
    put("qkconv", a["qk_conv_w"][0].reshape(4, 16, 96).transpose(2, 1, 0))
    put("conv_dw", feature_major(a["conv_dw_2"][0]))
    put("conv_b", feature_major(a["conv_b_2"][0]))
    put("conv_g", feature_major(a["conv_ln_g_2"][0]))
    put("conv_lb", feature_major(a["conv_ln_b_2"][0]))
    put("b_gate", np.ascontiguousarray(a["b_gate_2"][0].reshape(24, 128).T))
    put("pool_scale", feature_major(a["pool_scale_2"][0]))
    put("q_g", feature_major(a["q_norm_g_2"][0]))
    put("kv_g", feature_major(a["kv_norm_g_2"][0]))
    put("pool_w", np.ascontiguousarray(a["pool_w_2"][0].transpose(1, 0, 2)))
    put("ident", np.eye(128, dtype=np.float32))
    mask = np.zeros((128, 384), np.float32)
    mask[0:64, 64:128] = -1e30
    mask[0:64, 128 + 192:384] = -1e30
    put("mask", mask)
    cnt = np.zeros((128, 4, 16), np.float32)
    for g in range(4):
        cnt[:, g, :] = 1.0 / np.minimum(np.arange(16) + 1, 2 << g)
    put("cnt", cnt)
    invf = np.power(np.float32(10000.0), -np.arange(0, 32, 2, dtype=np.float32) / np.float32(32))
    put("invf", np.tile(invf.astype(np.float32), (128, 1)))

    g = [a["ln_g"][l, j] for l in range(2) for j in range(3)] + [a["ln_in_g_2"], a["ln1_g_2"][0], a["ln2_g_2"][0]]
    b = [a["ln_b"][l, j] for l in range(2) for j in range(3)] + [a["ln_in_b_2"], a["ln1_b_2"][0], a["ln2_b_2"][0]]
    ln = np.stack([np.concatenate([p, q]) for p, q in zip(g, b)])
    rows = np.concatenate([a["b_gates"][0], a["router_bias_2"], a["head_norm_g"][0].reshape(-1)])[None, :]
    return {"ws": ws, "par": par, "ln": ln, "rows": np.ascontiguousarray(rows), "x": a["x"], "xT": token_major_T(a["x"][0]),
            "memT": token_major_T(a["mem"][0]), "pT": token_major_T(a["p_2"][0, 0]), "pos": a["positions_2"].reshape(2, 128).T}


def kernel(**inputs):
    import concourse.bacc as _bacc
    from concourse.bass_utils import run_bass_kernel_spmd as _run

    nc = _bacc.Bacc("TRN2", target_bir_lowering=False, num_devices=1)
    arrays, aps = {}, {}
    for name, a in lay_out(inputs).items():
        a = np.ascontiguousarray(a)
        arrays[f"in_{name}"] = a
        aps[name] = nc.dram_tensor(f"in_{name}", a.shape, mybir.dt.from_np(a.dtype), kind="ExternalInput").ap()
    out = nc.dram_tensor("out_0", (1, T, D), mybir.dt.float32, kind="ExternalOutput").ap()
    program(nc, aps, out)
    res = _run(nc, [arrays], core_ids=[0])
    return res.results[0]["out_0"]
```

```python
import math
from contextlib import ExitStack

import numpy as np

import concourse.bass as bass
from concourse import mybir
from concourse.alu_op_type import AluOpType as ALU

D = 1024
T = 256
FF = 2816
NEXP = 16
NG = 4
ALPHA1 = 4.0 ** 0.25
ALPHA2 = 2.0 ** 0.25
LN_EPS = 1e-5
RMS_EPS = 1e-6
TILE = 2048
PI = math.pi
MIX_ORDER = (6, 0, 2, 4)


def weight_tiles():
    tiles = []

    def ffn(gate, up, down, gi, ui, di, chunks, up0, late=None):
        for c in range(chunks):
            tiles.append((gate, gi(c), 0, 8, *up0(0, c)))
            tiles.append((up, ui(c), 0, 8, *up0(1, c)))
            if c:
                tiles.append((down, di(c - 1), *late(c - 1), 0, D))
        tiles.append((down, di(chunks - 1), *late(chunks - 1), 0, D))

    def first_ffn(l, s):
        i = (l, s)
        ffn("ffn_w_gate", "ffn_w_up", "ffn_w_down", lambda c: i, lambda c: i, lambda c: i, FF // 256,
            lambda part, c: (256 * c, 256 * c + 256), lambda c: (2 * c, 2 * c + 2))

    def rows(name, idx, blocks, n0, n1, step=2):
        for k in range(0, blocks, step):
            tiles.append((name, idx, k, k + step, n0, n1))

    def mixed(l):
        for k in MIX_ORDER:
            tiles.append(("w_out", (l,), k, k + 2, 0, D))

    def memory(l, part):
        tiles.append(("w_kv_mem", (l,), 0, 8, 256 * part, 256 * part + 256))

    first_ffn(0, 0)
    memory(0, 0)
    memory(0, 1)
    tiles.append(("w_in_conv", (0,), 0, 8, 2304, 2560))
    for j in range(3):
        for part in (1, 2, 0):
            n = 768 * part + 256 * j
            tiles.append(("w_in_conv", (0,), 0, 8, n, n + 256))
    mixed(0)
    first_ffn(0, 1)
    memory(1, 0)
    first_ffn(1, 0)
    memory(1, 1)
    tiles.append(("w_in_mlstm", (0,), 0, 8, 3072, 3080))
    tiles.append(("w_in_mlstm", (0,), 0, 8, 3080, 3336))
    rows("w_in_mlstm", (0,), 8, 1536, 2304)
    for h in range(4):
        for part in range(2):
            n = 768 * part + 192 * h
            tiles.append(("w_in_mlstm", (0,), 0, 8, n, n + 192))
    rows("w_in_mlstm", (0,), 8, 2304, 3072)
    mixed(1)
    first_ffn(1, 1)

    rows("w_in_2", (0,), 8, 1536, 2208)
    for j in range(2):
        tiles.append(("w_in_2", (0,), 0, 8, 256 * j, 256 * j + 256))
    for j in range(2):
        for part in range(2):
            n = 512 + 512 * part + 256 * j
            tiles.append(("w_in_2", (0,), 0, 8, n, n + 256))
    tiles.append(("w_uq_2", (0,), 0, 3, 0, 512))
    tiles.append(("w_uq_2", (0,), 0, 3, 512, 768))
    tiles.append(("w_ukv_2", (0,), 0, 2, 0, D))

    def gates(b):
        for j in range(4):
            n = 2208 + 1024 * b + 256 * j
            tiles.append(("w_in_2", (0,), 0, 8, n, n + 256))

    def proj(name):
        for j in range(2):
            tiles.append((name, (0,), 0, 4, 512 * j, 512 * j + 512))

    gates(0)
    proj("pool_proj_2")
    gates(1)
    gates(2)
    proj("mla_proj_2")
    proj("conv_proj_2")
    rows("w_out_2", (0,), 8, 0, D)
    tiles.append(("ple_proj_2", (0,), 0, 2, 0, D))
    tiles.append(("w_router_2", (), 0, 8, 0, NEXP))
    rows("ple_gate_2", (0,), 8, 0, D)
    for e in range(NEXP + 1):
        if e < NEXP:
            rows("exp_w_up_2", (0, e), 8, 0, D)
        if e:
            for n in range(2):
                tiles.append(("exp_w_down_2", (0, e - 1), 0, 4, 512 * n, 512 * n + 512))
    return tiles


def tile_width(t):
    return (t[3] - t[2]) * (t[5] - t[4])


PARAMS = [("conv_w", 18), ("qkconv", 64), ("conv_dw", 124), ("conv_b", 4), ("conv_g", 4), ("conv_lb", 4),
          ("b_gate", 24), ("pool_scale", 4), ("q_g", 3), ("kv_g", 2), ("pool_w", 512),
          ("ident", 128), ("mask", 384), ("cnt", 64), ("invf", 16), ("b_gates", 2)]
POFF = {}
_o = 0
for _n, _w in PARAMS:
    POFF[_n] = (_o, _o + _w)
    _o += _w
NPAR = _o
ROWS = 8 + 16 + 768


class Queue:

    def __init__(self, sem, name):
        self.sem, self.name, self.count, self.items = sem, name, 0, []

    def __call__(self, fn, *after, sig=True):
        self.count += 1 if sig else 0
        self.items.append((flat(after), fn, (self.sem, 1) if sig else None))
        return (self.sem, self.count)

    def dma(self, out, in_, sem, *after):
        sem[1] += 16
        self.items.append((flat(after), lambda e: e.dma_start(out, in_), (sem[0], 16)))
        return (sem[0], sem[1])

    def wait(self, *after):
        self.items.append((flat(after), None, None))

    def branch(self, other, flag, after):
        self.items.append(([after], None, (other, flag)))

    def emit(self, eng):
        seen = {}
        for after, fn, inc in self.items:
            for sem, value in after:
                if seen.get(id(sem), 0) < value:
                    eng.wait_ge(sem, value)
                    seen[id(sem)] = value
            if fn is None and inc is not None:
                other, flag = inc
                reg = eng.alloc_register("flag_" + other.name)
                eng.reg_load(reg, flag)
                with eng.If_ne(reg, 0):
                    other.emit(eng)
            if fn is not None:
                ins = fn(eng)
                if inc is not None:
                    ins.then_inc(*inc)


def flat(after):
    out = []
    for a in after:
        if a is None:
            continue
        if isinstance(a, dict):
            out += flat(list(a.values()))
        elif isinstance(a, list):
            out += flat(a)
        else:
            out.append(a)
    return out


def at(after, k):
    return [a[k // 4] if isinstance(a, dict) else a for a in after]


class Bank:

    def __init__(self, t):
        self.t, self.free = t, []


def program(nc, A, out):
    f32, f32r, i32 = mybir.dt.float32, mybir.dt.float32r, mybir.dt.int32
    ACT = mybir.ActivationFunctionType
    X = mybir.AxisListType.X
    NR, NS, LOOK = 4, 3, 2
    OPEN = 0

    ctx = ExitStack()
    with ctx:
        def sb(name, shape, dt=f32):
            return ctx.enter_context(nc.sbuf_tensor(name, shape, dt))

        def sem(name):
            return ctx.enter_context(nc.semaphore(name))

        raw = [sb(f"raw{i}", [128, TILE]) for i in range(NR)]
        whi = [sb(f"whi{i}", [128, TILE], f32r) for i in range(NS)]
        wlo = [sb(f"wlo{i}", [128, TILE], f32r) for i in range(NS)]
        x = sb("x", [128, 2, D])
        r = sb("r", [128, 2, D])
        xhi = sb("xhi", [128, 8, T], f32r)
        xlo = sb("xlo", [128, 8, T], f32r)
        mhi = sb("mhi", [128, 8, T], f32r)
        mlo = sb("mlo", [128, 8, T], f32r)
        hf = sb("hf", [128, 2, 2, T])
        hhi = sb("hhi", [128, 2, 2, T], f32r)
        hlo = sb("hlo", [128, 2, 2, T], f32r)
        gb = sb("gb", [128, 2, D])
        par = sb("par", [128, NPAR])
        brow = sb("brow", [128, 24])
        kT = sb("kT", [128, 2, 2, T])
        vm = sb("vm", [128, 2, 2, T])
        stat = sb("stat", [128, 2, 12])
        mv = sb("mv", [128, 2, 2])
        ve = sb("ve", [128, 2])
        rstd = sb("rstd", [128, 2])
        mhalf = sb("mhalf", [128, 8])
        posi = sb("posi", [128, 2], i32)
        cs = sb("cs", [128, 2, 2, 16])
        gsel = sb("gsel", [128, 2, T], f32r)
        tsel = sb("tsel", [128, 2, T], f32r)
        AR = 10500
        ar = sb("ar", [128, AR])
        W = [Bank(ctx.enter_context(nc.psum_tensor(f"psw{i}", [128, 512], f32))) for i in range(4)]
        Y = [Bank(ctx.enter_context(nc.psum_tensor(f"psy{i}", [128, 512], f32))) for i in range(4)]

        pe, act, dve, pool, sp = [Queue(sem(n), n) for n in ("s_pe", "s_act", "s_dve", "s_pool", "s_sp")]
        s_raw = [[sem(f"s_raw{i}"), 0] for i in range(NR + 2)]
        s_par, s_brow, s_pos, s_x, s_xT, s_mem, s_p = [[sem(n), 0] for n in
                                                        ("s_par", "s_brow", "s_pos", "s_x", "s_xT", "s_mem", "s_p")]
        s_gb, s_gbin, s_hn, s_out, s_xT2, s_half = [[sem(n), 0] for n in ("s_gb", "s_gbin", "s_hn", "s_out", "s_xT2", "s_half")]

        def P(name, a=0, b=None):
            lo, hi = POFF[name]
            return par[:, lo + a:(hi if b is None else lo + b)]

        ident = P("ident")

        class Arena:
            def __init__(self):
                self.at = 0

            def take(self, n):
                self.at += n
                assert self.at <= AR, self.at
                return ar[:, self.at - n:self.at]

        def blocks(ap, n):
            return ap.rearrange("p (b n) -> p b n", n=n)

        tiles = weight_tiles()
        offs = [0]
        for t in tiles:
            offs.append(offs[-1] + 128 * tile_width(t))
        main_tiles = len(tiles)
        expert0 = next(i for i, t in enumerate(tiles) if t[0] == "exp_w_up_2")
        offs = offs[:-1] + offs[expert0:-1]
        tiles = tiles + tiles[expert0:]
        ready = [None] * len(tiles)
        used = [None] * len(tiles)
        raw_in = [None] * len(tiles)
        state = {"load": 0, "split": 0, "use": 0, "w": 0, "end": main_tiles}

        raw_free = [(raw[i][:, :], s_raw[i], None) for i in range(NR)]
        raw_at = [None] * len(tiles)

        def load_tile():
            i = state["load"]
            if i >= state["end"]:
                return
            w = tile_width(tiles[i])
            src = A["ws"][offs[i]:offs[i] + 128 * w].rearrange("(p c) -> p c", c=w)
            raw_at[i], s_in, free = raw_free.pop(0)
            halves = [0, w // 2, w] if i == 0 else [0, w]
            raw_in[i] = []
            for n, (c0, c1) in enumerate(zip(halves, halves[1:])):
                if i == 0:
                    t_xT.append(sp.dma(xTr[:, 4 * n:4 * n + 4, :], blocks(A["xT"][:, :], T)[:, 4 * n:4 * n + 4, :], (s_xT, s_xT2)[n]))
                raw_in[i].append(sp.dma(raw_at[i][:, c0:c1], src[:, c0:c1], s_in if n == 0 else s_half, free))
            raw_at[i] = (raw_at[i], s_in)
            state["load"] += 1

        def split_tile():
            i = state["split"]
            if i >= state["end"]:
                return
            t = tiles[i]
            w = tile_width(t)
            kb = t[3] - t[2]
            free = used[i - NS] if i >= NS else None
            assert i < NS or free is not None
            cuts = [0, kb // 2, kb] if w > 512 and kb > 1 else [0, kb]
            ready[i] = []
            for n, (k0, k1) in enumerate(zip(cuts, cuts[1:])):
                c0, c1 = k0 * (w // kb), k1 * (w // kb)
                src, hi, lo = raw_at[i][0][:, c0:c1], whi[i % NS][:, c0:c1], wlo[i % NS][:, c0:c1]
                h = act(lambda e, hi=hi, src=src: e.activation(hi, src, ACT.Copy), raw_in[i][min(n, len(raw_in[i]) - 1)], free)
                l = dve(lambda e, hi=hi, lo=lo, src=src: e.tensor_tensor(lo, src, hi.bitcast(f32), ALU.subtract), h, free)
                ready[i] += [(k1, [h, l])]
            raw_free.append((*raw_at[i], l))
            state["split"] += 1
            load_tile()

        def ahead(look=LOOK):
            while state["split"] < min(state["use"] + look, state["end"]):
                split_tile()

        class Tile:

            def __init__(self, name, n0=None, look=LOOK):
                self.i = i = state["use"]
                t = tiles[i]
                assert t[0] == name and (n0 is None or t[4] == n0), (t, name, n0)
                while state["split"] <= min(i + look, state["end"] - 1):
                    split_tile()
                state["use"] += 1
                self.kb, self.k0, self.n = t[3] - t[2], t[2], t[5] - t[4]
                w = tile_width(t)
                self.hi = blocks(whi[i % NS][:, 0:w], self.n)
                self.lo = blocks(wlo[i % NS][:, 0:w], self.n)
                self.parts = ready[i]

            def ready(self, k):
                return next(t for k1, t in self.parts if k < k1)

            def done(self, ticket):
                used[self.i] = ticket

        def bank():
            state["w"] += 1
            return W[(state["w"] - 1) % 4]

        def mm(o, l, rr, start, stop, *after, sig=False):
            return pe(lambda e: e.matmul(o, l, rr, start=start, stop=stop), *after, sig=sig)

        def tr(o, i, n, *after, sig=False):
            return pe(lambda e: e.transpose(o, i, ident[0:n, 0:n]), *after, sig=sig)

        def cols(o, w, c0, m, hi, lo, *after):
            for k in range(w.kb):
                wh, wl = w.hi[:, k, c0:c0 + m], w.lo[:, k, c0:c0 + m]
                mm(o, wh, hi[:, k, :], k == 0, False, w.ready(k), at(after, k))
                mm(o, wh, lo[:, k, :], False, False)
                tick = mm(o, wl, hi[:, k, :], False, k == w.kb - 1, sig=(k == w.kb - 1))
            return tick

        def pair(w, hi, lo, *after, m=128):
            b = bank()
            for j in range(w.n // m):
                tick = cols(b.t[0:m, 256 * j:256 * j + 256], w, m * j, m, hi, lo, b.free, *after)
            b.free = None
            w.done(tick)
            return b, tick

        def rows_of(w, t, hi, lo, k0, mine, first, last, *after):
            ticks = []
            for outs in ([[o] for o in mine] if last else [mine]):
                for k in range(w.kb):
                    lh, ll = hi[:, k0 + k, 128 * t:128 * t + 128], lo[:, k0 + k, 128 * t:128 * t + 128]
                    st = first and k == 0
                    en = last and k == w.kb - 1
                    for o, c0, c1 in outs:
                        mm(o, lh, w.hi[:, k, c0:c1], st, False, w.ready(k), at(after, k0 + k))
                    for o, c0, c1 in outs:
                        mm(o, lh, w.lo[:, k, c0:c1], False, False)
                    for n, (o, c0, c1) in enumerate(outs):
                        tick = mm(o, ll, w.hi[:, k, c0:c1], False, en, sig=(k == w.kb - 1 and n == len(outs) - 1))
                ticks.append(tick)
            if last:
                yt[t] = ticks
            return tick

        def rowsof(w, hi, lo, k0, outs, first, last, *after):
            for t in range(2):
                tick = rows_of(w, t, hi, lo, k0, [o[1:] for o in outs if o[0] == t], first, last, *after)
            w.done(tick)
            return tick

        yt = [None, None]

        def big_rows(name, ntile, hi, lo, *after, n=D, splits=((0, 512), (512, 1024)), n0=None, each=None, hook={}, tail=False, opened=None):
            free = [b.free for b in Y]
            outs = [[(Y[2 * t + i].t[:, 0:c1 - c0], c0, c1) for i, (c0, c1) in enumerate(splits)] for t in range(2)]
            groups = [[j] for j in range(ntile)]
            if opened:
                groups = [[0, 1]] + groups[2:]
            if tail:
                groups = groups[:-2] + [[ntile - 2, ntile - 1]]
            for group in groups:
                begun = opened and group[0] == 0
                ws = opened if begun else [Tile(name, n0, look=LOOK - i) for i in range(len(group))]
                for t in range(1 if begun else 0, 2):
                    for j, w in zip(group, ws):
                        tk = rows_of(w, t, hi, lo, w.k0, outs[t], j == 0, j == ntile - 1, *(list(after) + free + (each[j] if each else [])))
                        if t:
                            w.done(tk)
                for j in group:
                    if j in hook:
                        hook[j]()
            return [yt[0], yt[1]]

        def rows_opening(name, hi, lo, splits):
            ws = []

            def tiles_():
                ws.extend([Tile(name, look=1), Tile(name, look=OPEN)])

            def first(xt):
                for j, w in enumerate(ws):
                    rows_of(w, 0, hi, lo, w.k0, [(Y[i].t[:, 0:c1 - c0], c0, c1) for i, (c0, c1) in enumerate(splits)], j == 0, False,
                            xt, Y[0].free, Y[1].free)

            return ws, (tiles_, first)

        def split_to(hi, lo, src, *after, scale=1.0):
            a = act(lambda e: e.activation(hi, src, ACT.Copy, scale=scale), *after)
            if isinstance(scale, float):
                d = dve(lambda e: e.tensor_tensor(lo, src, hi.bitcast(f32), ALU.subtract), a)
            else:
                d = dve(lambda e: e.scalar_tensor_tensor(out=lo, in0=src, scalar=scale, in1=hi.bitcast(f32),
                                                         op0=ALU.mult, op1=ALU.subtract), a)
            return [a, d]

        first = Arena()
        memT = blocks(first.take(8 * T), T)
        xTr = blocks(first.take(8 * T), T)
        t_xT = []
        for _ in range(NR):
            load_tile()
        t_par = sp.dma(par[:, :], A["par"][:, :], s_par)
        t_pos = sp.dma(posi[:, :], A["pos"][:, :], s_pos)
        t_x = sp.dma(x[:, :, :], A["x"][0].rearrange("(t p) d -> p t d", p=128), s_x)
        t_brow = sp.dma(brow[:, :], A["rows"][:, 0:24].broadcast_to((128, 24)), s_brow)
        t_mem = sp.dma(memT, blocks(A["memT"][:, :], T), s_mem)
        t_gb = pool.dma(gb[:, :, :].rearrange("p a d -> p (a d)"), A["ln"][0:1, :].broadcast_to((128, 2 * D)), s_gb, raw_in[3])
        t_mhalf = pool(lambda e: e.memset(mhalf[:, :], -0.5))
        xt_ready = {}
        for q in range(2):
            xt_ready[q] = split_to(xhi[:, 4 * q:4 * q + 4, :], xlo[:, 4 * q:4 * q + 4, :], xTr[:, 4 * q:4 * q + 4, :], t_xT[q])
            if q == 0:
                split_tile()

        kv_ready = {}

        def memory_keys(l, t_m):
            b, tk = pair(Tile("w_kv_mem", 0, look=1), mhi, mlo, t_m)
            o = kT[:, l, :, :].rearrange("p b n -> p (b n)")
            b.free = act(lambda e: e.activation(o, b.t[:, :], ACT.Copy), tk)
            kv_ready[l] = [b.free]

        def memory_values(l, t_m):
            w = Tile("w_kv_mem", 256, look=1)
            b = bank()
            tk = rowsof(w, mhi, mlo, 0, [(t, b.t[:, 256 * t:256 * t + 256], 0, 256) for t in range(2)], True, True, b.free, t_m)
            o = vm[:, l, :, :].rearrange("p b n -> p (b n)")
            b.free = act(lambda e: e.activation(o, b.t[:, :], ACT.Copy), tk)
            kv_ready[l].append(b.free)

        cw = first.take(2 * 16 * 4).rearrange("p (s t n) -> p s t n", s=4, t=2)
        posf = first.take(2)
        cosA = cs[:, 0, :, :]
        sinA = cs[:, 1, :, :]

        def rotary():
            ang, kk, rr, ab = [cw[:, i, :, :] for i in range(4)]
            tk = dve(lambda e: e.tensor_copy(posf, posi[:, :]), t_pos)
            for t in range(2):
                a1 = dve(lambda e, t=t: e.tensor_scalar(ang[:, t, :], P("invf"), posf[:, t:t + 1], None, ALU.mult), tk, t_par)
            MAGIC = 1.5 * 2.0 ** 23
            a2 = dve(lambda e: e.tensor_scalar(kk, ang, 1.0 / (2 * PI), MAGIC, ALU.mult, ALU.add), a1)
            a2 = dve(lambda e: e.tensor_scalar(kk, kk, MAGIC, None, ALU.subtract), a2)
            C1 = 6.28125
            C2 = float(np.float32(np.round((2 * PI - C1) * 2.0 ** 21) / 2.0 ** 21))
            C3 = float(2 * PI - C1 - C2)
            src = ang
            for c in (C1, C2, C3):
                a2 = dve(lambda e, c=c, src=src: e.scalar_tensor_tensor(out=rr, in0=kk, scalar=-c, in1=src,
                                                                        op0=ALU.mult, op1=ALU.add), a2)
                src = rr
            a2 = dve(lambda e: e.tensor_scalar(rr, rr, 3.1415925, -3.1415925, ALU.min, ALU.max), a2)
            a3 = dve(lambda e: e.scalar_tensor_tensor(out=ab, in0=rr, scalar=-1.0, in1=rr, op0=ALU.mult, op1=ALU.min), a2)
            a3 = dve(lambda e: e.tensor_scalar(ab, ab, PI / 2, None, ALU.add), a3)
            act(lambda e: e.activation(sinA, rr, ACT.Sin), a2)
            t_cs = act(lambda e: e.activation(cosA, ab, ACT.Sin), a3)
            return t_cs

        def scale_x(alpha, *after):
            return [pool(lambda e, t=t: e.tensor_scalar(x[:, t, :], x[:, t, :], alpha, None, ALU.mult), *after)
                    for t in range(2)]

        def ffn_opening(gate, up):
            st = {"b": []}

            def half(t, xt):
                b = bank()
                for i, w in enumerate(st["w"]):
                    tk = rows_of(w, t, xhi, xlo, 0, [(b.t[:, 256 * i:256 * i + 256], 0, 256)], True, True, xt, b.free)
                    if t:
                        w.done(tk)
                st["b"].append((b, tk))

            def tiles_():
                st["w"] = [Tile(gate, look=1), Tile(up, look=OPEN)]

            def first(xt):
                half(0, xt)

            def second(xt):
                half(1, xt)
                st["h"] = []
                for t, (b, tk) in enumerate(st["b"]):
                    t1 = act(lambda e, t=t, b=b: e.activation(hf[:, 0, t, :], b.t[:, 0:256], ACT.Silu), tk)
                    t2 = dve(lambda e, t=t, b=b: e.tensor_tensor(hf[:, 0, t, :], hf[:, 0, t, :], b.t[:, 256:512], ALU.mult), t1)
                    b.free = t2
                    st["h"].append(t2)

            def turn():
                b = bank()
                for f in range(2):
                    for t in range(2):
                        tk = tr(b.t[:, 256 * f + 128 * t:256 * f + 128 * t + 128], hf[:, 0, t, 128 * f:128 * f + 128], 128, st["h"],
                                b.free, sig=(f == 1 and t == 1))
                b.free = split_to(hhi[:, 0, :, :], hlo[:, 0, :, :], blocks(b.t[:, :], 256), tk)
                return b.free

            return (tiles_, first), second, turn

        def ffn(gate, up, down, chunks, *after, between={}, opened=None):
            h_read = [None, None]
            pend = []
            y0 = [b.free for b in Y]

            def outs(t):
                return [(Y[2 * t + i].t[:, :], 512 * i, 512 * i + 512) for i in range(2)]

            def down_chunk():
                c, ready = pend.pop(0)
                w = Tile(down)
                s = c % 2
                for t in range(2):
                    tk = rows_of(w, t, hhi[:, s, :, :], hlo[:, s, :, :], 0, outs(t), c == 0, False, ready, y0)
                w.done(tk)
                h_read[s] = tk

            def last_chunks():
                ws = [Tile(down), Tile(down, look=1)]
                for t in range(2):
                    for w, (c, ready) in zip(ws, pend):
                        s = c % 2
                        tk = rows_of(w, t, hhi[:, s, :, :], hlo[:, s, :, :], 0, outs(t), False, c == chunks - 1, ready)
                        if t:
                            w.done(tk)

            for c in range(chunks):
                s = c % 2
                if opened and c == 0:
                    opened[1](*after)
                    continue
                wg = Tile(gate)
                bg, tg = pair(wg, xhi, xlo, *after)
                if opened and c == 1:
                    pend.append((0, opened[2]()))
                wu = Tile(up)
                bu, tu = pair(wu, xhi, xlo, *after)
                hs = hf[:, s, :, :].rearrange("p b n -> p (b n)")
                hh, hl = [q[:, s, :, :].rearrange("p b n -> p (b n)") for q in (hhi, hlo)]
                t1 = act(lambda e, hs=hs, bg=bg: e.activation(hs, bg.t[:, :], ACT.Silu), tg)
                t2 = dve(lambda e, hs=hs, bu=bu: e.tensor_tensor(hs, hs, bu.t[:, :], ALU.mult), t1, tu)
                bg.free, bu.free = t1, t2
                if c in between:
                    between[c]()
                if 0 < c < chunks - 1:
                    down_chunk()
                pend.append((c, split_to(hh, hl, hs, t2, h_read[s])))
            last_chunks()
            return [yt[0], yt[1]]

        def half_of(z, t, h):
            return z[:, t, 512 * h:512 * h + 512]

        def norm_parts(ticks, t_ax, half, gbt, t_g, dst=x):
            g, bb = gbt[:, 0:D], gbt[:, D:2 * D]

            def add(t, h):
                o, y = half_of(r, t, h), Y[2 * t + h]
                q = t_ax[t]
                if ticks is not None:
                    xa = half_of(x, t, h)
                    if half:
                        q = dve(lambda e: e.scalar_tensor_tensor(out=o, in0=y.t[:, :], scalar=0.5, in1=xa, op0=ALU.mult, op1=ALU.add),
                                ticks[t][h], q)
                    else:
                        q = dve(lambda e: e.tensor_tensor(o, y.t[:, :], xa, ALU.add), ticks[t][h], q)
                    y.free = q
                return dve(lambda e: e.bn_stats(stat[:, t, 6 * h:6 * h + 6], o), q)

            def spread_of(t, s1):
                s2 = dve(lambda e: e.bn_aggr(mv[:, t, :], stat[:, t, :]), s1)
                s3 = dve(lambda e: e.tensor_scalar(ve[:, t:t + 1], mv[:, t, 1:2], LN_EPS, None, ALU.add), s2)
                return pool(lambda e: e.tensor_tensor(rstd[:, t:t + 1], ve[:, t:t + 1], mhalf[:, 0:1], ALU.pow), s3, t_mhalf)

            def stats(t, between=None):
                s1 = add(t, 0)
                if between:
                    between()
                return spread_of(t, [s1, add(t, 1)])

            def norm(t, rs, between=None):
                out_ = []
                for h in range(2):
                    if h and between:
                        between()
                    o, src, d = half_of(x, t, h), half_of(r, t, h), half_of(dst, t, h)
                    gh, bh = g[:, 512 * h:512 * h + 512], bb[:, 512 * h:512 * h + 512]
                    n1 = dve(lambda e, o=o, src=src, gh=gh: e.scalar_tensor_tensor(
                        out=o, in0=src, scalar=mv[:, t, 0:1], in1=gh, op0=ALU.subtract, op1=ALU.mult), rs, t_g)
                    out_.append(dve(lambda e, o=o, d=d, bh=bh: e.scalar_tensor_tensor(
                        out=d, in0=o, scalar=rstd[:, t:t + 1], in1=bh, op0=ALU.mult, op1=ALU.add), n1))
                return out_

            return add, spread_of, stats, norm

        def layer_norm(ticks, t_ax, half, gbt, t_g, alpha=None, fill=(), opening=None, before=None):
            xt, read = {0: [], 1: []}, []
            t_ax = list(t_ax)
            _, _, stats, norm = norm_parts(ticks, t_ax, half, gbt, t_g)

            def turned(t, n):
                bs = []
                for q in range(2):
                    b = bank()
                    for k in range(4):
                        kb = 4 * q + k
                        tk = tr(b.t[:, 128 * k:128 * k + 128], x[:, t, 128 * kb:128 * kb + 128], 128, n[q], b.free,
                                sig=(k == 3))
                    bs.append((q, (b, tk)))
                read.append(tk)
                return bs

            def parts(t, bs):
                for q, (b, tk) in bs:
                    o = [z[:, 4 * q:4 * q + 4, 128 * t:128 * t + 128] for z in (xhi, xlo)]
                    ev = split_to(o[0], o[1], blocks(b.t[:, :], 128), tk)
                    b.free = ev
                    xt[q].append(ev)

            if before:
                _, _, stats_, norm_ = before
                t_ax[0] = norm_(0, stats_(0))
                rs0 = stats(0)
                rs1 = stats_(1)
            else:
                rs0 = stats(0)
            n0 = norm(0, rs0)
            b0 = turned(0, n0)
            if before:
                t_ax[1] = norm_(1, rs1, lambda: parts(0, b0))
            if opening:
                rs1 = stats(1, None if before else lambda: parts(0, b0))
                for f in fill:
                    f()
                opening[0]()
            else:
                rs1 = stats(1)
                parts(0, b0[:1])
            n1 = norm(1, rs1)
            done = [n0[-1], n1[-1]]
            if not opening:
                parts(0, b0[1:])
                for f in fill:
                    f()
            else:
                opening[1](dict((q, list(ev)) for q, ev in xt.items()))
            parts(1, turned(1, n1))
            if opening:
                ahead(1)
            if alpha is None:
                return done, xt, read
            return done, xt, [pool(lambda e, t=t: e.tensor_scalar(x[:, t, :], x[:, t, :], alpha, None, ALU.mult), read[t])
                              for t in range(2)]

        def next_gb(k, *after):
            return pool.dma(gb[:, :, :].rearrange("p a d -> p (a d)"), A["ln"][k:k + 1, :].broadcast_to((128, 2 * D)), s_gb, *after)

        gbv = gb[:, :, :].rearrange("p a d -> p (a d)")

        def mem_attention(l, qT, t_q, pbuf, arena, *after):
            pT = [arena.take(2 * T).rearrange("p (m n) -> p m n", m=2) for _ in range(2)]
            ob = r[:, :, 768:1024]
            mx = arena.take(8)
            sm = arena.take(8)
            ri = arena.take(8)
            ex, t_pT, pv, t_o = [], {}, [None, None], [None]
            o_b = Y[0]

            def score(h):
                b = bank()
                s, blk = 64 * (h % 2), h // 2
                for t in range(2):
                    tk = mm(b.t[:, 256 * t:256 * t + 256], qT[s:s + 64, blk, 128 * t:128 * t + 128], kT[s:s + 64, l, blk, :],
                            True, True, t_q, kv_ready[l], b.free, sig=(t == 1))
                m2 = mx[:, 2 * h:2 * h + 2]
                t1 = dve(lambda e: e.tensor_reduce(m2, blocks(b.t[:, :], 256), X, ALU.max, negate=True), tk, list(after))
                t2 = dve(lambda e: e.tensor_scalar(m2, m2, 0.125, None, ALU.mult), t1)
                for t in range(2):
                    t3 = act(lambda e, t=t: e.activation(pbuf[:, h, t, :], b.t[:, 256 * t:256 * t + 256], ACT.Exp,
                                                         bias=mx[:, 2 * h + t:2 * h + t + 1], scale=0.125,
                                                         accum_out=sm[:, 2 * h + t:2 * h + t + 1]), t2, list(after))
                b.free = t3
                ex.append(t3)

            def turn(h):
                b = bank()
                for m in range(2):
                    for t in range(2):
                        tk = tr(b.t[:, 256 * m + 128 * t:256 * m + 128 * t + 128], pbuf[:, h, t, 128 * m:128 * m + 128], 128,
                                ex[h], b.free, sig=(m == 1 and t == 1))
                p2 = pT[h % 2]
                b.free = t_pT[h] = act(lambda e: e.activation(p2.rearrange("p m n -> p (m n)"), b.t[:, :], ACT.Copy), tk, pv[h % 2],
                                       list(after))

            def value(h):
                p2 = pT[h % 2]
                for t in range(2):
                    for m in range(2):
                        c = 256 * t + 64 * h
                        pv[h % 2] = mm(o_b.t[:, c:c + 64], p2[:, m, 128 * t:128 * t + 128], vm[:, l, m, 64 * h:64 * h + 64],
                                       m == 0, m == 1, t_pT[h], o_b.free, sig=(t == 1 and m == 1))

            def scale():
                t_r = dve(lambda e: e.reciprocal(ri, sm), ex[-1])
                for t in range(2):
                    rv = ri.rearrange("p (h t) -> p t h", t=2)[:, t, :].unsqueeze(2).to_broadcast([128, 4, 64])
                    t_o[0] = dve(lambda e, t=t, rv=rv: e.tensor_tensor(ob[:, t, :].rearrange("p (h n) -> p h n", n=64),
                                                                       o_b.t[:, 256 * t:256 * t + 256].rearrange("p (h n) -> p h n", n=64),
                                                                       rv, ALU.mult), pv[1], t_r, list(after))
                o_b.free = t_o[0]

            def finish():
                b = bank()
                for k in range(2):
                    for t in range(2):
                        tk = tr(b.t[:, 256 * k + 128 * t:256 * k + 128 * t + 128], ob[:, t, 128 * k:128 * k + 128], 128, t_o[0], b.free,
                                sig=(k == 1 and t == 1))
                b.free = split_to(mhi[:, 6:8, :], mlo[:, 6:8, :], blocks(b.t[:, :], 256), tk)
                return b.free

            return score, turn, value, scale, finish

        def prob_buffer(z):
            return z.rearrange("p (h t n) -> p h t n", h=4, t=2)

        def xa_queries(name, n0, qT, *after):
            w = Tile(name, n0)
            b, tk = pair(w, xhi, xlo, *after)
            b.free = act(lambda e: e.activation(qT.rearrange("p b n -> p (b n)"), b.t[:, :], ACT.Copy), tk)
            return b.free

        def conv_mixer(t_xt, t_prev):
            arena = Arena()
            qT = arena.take(2 * T).rearrange("p (b n) -> p b n", b=2)
            t_q = xa_queries("w_in_conv", 2304, qT, t_xt)
            cb = arena.take(2 * T)
            z = [arena.take(2 * 258).rearrange("p (b n) -> p b n", b=2) for _ in range(2)]
            acc = [arena.take(2 * T).rearrange("p (b n) -> p b n", b=2) for _ in range(2)]
            cwt = P("conv_w").rearrange("p (b w) -> p b w", w=3)
            zz = [pool(lambda e, q=q: e.memset(z[q][:, :, 0:2], 0.0), t_q) for q in range(2)]
            done = []
            score, turn, value, scale, finish = mem_attention(0, qT, t_q, prob_buffer(arena.take(8 * T)), arena, t_prev)
            t_mem = []
            steps = [lambda: (score(0), score(1)), lambda: (score(2), score(3)), lambda: turn(0), lambda: (value(0), turn(1)),
                     lambda: (value(1), turn(2)), lambda: (value(2), turn(3)), lambda: (value(3), scale()),
                     lambda: t_mem.append(finish()), lambda: None]

            def part(j):
                q = j % 2
                bc, tc = pair(Tile("w_in_conv", 768 + 256 * j), xhi, xlo)
                t1 = act(lambda e: e.activation(cb, bc.t[:, :], ACT.Copy), tc, done[j - 1] if j else None)
                bc.free = t1
                steps.pop(0)()
                bx, tx = pair(Tile("w_in_conv", 1536 + 256 * j), xhi, xlo)
                t2 = dve(lambda e: e.tensor_tensor(z[q][:, :, 2:258], blocks(cb, 256), blocks(bx.t[:, :], 256), ALU.mult), t1, tx)
                bx.free = t2
                steps.pop(0)()
                t3 = [t2, t2]
                for f in range(2):
                    blk = 2 * j + f
                    t3[f] = dve(lambda e, f=f, blk=blk: e.tensor_scalar(acc[q][:, f, :], z[q][:, f, 2:258], cwt[:, blk, 2:3], None,
                                                                        ALU.mult), t2, zz[q])
                for s in range(2):
                    for f in range(2):
                        blk = 2 * j + f
                        t3[f] = dve(lambda e, f=f, blk=blk, s=s: e.scalar_tensor_tensor(
                            out=acc[q][:, f, :], in0=z[q][:, f, s:s + 256], scalar=cwt[:, blk, s:s + 1], in1=acc[q][:, f, :],
                            op0=ALU.mult, op1=ALU.add), t3[f])
                bb, tb = pair(Tile("w_in_conv", 256 * j), xhi, xlo)
                t4 = dve(lambda e: e.tensor_tensor(acc[q], acc[q], blocks(bb.t[:, :], 256), ALU.mult), t3, tb)
                bb.free = t4
                steps.pop(0)()
                done.append(split_to(mhi[:, 2 * j:2 * j + 2, :], mlo[:, 2 * j:2 * j + 2, :], acc[q], t4))

            for j in range(3):
                part(j)
            return t_mem + done

        def mlstm_mixer(t_xt, t_prev):
            arena = Arena()
            qT = arena.take(2 * T).rearrange("p (b n) -> p b n", b=2)
            hn = arena.take(768)
            t_hn = pool.dma(hn, A["rows"][:, 24:792].broadcast_to((128, 768)), s_hn, t_prev)
            sel = arena.take(512)[0:4].rearrange("p (h n) -> p h n", h=4)
            s0 = pool(lambda e: e.memset(sel, 0.0), t_prev)
            t_sel = pool(lambda e: e.affine_select(out=sel, in_=sel, compare_op=ALU.not_equal, fill=1.0, base=0,
                                                   pattern=[[-1, 4], [0, 128]], channel_multiplier=1), s0)
            w = Tile("w_in_mlstm", 3072)
            gbk = bank()
            for i in range(2):
                t1 = cols(gbk.t[0:4, 256 * i:256 * i + 256], w, 4 * i, 4, xhi, xlo, t_xt, gbk.free)
            w.done(t1)
            t_q = xa_queries("w_in_mlstm", 3080, qT)
            gs = arena.take(5 * T).rearrange("p (s n) -> p s n", s=5)[0:4]
            li, z, e1, AA, em = [gs[:, i, :] for i in range(5)]
            lf, B, aa = e1, z, li
            t_c = {}

            def decays():
                for i in range(2):
                    t2 = dve(lambda e, i=i: e.tensor_scalar(gs[:, i, :], gbk.t[0:4, 256 * i:256 * i + 256], P("b_gates", i, i + 1)[0:4], None,
                                                            ALU.add), t1, t_prev)
                gbk.free = t2
                t3 = dve(lambda e: e.scalar_tensor_tensor(out=e1, in0=z, scalar=-1.0, in1=z, op0=ALU.mult, op1=ALU.max), t2)
                t4 = act(lambda e: e.activation(e1, e1, ACT.Exp, scale=-1.0), t3)
                t4 = act(lambda e: e.activation(e1, e1, ACT.Ln, bias=1.0), t4)
                t5 = dve(lambda e: e.scalar_tensor_tensor(out=lf, in0=z, scalar=0.0, in1=e1, op0=ALU.min, op1=ALU.subtract), t4)
                one = em
                t6 = dve(lambda e: e.memset(one, 1.0))
                t6 = dve(lambda e: e.tensor_tensor_scan(B, one, lf, 0.0, ALU.mult, ALU.add), t5, t6)
                t7 = dve(lambda e: e.tensor_tensor(aa, li, B, ALU.subtract), t6)
                t_c[8] = dve(lambda e: e.tensor_tensor_scan(AA, aa, aa, 0.0, ALU.max, ALU.max), t7)
                t9 = dve(lambda e: e.tensor_tensor(em, AA, B, ALU.add), t_c[8])
                t_c[9] = act(lambda e: e.activation(em, em, ACT.Exp, scale=-1.0), t9)

            ac = arena.take(16).rearrange("p (t n) -> p t n", t=2)

            def decay_columns():
                b = bank()
                for t in range(2):
                    for i, s in enumerate((aa, em)):
                        tk = tr(b.t[:, 8 * t + 4 * i:8 * t + 4 * i + 4], s[:, 128 * t:128 * t + 128], 4, t_c[8], t_c[9], b.free,
                                sig=(t == 1 and i == 1))
                b.free = t_c[10] = dve(lambda e: e.tensor_copy(ac, blocks(b.t[:, 0:16], 8)), tk)

            wt = arena.take(4 * 384).rearrange("p (h n) -> p h n", h=4)
            t_wt = []

            def weights(h):
                b = bank()
                tk = mm(b.t[:, 0:256], sel[:, h, :], AA, True, True, t_c[8], t_sel, b.free, sig=True)
                a1 = act(lambda e: e.activation(wt[:, h, 0:256], b.t[:, 0:256], ACT.Exp, bias=ac[:, 0, h:h + 1],
                                                scale=-1.0), tk, t_c[10])
                a2 = act(lambda e: e.activation(wt[:, h, 256:384], b.t[:, 128:256], ACT.Exp, bias=ac[:, 1, h:h + 1],
                                                scale=-1.0), tk, t_c[10])
                b.free = a2
                for c in (0, 256):
                    a3 = pool(lambda e, c=c: e.affine_select(out=wt[:, h, c:c + 128], in_=wt[:, h, c:c + 128],
                                                             compare_op=ALU.is_ge, fill=0.0, base=0, pattern=[[1, 128]],
                                                             channel_multiplier=-1), a1, a2)
                t_wt.append(a3)

            va = arena.take(2 * 4 * 194).rearrange("p (t h n) -> p t h n", t=2, h=4)
            t_one = pool(lambda e: e.memset(va[:, :, :, 192:194], 1.0), t1)
            cwt = P("qkconv").rearrange("p (b w) -> p b w", w=4)
            zp = [arena.take(2 * 259).rearrange("p (b n) -> p b n", b=2)[0:96] for _ in range(2)]
            zz = [pool(lambda e, q=q: e.memset(zp[q][:, :, 0:3], 0.0), t1) for q in range(2)]
            qk = [[arena.take(2 * T).rearrange("p (b n) -> p b n", b=2)[0:96] for _ in range(2)], [hf[0:96, s, :, :] for s in range(2)]]
            sc = [arena.take(384) for _ in range(2)]
            score, turn, value, scale, finish = mem_attention(1, qT, t_q, prob_buffer(gbv), arena, t_prev)
            ty = big_rows("w_in_mlstm", 4, xhi, xlo, n=768, splits=((0, 384), (384, 768)), n0=1536,
                          hook={0: decays, 1: lambda: (score(0), score(1)), 2: lambda: (decay_columns(), score(2)), 3: lambda: score(3)})
            t_v = []
            for t in range(2):
                for i in range(2):
                    y = Y[2 * t + i]
                    y.free = act(lambda e, t=t, i=i, y=y: e.activation(va[:, t, 2 * i:2 * i + 2, 0:192],
                                                                       blocks(y.t[:, 0:384], 192), ACT.Copy), ty[t])
                    t_v.append(y.free)
            hb = r[:, :, 0:768].rearrange("p t (h n) -> p t h n", h=4)
            den = arena.take(16).rearrange("p (s h t) -> p s h t", s=2, h=4)
            hst = arena.take(2 * 4 * 6).rearrange("p (t h n) -> p t h n", t=2, h=4)
            hmv = arena.take(2 * 4 * 2).rearrange("p (t h n) -> p t h n", t=2, h=4)
            hve = arena.take(16).rearrange("p (s h t) -> p s h t", s=2, h=4)
            t_h, t_a = {}, {}
            t_ready = {}
            conv_read = [None, None]
            qk_read = [None, None]
            sc_read = [None, None]

            def head(h, part):
                b, tk = pair(Tile("w_in_mlstm", 768 * part + 192 * h), xhi, xlo, m=96)
                z_ = zp[part]
                q_ = qk[h % 2][part]
                c1 = act(lambda e: e.activation(z_[:, :, 3:259], blocks(b.t[0:96, :], 256), ACT.Copy), tk, conv_read[part])
                c2 = [None, None]
                for f in range(2):
                    blk = 8 * part + 2 * h + f
                    c2[f] = act(lambda e, f=f, blk=blk: e.activation(q_[:, f, :], b.t[0:96, 256 * f:256 * f + 256], ACT.Copy,
                                                                     scale=cwt[0:96, blk, 3:4]), tk, qk_read[h % 2])
                b.free = c2[1]
                for s in range(3):
                    for f in range(2):
                        blk = 8 * part + 2 * h + f
                        c2[f] = dve(lambda e, f=f, blk=blk, s=s: e.scalar_tensor_tensor(
                            out=q_[:, f, :], in0=z_[:, f, s:s + 256], scalar=cwt[0:96, blk, s:s + 1], in1=q_[:, f, :], op0=ALU.mult,
                            op1=ALU.add), c2[f], c1, zz[part])
                conv_read[part] = c2

            def head_silu(h, part):
                q_ = qk[h % 2][part]
                t_ready[h, part] = act(lambda e: e.activation(q_, q_, ACT.Silu), conv_read[part])

            def attend(h):
                q_, k_ = qk[h % 2]
                b = bank()
                for f in range(2):
                    mm(b.t[:, 0:256], k_[:, f, 0:128], q_[:, f, :], f == 0, f == 1, t_ready[h, 0], t_ready[h, 1], b.free)
                for f in range(2):
                    tk = mm(b.t[:, 256:384], k_[:, f, 128:256], q_[:, f, 128:256], f == 0, f == 1, sig=(f == 1))
                qk_read[h % 2] = tk
                b.free = t_a[h] = dve(lambda e: e.scalar_tensor_tensor(out=sc[h % 2], in0=b.t[:, 0:384], scalar=192.0 ** -0.5,
                                                                       in1=wt[:, h, :], op0=ALU.mult, op1=ALU.mult),
                                      tk, t_wt[h], sc_read[h % 2])

            def states(h):
                nb = bank()
                s_ = sc[h % 2]
                mm(nb.t[:, 0:193], s_[:, 0:128], va[:, 0, h, 0:193], True, True, t_a[h], t_v, t_one, nb.free)
                mm(nb.t[:, 256:449], s_[:, 128:256], va[:, 0, h, 0:193], True, False)
                pv = mm(nb.t[:, 256:449], s_[:, 256:384], va[:, 1, h, 0:193], False, True, sig=True)
                sc_read[h % 2] = pv
                nd = blocks(nb.t[:, :], 256)[:, :, 192]
                d1 = dve(lambda e: e.scalar_tensor_tensor(out=den[:, 0, h, :], in0=nd, scalar=-1.0, in1=ac[:, :, 4 + h],
                                                          op0=ALU.mult, op1=ALU.max), pv)
                d1 = dve(lambda e: e.tensor_tensor(den[:, 0, h, :], nd, den[:, 0, h, :], ALU.max), d1)
                d1 = dve(lambda e: e.reciprocal(den[:, 1, h, :], den[:, 0, h, :]), d1)
                d2 = []
                for t in range(2):
                    d2.append(act(lambda e, t=t: e.activation(hb[:, t, h, :], nb.t[:, 256 * t:256 * t + 192], ACT.Copy,
                                                              scale=den[:, 1, h, t:t + 1]), d1, t_prev))
                nb.free = d2
                for t in range(2):
                    d3 = dve(lambda e, t=t: e.bn_stats(hst[:, t, h, :], hb[:, t, h, :]), d2[t])
                for t in range(2):
                    d3 = dve(lambda e, t=t: e.bn_aggr(hmv[:, t, h, :], hst[:, t, h, :]), d3)
                d3 = dve(lambda e: e.tensor_scalar(hve[:, 0, h, :], hmv[:, :, h, 1], LN_EPS, None, ALU.add), d3)
                d4 = pool(lambda e: e.tensor_tensor(hve[:, 1, h, :], hve[:, 0, h, :], mhalf[:, 0:2], ALU.pow), d3, t_mhalf)
                for t in range(2):
                    t_h[h] = pool(lambda e, t=t: e.tensor_scalar(hb[:, t, h, :], hb[:, t, h, :], hmv[:, t, h, 0:1],
                                                                 hve[:, 1, h, t:t + 1], ALU.subtract, ALU.mult), d4)

            t_mem = []
            steps = [lambda: (turn(0), [weights(h) for h in range(4)]), lambda: (value(0), turn(1)),
                     lambda: (attend(0), value(1), turn(2)), lambda: (states(0), value(2), turn(3)),
                     lambda: (attend(1), value(3), scale()), lambda: (states(1), t_mem.append(finish())),
                     lambda: attend(2), lambda: states(2)]
            for h in range(4):
                for part in range(2):
                    head(h, part)
                    steps.pop(0)()
                    head_silu(h, part)

            ty = big_rows("w_in_mlstm", 4, xhi, xlo, n=768, splits=((0, 384), (384, 768)), n0=2304,
                          hook={0: lambda: attend(3), 1: lambda: states(3)})
            og = wt.rearrange("p h n -> p (h n)")[:, 0:1536].rearrange("p (t n) -> p t n", t=2)
            hv = [hb[:, t, :, :].rearrange("p h n -> p (h n)") for t in range(2)]
            t_g = [[], []]
            for t in range(2):
                for i in range(2):
                    y = Y[2 * t + i]
                    c = slice(384 * i, 384 * i + 384)
                    y.free = act(lambda e, y=y, t=t, c=c: e.activation(og[:, t, c], y.t[:, 0:384], ACT.Sigmoid), ty[t], t_a[3])
                    d6 = dve(lambda e, t=t, c=c: e.tensor_tensor(og[:, t, c], og[:, t, c], hn[:, c], ALU.mult), y.free, t_hn)
                    t_g[i].append(dve(lambda e, t=t, c=c: e.tensor_tensor(hv[t][:, c], hv[t][:, c], og[:, t, c], ALU.mult), d6,
                                      [t_h[h] for h in range(4)]))
            done = [[], [], []]

            def turned(q):
                b = bank()
                for k in range(2):
                    for t in range(2):
                        tk = tr(b.t[:, 256 * k + 128 * t:256 * k + 128 * t + 128], hv[t][:, 128 * (2 * q + k):128 * (2 * q + k) + 128],
                                128, t_g[0], t_g[1] if q else None, b.free, sig=(k == 1 and t == 1))
                b.free = split_to(mhi[:, 2 * q:2 * q + 2, :], mlo[:, 2 * q:2 * q + 2, :], blocks(b.t[:, :], 256), tk)
                done[q].extend(b.free)

            return t_mem + done, {0: lambda: (turned(0), turned(1), turned(2))}

        t_ax = scale_x(ALPHA1, t_x)
        t_m = []
        t_cs = []

        def split_memory(t_load):
            for q in range(4):
                t_m.append(split_to(mhi[:, 2 * q:2 * q + 2, :], mlo[:, 2 * q:2 * q + 2, :], memT[:, 2 * q:2 * q + 2, :], t_load))

        FFN = ("ffn_w_gate", "ffn_w_up", "ffn_w_down", FF // 256)
        for l in range(2):
            ty = ffn(*FFN, xt_ready, opened=opened if l else None, between={4: lambda: t_cs.extend([rotary()]), 6: lambda: split_memory(t_mem)} if l == 0 else {})
            fill = [lambda: memory_keys(0, t_m), lambda: memory_values(0, t_m)] if l == 0 else [lambda: memory_values(1, t_m)]
            done, xt_ready, t_ax = layer_norm(ty, t_ax, True, gbv, t_gb, ALPHA1, fill=fill)
            if l == 0:
                t_gb = next_gb(1, done)
                mix, hook = conv_mixer(xt_ready, done), {}
            else:
                mix, hook = mlstm_mixer(xt_ready, done)
                t_gb = next_gb(4, mix[0])
            ty = big_rows("w_out", 4, mhi, mlo, each=mix, hook=hook, tail=True)
            opened = ffn_opening(*FFN[0:2])
            done, xt_ready, t_ax = layer_norm(ty, t_ax, False, gbv, t_gb, ALPHA1, opening=opened[0])
            t_gb = next_gb(3 * l + 2, done)
            if l == 0:
                t_mem = sp.dma(memT, blocks(A["memT"][:, :], T), s_mem, done, xt_ready)
                t_m = []
                ty = ffn(*FFN, xt_ready, between={6: lambda: split_memory(t_mem)}, opened=opened)
                opened = ffn_opening(*FFN[0:2])
                done, xt_ready, t_ax = layer_norm(ty, t_ax, True, gbv, t_gb, ALPHA1, opening=opened[0],
                                                  fill=[lambda: memory_keys(1, t_m)])
                t_gb = next_gb(3, done)
            else:
                gin = ar[:, 0:2 * D]
                t_gin = pool.dma(gin, A["ln"][6:7, :].broadcast_to((128, 2 * D)), s_gbin, done, xt_ready)
                ty = ffn(*FFN, xt_ready, opened=opened)
                before = norm_parts(ty, t_ax, True, gbv, t_gb, dst=r)
        LATENT = ((0, 384), (384, 672))
        latents, opening = rows_opening("w_in_2", xhi, xlo, LATENT)
        done, xt_ready, t_ax = layer_norm(None, [None, None], False, gin, t_gin, ALPHA2, opening=opening, before=before)

        arena = Arena()
        ty = big_rows("w_in_2", 4, xhi, xlo, xt_ready, n=672, splits=LATENT, opened=latents)
        va = ar[:, 0:1024].rearrange("p (t h n) -> p t h n", t=2, h=8)
        cq = arena.take(2 * 384).rearrange("p (t n) -> p t n", t=2)
        ck = arena.take(2 * 288).rearrange("p (t n) -> p t n", t=2)
        ss = arena.take(8)
        hfl = hf[:, :, :, :].rearrange("p a b n -> p (a b n)")
        junk = hfl[:, 512:896]
        tmp = arena.take(4 * 128).rearrange("p (s n) -> p s n", s=4)
        q1 = None
        for t in range(2):
            for i, wdt in ((0, 384), (1, 256)):
                y = Y[2 * t + i]
                q1 = act(lambda e, t=t, i=i, wdt=wdt, y=y: e.activation(junk[:, 0:wdt], y.t[:, 0:wdt], ACT.Square,
                                                                        accum_out=ss[:, 2 * t + i:2 * t + i + 1]), ty[t], done, q1)
        for i, wdt in ((0, 384), (1, 256)):
            sv = ss[:, 0:4].rearrange("p (t i) -> p t i", i=2)[:, :, i]
            q2 = dve(lambda e, sv=sv, wdt=wdt: e.tensor_scalar(sv, sv, 1.0 / wdt, RMS_EPS, ALU.mult, ALU.add), q1)
        q3 = pool(lambda e: e.tensor_tensor(ss[:, 4:8], ss[:, 0:4], mhalf[:, 0:4], ALU.pow), q2, t_mhalf)
        for t in range(2):
            for i, o, wdt in ((0, cq, 384), (1, ck, 256)):
                y = Y[2 * t + i]
                q4 = dve(lambda e, t=t, i=i, o=o, wdt=wdt, y=y: e.tensor_scalar(o[:, t, 0:wdt], y.t[:, 0:wdt],
                                                                                 ss[:, 4 + 2 * t + i:5 + 2 * t + i], None, ALU.mult), q3)
                y.free = q4
        t_kr = None
        kr = arena.take(2 * 32).rearrange("p (t n) -> p t n", t=2)
        for t in range(2):
            y = Y[2 * t + 1]
            y1, y2 = y.t[:, 256:272], y.t[:, 272:288]
            c_, s_ = cosA[:, t, :], sinA[:, t, :]
            q5 = dve(lambda e, y1=y1, c_=c_: e.tensor_tensor(tmp[:, 0, 0:16], y1, c_, ALU.mult), q4, t_cs, t_kr)
            q5 = dve(lambda e, y2=y2, s_=s_: e.tensor_tensor(tmp[:, 1, 0:16], y2, s_, ALU.mult))
            q5 = dve(lambda e, y2=y2, c_=c_: e.tensor_tensor(tmp[:, 2, 0:16], y2, c_, ALU.mult))
            q5 = dve(lambda e, y1=y1, s_=s_: e.tensor_tensor(tmp[:, 3, 0:16], y1, s_, ALU.mult))
            y.free = q5
            dve(lambda e, t=t: e.tensor_tensor(kr[:, t, 0:16], tmp[:, 0, 0:16], tmp[:, 1, 0:16], ALU.subtract), q5)
            t_kr = dve(lambda e, t=t: e.tensor_tensor(kr[:, t, 16:32], tmp[:, 2, 0:16], tmp[:, 3, 0:16], ALU.add), q5)
        up_ = arena.take(4 * 272).rearrange("p (b n) -> p b n", b=4)
        up_wsum = ar[:, arena.at - 4 * 272:arena.at + 4 * 272]
        wsum = arena.take(4 * 272).rearrange("p (b n) -> p b n", b=4)
        p0 = pool(lambda e: e.memset(up_[:, :, 0:16], 0.0), done)
        for j in range(2):
            b, tk = pair(Tile("w_in_2", 256 * j), xhi, xlo)
            ev = act(lambda e, j=j, b=b: e.activation(up_[:, 2 * j:2 * j + 2, 16:272], blocks(b.t[:, :], 256), ACT.Copy), tk)
            b.free = ev
        wt2 = arena.take(4 * 272).rearrange("p (b n) -> p b n", b=4)
        t_pl = []
        for g in range(4):
            src, cur = up_[:, g, :], ev
            bufs = [wsum[:, g, :], wt2[:, g, :]]
            lo = 0
            for s in range(g + 1):
                step = 1 << s
                dst = bufs[s % 2]
                lo += step
                cur = pool(lambda e, dst=dst, src=src, lo=lo, step=step: e.tensor_tensor(
                    dst[:, lo:272], src[:, lo:272], src[:, lo - step:272 - step], ALU.add), cur, p0)
                src = dst
            o = wt2[:, g, :] if g % 2 == 0 else wsum[:, g, :]
            cur = pool(lambda e, src=src, o=o, g=g: e.tensor_tensor(o[:, 16:32], src[:, 16:32], P("cnt", 16 * g, 16 * g + 16), ALU.mult), cur)
            cu2 = pool(lambda e, src=src, o=o, g=g: e.tensor_scalar(o[:, 32:272], src[:, 32:272], 1.0 / (2 << g), None, ALU.mult), cur)
            cur = pool(lambda e, o=o, g=g: e.tensor_tensor(o[:, 16:272], o[:, 16:272], up_[:, g, 16:272], ALU.subtract), cur, cu2)
            t_pl.append((o, cur))

        t_lat = []
        for i, o, nb_, g in ((0, cq, 3, "q_g"), (1, ck, 2, "kv_g")):
            for k in range(nb_):
                b = bank()
                for t in range(2):
                    tk = tr(b.t[:, 128 * t:128 * t + 128], o[:, t, 128 * k:128 * k + 128], 128, q4, b.free, sig=(t == 1))
                dst = (mhi[:, 4 + k, :], mlo[:, 4 + k, :]) if i == 0 else (hhi[:, 0, k, :], hlo[:, 0, k, :])
                ev = split_to(dst[0], dst[1], b.t[:, 0:256], tk, scale=P(g, k, k + 1))
                b.free = ev
                t_lat.append(ev)

        zc = arena.take(4 * 286).rearrange("p (b n) -> p b n", b=4)
        ca = kT[:, :, :, :].rearrange("p a b n -> p (a b) n")
        sg = hfl[:, 0:512]
        dwt = P("conv_dw").rearrange("p (b w) -> p b w", w=31)
        z0 = pool(lambda e: e.memset(zc[:, :, 0:30], 0.0), done)
        t_z, t_c = [], [None] * 4
        sg_read = None
        for j in range(2):
            ba, ta = pair(Tile("w_in_2", 512 + 256 * j), xhi, xlo)
            bg, tg = pair(Tile("w_in_2", 1024 + 256 * j), xhi, xlo)
            s1 = act(lambda e, bg=bg: e.activation(sg, bg.t[:, :], ACT.Sigmoid), tg, sg_read)
            bg.free = s1
            s2 = dve(lambda e, j=j, ba=ba: e.tensor_tensor(zc[:, 2 * j:2 * j + 2, 30:286], blocks(sg, 256),
                                                           blocks(ba.t[:, :], 256), ALU.mult), s1, ta, z0)
            ba.free = s2
            sg_read = s2
            t_z.append(s2)
            t_cz = s2
        conv_steps = [(q, w) for w in range(31) for q in range(2)]
        conv_taps = list(range(31))
        more = arena.take(2 * T)
        cp = [tmp.rearrange("p s n -> p (s n)"), more]
        cp_read = [None, None]

        def conv_some(n, m):
            for _ in range(min(n, len(conv_steps))):
                b, w = conv_steps.pop(0)
                if w == 0:
                    t_c[b] = dve(lambda e, b=b: e.tensor_scalar(ca[:, b, :], zc[:, b, 0:256], dwt[:, b, 0:1], P("conv_b", b, b + 1),
                                                                ALU.mult, ALU.add), t_z[b // 2])
                else:
                    t_c[b] = dve(lambda e, b=b, w=w: e.scalar_tensor_tensor(
                        out=ca[:, b, :], in0=zc[:, b, w:w + 256], scalar=dwt[:, b, w:w + 1], in1=ca[:, b, :],
                        op0=ALU.mult, op1=ALU.add), t_c[b])
            for _ in range(min(m, len(conv_taps))):
                w = conv_taps.pop(0)
                if w == 0:
                    for b in (2, 3):
                        t_c[b] = act(lambda e, b=b: e.activation(ca[:, b, :], zc[:, b, 0:256], ACT.Identity, scale=dwt[:, b, 0:1],
                                                                 bias=P("conv_b", b, b + 1)), t_z[1])
                else:
                    o = cp[w % 2]
                    for b in (2, 3):
                        m_ = act(lambda e, b=b, w=w, o=o: e.activation(o[:, 256 * b - 512:256 * b - 256], zc[:, b, w:w + 256], ACT.Copy,
                                                                       scale=dwt[:, b, w:w + 1]), t_z[1], cp_read[w % 2], t_q)
                    t_c[2] = t_c[3] = pool(lambda e, o=o: e.tensor_tensor(ca[:, 2:4, :], ca[:, 2:4, :], blocks(o, 256), ALU.add),
                                           m_, t_c[2], t_c[3])
                    cp_read[w % 2] = t_c[2]

        qf = arena.take(2 * 768).rearrange("p (t h n) -> p t h n", t=2, h=8)
        kf = r[:, :, 0:768].rearrange("p t (h n) -> p t h n", h=8)
        free = [b.free for b in Y]
        for i, wdt in ((0, 512), (1, 256)):
            w = Tile("w_uq_2", 512 * i)
            tk = rowsof(w, mhi[:, 4:7, :], mlo[:, 4:7, :], 0, [(t, Y[2 * t + i].t[:, 0:wdt], 0, wdt) for t in range(2)], True, True,
                        t_lat, free)
            conv_some(6, 0)
            for t in range(2):
                y = Y[2 * t + i]
                o = qf[:, t, :, :].rearrange("p h n -> p (h n)")[:, 512 * i:512 * i + wdt]
                y.free = act(lambda e, o=o, wdt=wdt, y=y: e.activation(o, y.t[:, 0:wdt], ACT.Copy), tk)
                q6 = y.free
        t_q = []
        for t in range(2):
            x1, x2 = qf[:, t, :, 64:80], qf[:, t, :, 80:96]
            tv = [tmp[:, s, :].rearrange("p (h n) -> p h n", h=8) for s in range(4)]
            cb_ = cosA[:, t, :].unsqueeze(1).to_broadcast([128, 8, 16])
            sb_ = sinA[:, t, :].unsqueeze(1).to_broadcast([128, 8, 16])
            m = [pool(lambda e, o=o, a=a, c=c: e.tensor_tensor(o, a, c, ALU.mult), q6, t_cs, t_kr, t_q)
                 for o, a, c in ((tv[0], x1, cb_), (tv[1], x2, sb_), (tv[2], x2, cb_), (tv[3], x1, sb_))]
            m1 = pool(lambda e, x1=x1, tv=tv: e.tensor_tensor(x1, tv[0], tv[1], ALU.subtract), m[-1])
            t_q = [pool(lambda e, x2=x2, tv=tv: e.tensor_tensor(x2, tv[2], tv[3], ALU.add), m1)]
        ty = big_rows("w_ukv_2", 1, hhi[:, 0, :, :], hlo[:, 0, :, :], t_lat)
        t_k, t_v = [], []
        for t in range(2):
            for i in range(2):
                y = Y[2 * t + i]
                yv = y.t[:, :].rearrange("p (h n) -> p h n", h=4)
                a1 = act(lambda e, t=t, i=i, yv=yv: e.activation(kf[:, t, 4 * i:4 * i + 4, 0:64], yv[:, :, 0:64], ACT.Copy), ty[t])
                y.free = act(lambda e, t=t, i=i, yv=yv: e.activation(va[:, t, 4 * i:4 * i + 4, :], yv[:, :, 64:128], ACT.Copy), ty[t])
                t_k.append(y.free)
            krb = kr[:, t, :].unsqueeze(1).to_broadcast([128, 8, 32])
            t_k.append(pool(lambda e, t=t, krb=krb: e.tensor_copy(kf[:, t, :, 64:96], krb), t_kr, ty))
        conv_some(8, 1)

        mg = arena.take(8 * T)
        mgb = mg.rearrange("p (b n) -> p b n", b=8)

        def flat3(z):
            return z.rearrange("p b n -> p (b n)")

        G0 = [mg[:, 512 * j:512 * j + 512] for j in range(4)]
        G1 = [flat3(z[:, s, :, :]) for z in (vm, hf) for s in range(2)]
        G2 = [gb[:, s, 512 * h:512 * h + 512] for s in range(2) for h in range(2)]
        gate = {"n": 0}
        t_gate = {}

        def gate_half(*after):
            n, j, f = gate["n"] // 8, gate["n"] // 2 % 4, gate["n"] % 2
            gate["n"] += 1
            if f == 0:
                gate["w"] = Tile("w_in_2", 2208 + 1024 * n + 256 * j)
            w, b = gate["w"], bank()
            tk = cols(b.t[:, 0:256], w, 128 * f, 128, xhi, xlo, b.free)
            if f == 1:
                w.done(tk)
            o, blk = (G0, G1, G2)[n][j][:, 256 * f:256 * f + 256], 8 * n + 2 * j + f
            b.free = act(lambda e: e.activation(o, b.t[:, 0:256], ACT.Identity if n else ACT.Sigmoid,
                                                bias=P("b_gate", blk, blk + 1)), tk, list(after))
            t_gate[n, j] = b.free

        def gate_sigmoid(n, j):
            o = (G0, G1, G2)[n][j]
            t_gate[n, j] = act(lambda e: e.activation(o, o, ACT.Sigmoid), t_gate[n, j])

        def project(name, hi, lo, ready, use, banks=Y):
            free_ = [b.free for b in banks]
            for j in range(2):
                w = Tile(name, 512 * j)
                for f in range(4):
                    blk = 4 * j + f
                    tk = cols(banks[blk // 2].t[:, 256 * (blk % 2):256 * (blk % 2) + 256], w, 128 * f, 128, hi, lo, ready, free_)
                w.done(tk)
                use(2 * j, tk)
                use(2 * j + 1, tk)

        for _ in range(8):
            gate_half()
            conv_some(3, 1)
        t_yp = []
        for g in range(4):
            o, cur = t_pl[g]
            b = bank()
            t_pw = mm(b.t[:, 0:256], P("pool_w", 128 * g, 128 * g + 128), o[:, 16:272], True, True, cur, b.free, sig=True)
            ev = split_to(mhi[:, g, :], mlo[:, g, :], b.t[:, 0:256], t_pw, scale=P("pool_scale", g, g + 1))
            b.free = ev
            t_yp.append(ev)
        conv_some(2, 1)
        t_mg = [None] * 4

        def use_pool(j, tk):
            y = Y[j]
            y.free = t_mg[j] = dve(lambda e: e.tensor_tensor(G0[j], G0[j], y.t[:, :], ALU.mult), tk, t_gate[0, j])
            conv_some(1, 1)

        project("pool_proj_2", mhi[:, 0:4, :], mlo[:, 0:4, :], t_yp, use_pool)

        qkT = [r[0:96, :, 768:1024], blocks(up_wsum[0:96, 1536:2048], 256)]
        S = [up_wsum[:, 384 * i:384 * i + 384] for i in range(2)]
        pTb = [up_wsum[:, 768 + 384 * i:1152 + 384 * i] for i in range(2)]
        ob = flat3(wt2)[:, 0:1024].rearrange("p (t n) -> p t n", t=2)
        mx = arena.take(16)
        sm = arena.take(16)
        ri = arena.take(16)
        qscale = 96.0 ** -0.5
        o_b = [Y[0], Y[1]]
        o_free = [Y[0].free, Y[1].free]
        p_read, pT_read, q_read = [t_pw] * 2, [t_pw] * 2, [None] * 2
        t_qk, t_s, t_pT = {}, {}, {}

        def turn_qk(h):
            i = h % 2
            b = bank()
            for n, src in enumerate((qf, kf)):
                for t in range(2):
                    tk = tr(b.t[0:96, 256 * n + 128 * t:256 * n + 128 * t + 128], src[:, t, h, :], 128, t_q, t_k, b.free,
                            sig=(n == 1 and t == 1))
            b.free = t_qk[h] = act(lambda e: e.activation(qkT[i], blocks(b.t[0:96, :], 256), ACT.Copy), tk, q_read[i], t_pw)

        def scores(h):
            i = h % 2
            b = bank()
            mm(b.t[:, 0:128], qkT[i][:, 0, 0:128], qkT[i][:, 1, 0:128], True, True, t_qk[h], b.free)
            tk = mm(b.t[:, 128:384], qkT[i][:, 0, 128:256], qkT[i][:, 1, :], True, True, sig=True)
            q_read[i] = tk
            d1 = dve(lambda e: e.scalar_tensor_tensor(out=S[i], in0=b.t[:, 0:384], scalar=qscale, in1=P("mask"),
                                                      op0=ALU.mult, op1=ALU.add), tk, p_read[i])
            b.free = d1
            for t, (c0, c1_) in enumerate(((0, 128), (128, 384))):
                d2 = dve(lambda e, t=t, c0=c0, c1_=c1_: e.tensor_reduce(mx[:, 2 * h + t:2 * h + t + 1], S[i][:, c0:c1_],
                                                                        X, ALU.max, negate=True), d1)
            for t, (c0, c1_) in enumerate(((0, 128), (128, 384))):
                t_s[h] = act(lambda e, t=t, c0=c0, c1_=c1_: e.activation(
                    S[i][:, c0:c1_], S[i][:, c0:c1_], ACT.Exp, bias=mx[:, 2 * h + t:2 * h + t + 1],
                    accum_out=sm[:, 2 * h + t:2 * h + t + 1]), d2)

        def turn_p(h):
            i = h % 2
            b = bank()
            for n in range(3):
                tk = tr(b.t[:, 128 * n:128 * n + 128], S[i][:, 128 * n:128 * n + 128], 128, t_s[h], b.free, sig=(n == 2))
            p_read[i] = tk
            b.free = t_pT[h] = act(lambda e: e.activation(pTb[i], b.t[:, 0:384], ACT.Copy), tk, pT_read[i])

        def values(h):
            i = h % 2
            mm(o_b[0].t[:, 64 * h:64 * h + 64], pTb[i][:, 0:128], va[:, 0, h, :], True, True, t_pT[h], t_k, o_free)
            mm(o_b[1].t[:, 64 * h:64 * h + 64], pTb[i][:, 128:256], va[:, 0, h, :], True, False)
            pT_read[i] = mm(o_b[1].t[:, 64 * h:64 * h + 64], pTb[i][:, 256:384], va[:, 1, h, :], False, True, sig=True)

        g_free = [done, t_cz, q1]
        for step in range(11):
            for back, stage in ((3, values), (2, turn_p), (1, scores), (0, turn_qk)):
                if 0 <= step - back < 8:
                    stage(step - back)
            gate_half(g_free)
            conv_some(3, 2)
        conv_some(1000, 1000)
        d3 = dve(lambda e: e.reciprocal(ri, sm), t_s[7])
        for t in range(2):
            rv = ri.rearrange("p (h t) -> p t h", t=2)[:, t, :].unsqueeze(2).to_broadcast([128, 8, 64])
            d4 = dve(lambda e, t=t, rv=rv: e.tensor_tensor(ob[:, t, :].rearrange("p (h n) -> p h n", n=64),
                                                           o_b[t].t[:, :].rearrange("p (h n) -> p h n", n=64), rv, ALU.mult),
                     d3, pT_read, t_pw)
            o_b[t].free = d4

        ones, dg, vc = more[:, 0:128], more[:, 128:384], more[:, 384:388]
        t_on = pool(lambda e: e.memset(ones, 1.0 / 512), t_c)
        bm = bank()
        for k in range(4):
            tk = mm(bm.t[:, 0:256], ones, ca[:, k, :], k == 0, k == 3, t_on, t_c, bm.free, sig=(k == 3))
        mb = bm.t[:, 0:256].unsqueeze(1).to_broadcast([128, 4, 256])
        c1 = dve(lambda e: e.tensor_tensor(ca, ca, mb, ALU.subtract), tk)
        bm.free = c1
        sq = zc[:, :, 0:256]
        c2 = act(lambda e: e.activation(sq, ca, ACT.Square), c1)
        gate_half(g_free)
        gate_half(g_free)
        t_yo = []
        for q in range(2):
            b = bank()
            for k in range(2):
                for t in range(2):
                    tk = tr(b.t[:, 256 * k + 128 * t:256 * k + 128 * t + 128], ob[:, t, 128 * (2 * q + k):128 * (2 * q + k) + 128], 128,
                            d4, b.free, sig=(k == 1 and t == 1))
            ev = split_to(mhi[:, 2 * q:2 * q + 2, :], mlo[:, 2 * q:2 * q + 2, :], blocks(b.t[:, :], 256), tk)
            b.free = ev
            t_yo.append(ev)
        bv = bank()
        for t in range(2):
            for k in range(4):
                tk = mm(bv.t[:, t:t + 1], sq[:, k, 128 * t:128 * t + 128], ones[:, 0:1], k == 0, k == 3, c2, bv.free,
                        sig=(t == 1 and k == 3))
        c3 = dve(lambda e: e.tensor_scalar(vc[:, 0:2], bv.t[:, 0:2], LN_EPS, None, ALU.add), tk)
        bv.free = c3
        c4 = pool(lambda e: e.tensor_tensor(vc[:, 2:4], vc[:, 0:2], mhalf[:, 0:2], ALU.pow), c3, t_mhalf)
        for t in range(2):
            c5 = dve(lambda e, t=t: e.tensor_scalar(dg[:, 128 * t:128 * t + 128], ident, vc[:, 2 + t:3 + t], 512.0, ALU.mult, ALU.mult), c4)
        gate_half(g_free)
        br = bank()
        tk = mm(br.t[:, 0:256], ones, dg, True, True, c5, br.free, sig=True)
        rb = br.t[:, 0:256].unsqueeze(1).to_broadcast([128, 4, 256])
        c6 = dve(lambda e: e.tensor_tensor(ca, ca, rb, ALU.mult), tk)
        br.free = c6
        for k in range(4):
            c7 = act(lambda e, k=k: e.activation(ca[:, k, :], ca[:, k, :], ACT.Silu, bias=P("conv_lb", k, k + 1),
                                                 scale=P("conv_g", k, k + 1)), c6)
        gate_half(g_free)
        gate_half(g_free)
        assert gate["n"] == 24
        for j in range(4):
            gate_sigmoid(2, j)
        t_yc = split_to(mhi[:, 4:8, :], mlo[:, 4:8, :], ca, c7)
        pTr = kT[:, 0, :, :]
        t_p = pool.dma(pTr, blocks(A["pT"][:, :], T), s_p, t_yc)


        def use_mla(j, tk):
            y = Y[j]
            s1 = dve(lambda e: e.tensor_tensor(G2[j], G2[j], y.t[:, :], ALU.mult), tk, t_gate[2, j])
            y.free = s1
            t_mg[j] = pool(lambda e: e.tensor_tensor(G0[j], G0[j], G2[j], ALU.add), s1, t_mg[j])

        project("mla_proj_2", mhi[:, 0:4, :], mlo[:, 0:4, :], t_yo, use_mla)
        t_gb = next_gb(7, t_mg)
        for j in range(4):
            gate_sigmoid(1, j)
        tm = []

        cbank = [bank() for _ in range(4)]

        def use_conv(j, tk):
            y = cbank[j]
            s1 = dve(lambda e: e.tensor_tensor(G1[j], G1[j], y.t[:, :], ALU.mult), tk, t_gate[1, j])
            y.free = s1
            s2 = dve(lambda e: e.tensor_tensor(G0[j], G0[j], G1[j], ALU.add), s1, t_mg[j])
            tm.append(split_to(mhi[:, 2 * j:2 * j + 2, :], mlo[:, 2 * j:2 * j + 2, :], mgb[:, 2 * j:2 * j + 2, :], s2))

        project("conv_proj_2", mhi[:, 4:8, :], mlo[:, 4:8, :], t_yc, use_conv, cbank)
        t_ph = split_to(hhi[:, 0, :, :], hlo[:, 0, :, :], pTr, t_p)
        ty = big_rows("w_out_2", 4, mhi, mlo, each=tm, tail=True)
        pp = blocks(ar[:, 0:2 * D], D)
        t_pp = []

        def embedding():
            w = Tile("ple_proj_2", look=1)
            for t in range(2):
                for n in range(2):
                    b = bank()
                    o = pp[:, t, 512 * n:512 * n + 512]
                    tk = rows_of(w, t, hhi[:, 0, :, :], hlo[:, 0, :, :], 0, [(b.t[:, :], 512 * n, 512 * n + 512)], True, True, t_ph, b.free)
                    b.free = act(lambda e, o=o, b=b: e.activation(o, b.t[:, :], ACT.Copy), tk)
                    t_pp.append(b.free)
            w.done(tk)

        done, xt_ready, t_ax = layer_norm(ty, t_ax, False, gbv, t_gb, fill=[embedding])
        t_gb = next_gb(8, done)

        arena = Arena()
        arena.at = 2 * D
        pbc = arena.take(NG * T).rearrange("p (e n) -> p e n", e=NG)
        sel4 = arena.take(NG * 128)[0:NG].rearrange("p (e n) -> p e n", e=NG)
        z16 = pool(lambda e: e.memset(sel4, 0.0), done)
        t_s4 = pool(lambda e: e.affine_select(out=sel4, in_=sel4, compare_op=ALU.not_equal, fill=1.0, base=0,
                                               pattern=[[-1, NG], [0, 128]], channel_multiplier=1), z16)
        before = arena.take(128)
        allone = arena.take(128)
        z1 = pool(lambda e: e.memset(before, 1.0), done)
        z1 = pool(lambda e: e.affine_select(out=before, in_=before, compare_op=ALU.is_gt, fill=0.0, base=0,
                                            pattern=[[1, 128]], channel_multiplier=-1), z1)
        t_bef = pool(lambda e: e.memset(allone, 1.0), z1)
        slot_i = arena.take(256).bitcast(i32)
        slot_row = arena.take(128)
        slot_col = arena.take(2)
        z2 = pool(lambda e: e.iota(slot_i[:, 0:128], [[1, 128]], base=0, channel_multiplier=0), done)
        z2 = pool(lambda e: e.iota(slot_i[:, 128:129], [[0, 1]], base=0, channel_multiplier=1), z2)
        z3 = pool(lambda e: e.tensor_copy(slot_row, slot_i[:, 0:128]), z2)
        t_slot = pool(lambda e: e.tensor_copy(slot_col[:, 0:1], slot_i[:, 128:129]), z3)
        for i in range(2):
            raw_free.append((arena.take(TILE), s_raw[NR + i], [done, t_s4]))
            load_tile()
        w = Tile("w_router_2", 0)
        rbk = bank()
        tk = cols(rbk.t[0:16, 0:256], w, 0, 16, xhi, xlo, xt_ready, rbk.free)
        w.done(tk)
        affT = arena.take(T)[0:16]
        rbk.free = t_aff = act(lambda e: e.activation(affT, rbk.t[0:16, 0:256], ACT.Sigmoid), tk, done)
        v = arena.take(32 * 8).rearrange("p (s t n) -> p s t n", s=8, t=2)
        aff, sel, s3, s4, oh1, oh2, desc, wgt = [v[:, i, :, :] for i in range(8)]
        for n in range(16):
            t_d = pool(lambda e, n=n: e.memset(desc[:, :, n:n + 1], 16.0 - n), done)
        t_tok = []
        for t in range(2):
            v0 = [z[:, :, :].rearrange("p b n -> p (b n)")[:, D * t:D * t + D] for z in (mhi, mlo)]
            t_tok.append(split_to(v0[0], v0[1], x[:, t, :], done))
        t_ax = [pool(lambda e, t=t: e.tensor_scalar(x[:, t, :], x[:, t, :], ALPHA2, None, ALU.mult), t_ax[t], t_tok[t]) for t in range(2)]

        gk = arena.take(8).rearrange("p (t g) -> p t g", t=2)

        def route():
            rb_ = brow[:, 8:24].unsqueeze(1).to_broadcast([128, 2, 16])
            b = bank()
            for t in range(2):
                tk = tr(b.t[:, 16 * t:16 * t + 16], affT[:, 128 * t:128 * t + 128], 16, t_aff, b.free, sig=(t == 1))
            a1 = dve(lambda e: e.tensor_copy(aff, blocks(b.t[:, 0:32], 16)), tk, done)
            b.free = a1
            d = dve(lambda e: e.tensor_tensor(sel, aff, rb_, ALU.add), a1, t_brow)
            sg4 = sel.rearrange("p t (g n) -> p (t g) n", n=4)
            pr = arena.take(8 * 6).rearrange("p (g n) -> p g n", n=6)
            d1 = dve(lambda e: e.tensor_tensor(pr[:, :, 0:3], sg4[:, :, 0:3], sg4[:, :, 1:4], ALU.add), d)
            d1 = dve(lambda e: e.tensor_tensor(pr[:, :, 3:5], sg4[:, :, 0:2], sg4[:, :, 2:4], ALU.add))
            d1 = dve(lambda e: e.tensor_tensor(pr[:, :, 5:6], sg4[:, :, 0:1], sg4[:, :, 3:4], ALU.add))
            gsc = arena.take(8).rearrange("p (t g) -> p t g", t=2)
            d1 = dve(lambda e: e.tensor_reduce(gsc.rearrange("p t g -> p (t g)"), pr, X, ALU.max), d1)

            small = arena.take(8)

            def first_max(oh, src, n, d):
                m_ = small[:, 0:2]
                dd = desc[:, :, 0:n]
                d = dve(lambda e: e.tensor_reduce(m_, src, X, ALU.max), d)
                d = dve(lambda e: e.tensor_tensor(oh, src, m_.unsqueeze(2).to_broadcast([128, 2, n]), ALU.is_equal), d)
                d = dve(lambda e: e.tensor_tensor(oh, oh, dd, ALU.mult), d, t_d)
                d = dve(lambda e: e.tensor_reduce(m_, oh, X, ALU.max), d)
                return dve(lambda e: e.tensor_tensor(oh, dd, m_.unsqueeze(2).to_broadcast([128, 2, n]), ALU.is_equal), d)

            d1 = first_max(gk, gsc, 4, d1)
            t_pick = d1
            BIG = 1e30
            gkb = arena.take(8).rearrange("p (t g) -> p t g", t=2)
            d2 = dve(lambda e: e.tensor_scalar(gkb, gk, BIG, -BIG, ALU.mult, ALU.add), d1)
            s34 = s3.rearrange("p t (g n) -> p (t g) n", n=4)
            gk8 = gk.rearrange("p t g -> p (t g)").unsqueeze(2).to_broadcast([128, 8, 4])
            gkb8 = gkb.rearrange("p t g -> p (t g)").unsqueeze(2).to_broadcast([128, 8, 4])
            d2 = dve(lambda e: e.tensor_tensor(s34, sg4, gk8, ALU.mult), d2)
            d2 = dve(lambda e: e.tensor_tensor(s34, s34, gkb8, ALU.add), d2)
            d2 = first_max(oh1, s3, 16, d2)
            d2 = dve(lambda e: e.scalar_tensor_tensor(out=s4, in0=oh1, scalar=-2 * BIG, in1=s3, op0=ALU.mult, op1=ALU.add), d2)
            d2 = first_max(oh2, s4, 16, d2)
            d2 = dve(lambda e: e.tensor_tensor(oh1, oh1, oh2, ALU.add), d2)
            d2 = dve(lambda e: e.tensor_tensor(wgt, oh1, aff, ALU.mult), d2)
            m_ = small[:, 2:4]
            d2 = dve(lambda e: e.tensor_reduce(m_, wgt, X, ALU.add), d2)
            d2 = dve(lambda e: e.reciprocal(small[:, 4:6], m_), d2)
            d2 = dve(lambda e: e.tensor_tensor(wgt, wgt, small[:, 4:6].unsqueeze(2).to_broadcast([128, 2, 16]), ALU.mult), d2)
            t_wgt = d2
            t_route.extend([t_pick, t_wgt])

        posm = arena.take(8).rearrange("p (t n) -> p t n", t=2)
        posT = tsel[0:NG, 0, :]
        s_of = blocks(flat3(hhi[:, 0, :, :]), 128)[0:NG]
        t_s = act(lambda e: e.activation(s_of, sel4, ACT.Copy), t_s4, t_pp)
        flag = arena.take(4)
        t_route, t_pb, t_place = [], [], {}

        def placing():
            t_pick = t_route[0]
            b = bank()
            mm(b.t[:, 0:4], before, gk[:, 0, :], True, True, t_pick, t_bef, b.free)
            mm(b.t[:, 4:8], before, gk[:, 1, :], True, False)
            mm(b.t[:, 4:8], allone, gk[:, 0, :], False, True)
            mm(b.t[:, 8:12], allone, gk[:, 0, :], True, False)
            tk = mm(b.t[:, 8:12], allone, gk[:, 1, :], False, True, sig=True)
            d3 = dve(lambda e, b=b: e.scalar_tensor_tensor(out=posm, in0=blocks(b.t[:, 0:8], NG), scalar=1e4, in1=gk,
                                                           op0=ALU.add, op1=ALU.mult), tk)
            d4 = dve(lambda e, b=b: e.tensor_reduce(flag[:, 0:1], b.t[:, 8:12], X, ALU.max), d3)
            b.free = d4
            d3 = dve(lambda e: e.tensor_scalar(posm, posm, 1e4, None, ALU.subtract), d3)
            t_flag = dve(lambda e: e.tensor_scalar(flag[:, 1:2].bitcast(i32), flag[:, 0:1], 128.5, None, ALU.is_gt), d4)
            t_place.update(d3=d3, flag=t_flag)

        def spread():
            d3 = t_place["d3"]
            b = bank()
            for t in range(2):
                tk = tr(b.t[0:NG, 128 * t:128 * t + 128], posm[:, t, :], 128, d3, b.free, sig=(t == 1))
            d5 = dve(lambda e, b=b: e.tensor_copy(posT, b.t[0:NG, 0:256]), tk)
            b.free = d5
            for e2 in range(NG // 2):
                b = bank()
                for q in range(2):
                    tk = mm(b.t[:, 256 * q:256 * q + 256], s_of[:, 2 * e2 + q, :], posT, True, True, d5, t_s, b.free, sig=(q == 1))
                ev = act(lambda e, e2=e2, b=b: e.activation(pbc[:, 2 * e2:2 * e2 + 2, :].rearrange("p e n -> p (e n)"), b.t[:, :], ACT.Copy), tk)
                b.free = ev
                t_pb.append(ev)

        ty = big_rows("ple_gate_2", 4, xhi, xlo, hook={0: route, 2: placing, 3: spread})
        t_wgt = t_route[1]
        d3, t_flag = t_place["d3"], t_place["flag"]
        t_tail = [ty]
        pg = r
        for t in range(2):
            for i in range(2):
                y = Y[2 * t + i]
                y.free = act(lambda e, t=t, i=i, y=y: e.activation(pg[:, t, 512 * i:512 * i + 512], y.t[:, :], ACT.Sigmoid), ty[t][i], done)
            e1 = pool(lambda e, t=t: e.tensor_tensor(pg[:, t, :], pg[:, t, :], pp[:, t, :], ALU.mult), y.free, t_pp)
            t_ax[t] = pool(lambda e, t=t: e.tensor_tensor(x[:, t, :], x[:, t, :], pg[:, t, :], ALU.add), e1, t_ax[t])


        y_hi, y_lo = [flat3(z[:, 1, :, :]) for z in (hhi, hlo)]
        tok_hi, tok_lo = [z[:, :, :].rearrange("p b n -> p (b n)").rearrange("p (t d) -> p t d", t=2) for z in (mhi, mlo)]
        hT_first = [blocks(flat3(z[:, 0, :, :]), 128) for z in (hhi, hlo)]
        hT_last = [z[:, 0:4, 0:128] for z in (xhi, xlo)]
        y_last = [flat3(z[:, 0, :, :]) for z in (hhi, hlo)]

        def hT_of(e):
            return hT_last if e == NEXP - 1 else hT_first

        def y_of(c, n):
            return y_last if n and c == NG - 1 else [y_hi, y_lo]
        wsl = arena.take(16)
        places = arena.take(8).rearrange("p (t n) -> p t n", t=2)
        col0 = arena.take(2)

        def experts(place0, t_x, t_acc, *after):
            after = list(after)
            start = place0 == 0
            if start:
                place, col, t_pl = posm, slot_col, [t_slot, d3]
            else:
                place, col = places, col0
                p1 = dve(lambda e: e.tensor_scalar(places, posm, float(place0), None, ALU.subtract), after)
                t_pl = [dve(lambda e: e.tensor_scalar(col0[:, 0:1], slot_col[:, 0:1], float(place0), None, ALU.add), after), p1]
            S_read, T_read, y_read, hT_read, up_done = [None], [None, None], [None], [None], [None]
            t_pick_, t_gx, t_ws, t_h, t_hT, t_y, t_T = {}, {}, {}, {}, {}, {}, {}
            t_sum = [[t_acc[t]] for t in range(2)]

            def pick(p):
                for s in range(2):
                    for t in range(2):
                        c = 2 * p + s
                        q = dve(lambda g, c=c, s=s, t=t: g.tensor_scalar(gsel[:, t, 128 * s:128 * s + 128], slot_row, place[:, t, c:c + 1],
                                                                         None, ALU.is_equal), t_pl, t_slot, S_read, [] if start else after)
                t_pick_[p] = q

            def gather(p):
                t_gx[p] = {0: [], 1: []}

                def part(q, src, dst):
                    b = bank()
                    for k in range(2):
                        c = 128 * (2 * q + k)
                        for t in range(2):
                            tk = mm(b.t[:, 256 * k:256 * k + 256], src[:, t, c:c + 128], gsel[:, t, :], t == 0, t == 1,
                                    t_pick_[p], t_x, b.free, sig=(k == 1 and t == 1))
                    b.free = act(lambda g: g.activation(dst[:, 2 * q:2 * q + 2, :], blocks(b.t[:, :], 256), ACT.Copy),
                                 tk, up_done[0], after)
                    t_gx[p][q // 2].append(b.free)
                    S_read[0] = tk

                def weights():
                    b = bank()
                    for s in range(2):
                        c = 8 * p + 4 * s
                        for t in range(2):
                            tk = mm(b.t[:, 4 * s:4 * s + 4], gsel[:, t, 128 * s:128 * s + 128].bitcast(f32), wgt[:, t, c:c + 4],
                                    t == 0, t == 1, t_pick_[p], t_wgt, b.free, sig=(s == 1 and t == 1))
                    b.free = t_ws[p] = dve(lambda g: g.tensor_copy(wsl[:, 8 * p:8 * p + 8], b.t[:, 0:8]), tk, after)

                return [weights] + [lambda q=q, z=z: part(q, *z) for q in range(4) for z in ((tok_hi, xhi), (tok_lo, xlo))]

            def up(e):
                bg, bu = bank(), bank()
                c0 = 128 * (e // 4 % 2)
                k0 = 0
                for j in range(4):
                    w = Tile("exp_w_up_2", look=LOOK)
                    for k in range(w.kb):
                        st, en = k0 + k == 0, k0 + k == 7
                        lh, ll = xhi[:, k0 + k, c0:c0 + 128], xlo[:, k0 + k, c0:c0 + 128]
                        for b, c in ((bg, 0), (bu, 512)):
                            mm(b.t[:, :], lh, w.hi[:, k, c:c + 512], st, False, w.ready(k), at([t_gx[e // 8]], k0 + k), b.free)
                        for b, c in ((bg, 0), (bu, 512)):
                            mm(b.t[:, :], lh, w.lo[:, k, c:c + 512], False, False)
                        for b, c in ((bg, 0), (bu, 512)):
                            tk = mm(b.t[:, :], ll, w.hi[:, k, c:c + 512], False, en, sig=(c == 512 and k == w.kb - 1))
                    w.done(tk)
                    k0 += w.kb
                up_done[0] = tk
                hs = flat3(hf[:, e % 2, :, :])
                t1 = act(lambda g: g.activation(hs, bg.t[:, :], ACT.Silu), tk, t_hT.get(e - 2), after)
                t2 = dve(lambda g: g.scalar_tensor_tensor(out=hs, in0=bu.t[:, :], scalar=wsl[:, e:e + 1], in1=hs, op0=ALU.mult, op1=ALU.mult),
                         t1, tk, t_ws[e // 8])
                bg.free, bu.free = t1, t2
                t_h[e] = t2
                ahead()

            def turn(e):
                hs = flat3(hf[:, e % 2, :, :])
                b = bank()
                for k in range(4):
                    tk = tr(b.t[:, 128 * k:128 * k + 128], hs[:, 128 * k:128 * k + 128], 128, t_h[e], b.free, sig=(k == 3))
                hT_hi, hT_lo = hT_of(e)
                b.free = t_hT[e] = split_to(hT_hi, hT_lo, blocks(b.t[:, :], 128), tk, up_done if e == NEXP - 1 else hT_read, after)

            def down(e, n):
                y = Y[2 * (e // 4 % 2) + n]
                w = Tile("exp_w_down_2", 512 * n)
                hT_hi, hT_lo = hT_of(e)
                for k in range(4):
                    mm(y.t[:, :], hT_hi[:, k, :], w.hi[:, k, :], e % 4 == 0 and k == 0, False, w.ready(k), t_hT[e],
                       y.free if e % 4 == 0 else None)
                    mm(y.t[:, :], hT_hi[:, k, :], w.lo[:, k, :], False, False)
                    tk = mm(y.t[:, :], hT_lo[:, k, :], w.hi[:, k, :], False, e % 4 == 3 and k == 3, sig=(k == 3))
                w.done(tk)
                if e < NEXP - 1:
                    hT_read[0] = tk
                return y, tk

            def take(c, n, y, tk):
                y.free = t_y[n] = split_to(*y_of(c, n), y.t[:, :], tk, hT_read if y_of(c, n) is y_last else y_read, after)
                if n == 0:
                    s = c % 2
                    t_T[c] = dve(lambda g: g.tensor_scalar(tsel[:, s, :], pbc[:, c, :], col[:, 0:1], None, ALU.is_equal),
                                 t_pb[c // 2], t_pl, T_read[s], after)

            def scatter(c, n):
                s = c % 2
                yh, yl = y_of(c, n)
                for t in range(2):
                    b = Y[2 * t + n] if c == NG - 1 else Y[2 * ((c + 1 + n) % 2) + t]
                    mm(b.t[:, :], tsel[:, s, 128 * t:128 * t + 128], yh, True, False, t_T[c], t_y[n], b.free)
                    tk = mm(b.t[:, :], tsel[:, s, 128 * t:128 * t + 128], yl, False, True, sig=True)
                    if c == NG - 1:
                        yt[t] = [yt[t][0], tk] if n else [tk, None]
                    else:
                        xa = x[:, t, 512 * n:512 * n + 512]
                        b.free = dve(lambda g, xa=xa, b=b: g.tensor_tensor(xa, xa, b.t[:, :], ALU.add), tk, t_acc[t])
                        t_sum[t].append(b.free)
                y_read[0] = T_read[s] = tk

            pick(0)
            for step in gather(0):
                step()
            pick(1)
            for e in range(NEXP + 1):
                ended = e and e % 4 == 0
                if e < NEXP:
                    up(e)
                if e > 1 and e % 4 == 1:
                    scatter(e // 4 - 1, 1)
                steps = gather(1) if e == 7 else []
                for step in steps[:7]:
                    step()
                if e:
                    first_ = down(e - 1, 0)
                    if ended:
                        take(e // 4 - 1, 0, *first_)
                    ahead()
                for step in steps[7:]:
                    step()
                if e == NEXP - 1:
                    turn(e)
                if e:
                    second = down(e - 1, 1)
                    if ended:
                        scatter(e // 4 - 1, 0)
                        take(e // 4 - 1, 1, *second)
                    ahead()
                if e < NEXP - 1:
                    turn(e)
            scatter(NG - 1, 1)
            return [yt[0], yt[1]], t_sum

        ty, t_ax = experts(0, t_tok, t_ax, t_tail)

        main = [pe, act, dve, pool, sp]
        kept = [b.free for b in W + Y]
        last = [(q.sem, q.count) for q in main[:4]] + [(s_raw[i][0], s_raw[i][1]) for i in range(NR + 2)]
        pe, act, dve, pool, sp = [Queue(sem(n), n) for n in ("o_pe", "o_act", "o_dve", "o_pool", "o_sp")]
        over = [pe, act, dve, pool, sp]
        for q in over:
            q.wait(last)
        state["end"] = len(tiles)
        while raw_free and state["load"] < state["end"]:
            load_tile()
        t_sum = []
        for t in range(2):
            for n in range(2):
                xa, b = x[:, t, 512 * n:512 * n + 512], Y[2 * t + n]
                t_sum.append(dve(lambda e, xa=xa, b=b: e.tensor_tensor(xa, xa, b.t[:, :], ALU.add), last))
                b.free = t_sum[-1]
        to, _ = experts(128, last, [t_sum, t_sum], last)
        for q in over:
            q.wait(to, [(z.sem, z.count) for z in (act, dve)])
        pe, act, dve, pool, sp = main
        for b, f in zip(W + Y, kept):
            b.free = f
        for q, o in zip(main, over):
            q.branch(o, flag[0:1, 1:2].bitcast(i32), t_flag)

        add, spread_of, _, norm = norm_parts(ty, t_ax, False, gbv, t_gb)
        s1 = [[add(t, 0)] for t in range(2)]
        rs = []
        for t in range(2):
            s1[t].append(add(t, 1))
            rs.append(spread_of(t, s1[t]))
        ov = out[0].rearrange("(t p) d -> p t d", p=128)
        for t in range(2):
            for h, n in enumerate(norm(t, rs[t])):
                t_out = sp.dma(half_of(ov, t, h), half_of(x, t, h), s_out, n)
        sp.wait(t_out)
        assert state["use"] == len(tiles)

        with nc.Block() as block:
            @block.sync
            def _(e):
                sp.emit(e)

            @block.scalar
            def _(e):
                act.emit(e)

            @block.vector
            def _(e):
                dve.emit(e)

            @block.gpsimd
            def _(e):
                pool.emit(e)

            @block.tensor
            def _(e):
                pe.emit(e)


def feature_major(a):
    a = np.asarray(a)
    n = a.shape[-1] // 128
    a = a.reshape(-1, n, 128).transpose(2, 1, 0)
    return a.reshape(128, -1)


def token_major_T(a):
    tok, f = a.shape
    return np.ascontiguousarray(a.T.reshape(f // 128, 128, tok).transpose(1, 0, 2).reshape(128, -1))


def lay_out(inputs):
    a = {k: np.asarray(v) for k, v in inputs.items()}
    parts = []
    for name, idx, k0, k1, n0, n1 in weight_tiles():
        w = a[name][idx] if idx else a[name]
        w = w[128 * k0:128 * k1, n0:n1].reshape(k1 - k0, 128, n1 - n0).transpose(1, 0, 2)
        parts.append(w.reshape(-1))
    ws = np.concatenate(parts)

    par = np.zeros((128, NPAR), np.float32)

    def put(name, v):
        lo, hi = POFF[name]
        par[:v.shape[0], lo:hi] = v.reshape(v.shape[0], -1)

    put("conv_w", feature_major(a["conv_w"][0]))
    put("qkconv", a["qk_conv_w"][0].reshape(4, 16, 96).transpose(2, 1, 0))
    put("conv_dw", feature_major(a["conv_dw_2"][0]))
    put("conv_b", feature_major(a["conv_b_2"][0]))
    put("conv_g", feature_major(a["conv_ln_g_2"][0]))
    put("conv_lb", feature_major(a["conv_ln_b_2"][0]))
    put("b_gate", np.ascontiguousarray(a["b_gate_2"][0].reshape(24, 128).T))
    put("pool_scale", feature_major(a["pool_scale_2"][0]))
    put("q_g", feature_major(a["q_norm_g_2"][0]))
    put("kv_g", feature_major(a["kv_norm_g_2"][0]))
    put("pool_w", np.ascontiguousarray(a["pool_w_2"][0].transpose(1, 0, 2)))
    put("ident", np.eye(128, dtype=np.float32))
    mask = np.zeros((128, 384), np.float32)
    mask[0:64, 64:128] = -1e30
    mask[0:64, 128 + 192:384] = -1e30
    put("mask", mask)
    put("b_gates", a["b_gates"][0].reshape(2, 4).T)
    cnt = np.zeros((128, 4, 16), np.float32)
    for g in range(4):
        cnt[:, g, :] = 1.0 / np.minimum(np.arange(16) + 1, 2 << g)
    put("cnt", cnt)
    invf = np.power(np.float32(10000.0), -np.arange(0, 32, 2, dtype=np.float32) / np.float32(32))
    put("invf", np.tile(invf.astype(np.float32), (128, 1)))

    g = [a["ln_g"][l, j] for l in range(2) for j in range(3)] + [a["ln_in_g_2"], a["ln1_g_2"][0], a["ln2_g_2"][0]]
    b = [a["ln_b"][l, j] for l in range(2) for j in range(3)] + [a["ln_in_b_2"], a["ln1_b_2"][0], a["ln2_b_2"][0]]
    ln = np.stack([np.concatenate([p, q]) for p, q in zip(g, b)])
    rows = np.concatenate([a["b_gates"][0], a["router_bias_2"], a["head_norm_g"][0].reshape(-1)])[None, :]
    return {"ws": ws, "par": par, "ln": ln, "rows": np.ascontiguousarray(rows), "x": a["x"], "xT": token_major_T(a["x"][0]),
            "memT": token_major_T(a["mem"][0]), "pT": token_major_T(a["p_2"][0, 0]), "pos": a["positions_2"].reshape(2, 128).T}


def kernel(**inputs):
    import concourse.bacc as _bacc
    from concourse.bass_utils import run_bass_kernel_spmd as _run

    nc = _bacc.Bacc("TRN2", target_bir_lowering=False, num_devices=1)
    arrays, aps = {}, {}
    for name, a in lay_out(inputs).items():
        a = np.ascontiguousarray(a)
        arrays[f"in_{name}"] = a
        aps[name] = nc.dram_tensor(f"in_{name}", a.shape, mybir.dt.from_np(a.dtype), kind="ExternalInput").ap()
    out = nc.dram_tensor("out_0", (1, T, D), mybir.dt.float32, kind="ExternalOutput").ap()
    program(nc, aps, out)
    res = _run(nc, [arrays], core_ids=[0])
    return res.results[0]["out_0"]
```
